# Optimizing a Trainium2 kernel written in Bass

```python
import jax
import jax.numpy as jnp
from jax import lax
import numpy as np
import jax, jax.numpy as jnp

D_MODEL = 1024
BATCH = 1
SEQ = 512
DEPTH = 1

CTX_LEN = 256
GRID_W = 64
FOURIER_W = 512
FOURIER_GROUPS = 8
RWKV_W = D_MODEL - FOURIER_W
HEAD = 64
N_HEADS = RWKV_W // HEAD
N_DIR = 2
DECAY_RANK = 64
ICLR_RANK = 64
GATE_RANK = 128
D_FF = 2816
RWKV_PROJ_W = 3 * RWKV_W + N_DIR * DECAY_RANK + N_DIR * ICLR_RANK + GATE_RANK
PROJ_W = FOURIER_W + RWKV_PROJ_W
NORM_EPS = 1e-6
GN_EPS = 64e-5
KK_EPS = 1e-12


def rms_norm(x, g):
    xf = x.astype(jnp.float32)
    y = xf * lax.rsqrt(jnp.mean(xf * xf, axis=-1, keepdims=True) + NORM_EPS)
    return (y * g.astype(jnp.float32)).astype(x.dtype)

def modulate(h, shift, scale):
    return h * (1 + scale) + shift

def conv1d_centred(u, w):
    up = jnp.pad(u, ((0, 0), (1, 1), (0, 0)))
    return up[:, :-2] * w[0] + up[:, 1:-1] * w[1] + up[:, 2:] * w[2]

def conv2d_grid(u, w, rows):
    b, t, ch = u.shape
    g = u.reshape(b, rows, GRID_W, ch)
    y = lax.conv_general_dilated(g, w[:, :, None, :].astype(u.dtype), (1, 1), "SAME",
                                 dimension_numbers=("NHWC", "HWIO", "NHWC"),
                                 feature_group_count=ch)
    return y.reshape(b, t, ch)

def fourier_mix(u, g):
    b, t, _ = u.shape
    uf = u.astype(jnp.float32).reshape(b, t, FOURIER_GROUPS, FOURIER_W // FOURIER_GROUPS)
    y = jnp.fft.fft2(uf, axes=(1, 3), norm="ortho").real
    return rms_norm(y.reshape(b, t, FOURIER_W), g).astype(u.dtype)

def rwkv_inputs(u, conv_w, w0, w2, a0, a2, k_k, k_a):
    b, t, _ = u.shape
    rkv = conv1d_centred(u[..., :3 * RWKV_W], conv_w)
    r, k, v = jnp.split(rkv, 3, axis=-1)
    o = 3 * RWKV_W
    wd = u[..., o:o + N_DIR * DECAY_RANK].reshape(b, t, N_DIR, DECAY_RANK)
    o += N_DIR * DECAY_RANK
    ad = u[..., o:o + N_DIR * ICLR_RANK].reshape(b, t, N_DIR, ICLR_RANK)
    o += N_DIR * ICLR_RANK
    gd = u[..., o:]
    w_lora = (w0 + jnp.einsum("btdr,drc->btdc", jnp.tanh(wd), w2)).astype(jnp.float32)
    decay = jnp.exp(-jnp.exp(-jax.nn.softplus(-w_lora) - 0.5))
    a = jax.nn.sigmoid((a0 + jnp.einsum("btdr,drc->btdc", ad, a2)).astype(jnp.float32))
    kk = (k * k_k).astype(jnp.float32).reshape(b, t, N_HEADS, HEAD)
    kk = kk * lax.rsqrt(jnp.sum(kk * kk, axis=-1, keepdims=True) + KK_EPS)
    kk = kk.reshape(b, t, RWKV_W)
    kd = k.astype(jnp.float32)[:, :, None] * (1 + (a - 1) * k_a)
    return r, kd, v, kk, a, decay, gd

def _heads_time_major(x2):
    d, b, t, _ = x2.shape
    return x2.astype(jnp.float32).reshape(d, b, t, N_HEADS, HEAD).transpose(2, 0, 1, 3, 4)

def shared_dirs(x):
    return _heads_time_major(jnp.stack([x, jnp.flip(x, axis=1)], axis=0))

def per_dir(x):
    return _heads_time_major(jnp.stack([x[:, :, 0], jnp.flip(x[:, :, 1], axis=1)], axis=0))

def merge_dirs(y):
    y = y.transpose(1, 2, 0, 3, 4)
    return y[0] + jnp.flip(y[1], axis=1)

def rwkv_scan(prep, state0, readout):
    r, kd, v, kk, a, decay, _ = prep
    xs = (shared_dirs(r), per_dir(kd), shared_dirs(v), shared_dirs(kk), per_dir(a), per_dir(decay))

    def step(s, inp):
        r_t, k_t, v_t, kk_t, a_t, w_t = inp
        sa = jnp.einsum("dbhij,dbhj->dbhi", s, kk_t)
        s = (s * w_t[..., None, :] - sa[..., :, None] * (kk_t * a_t)[..., None, :]
             + v_t[..., :, None] * k_t[..., None, :])
        y = jnp.einsum("dbhij,dbhj->dbhi", s, r_t) if readout else None
        return s, y

    return lax.scan(step, state0, xs)

def rwkv_output(y, prep, g2, r_k, gn_g, gn_b):
    r, kd, v, _, _, _, gd = prep
    b, t = r.shape[:2]
    mu = jnp.mean(y, axis=-1, keepdims=True)
    var = jnp.mean(jnp.square(y - mu), axis=-1, keepdims=True)
    yn = ((y - mu) * lax.rsqrt(var + GN_EPS)).reshape(b, t, RWKV_W)
    yn = yn * gn_g.astype(jnp.float32) + gn_b.astype(jnp.float32)
    rh = r.astype(jnp.float32).reshape(b, t, N_HEADS, HEAD)
    vh = v.astype(jnp.float32).reshape(b, t, N_HEADS, HEAD)
    kdh = kd.reshape(b, t, N_DIR, N_HEADS, HEAD)
    bonus = jnp.einsum("bthn,btdhn,hn->bth", rh, kdh, r_k.astype(jnp.float32))[..., None] * vh
    gate = jax.nn.sigmoid(gd.astype(jnp.float32)) @ g2.astype(jnp.float32)
    return (yn + bonus.reshape(b, t, RWKV_W)) * gate

def token_mixer(h, hc, w_in, conv_w, w0, w2, a0, a2, g2, k_k, k_a, r_k, gn_g, gn_b,
                f_g, w_out, ctx_out):
    u = h @ w_in
    uc = hc @ (w_in if ctx_out else w_in[:, FOURIER_W:])
    uc_r = uc[..., FOURIER_W:] if ctx_out else uc
    prep_l = rwkv_inputs(u[..., FOURIER_W:], conv_w, w0, w2, a0, a2, k_k, k_a)
    prep_c = rwkv_inputs(uc_r, conv_w, w0, w2, a0, a2, k_k, k_a)
    state0 = jnp.zeros((N_DIR, hc.shape[0], N_HEADS, HEAD, HEAD), jnp.float32)
    state_c, y_c = rwkv_scan(prep_c, state0, ctx_out)
    _, y_l = rwkv_scan(prep_l, state_c, True)
    rw_l = rwkv_output(merge_dirs(y_l), prep_l, g2, r_k, gn_g, gn_b).astype(h.dtype)
    out = jnp.concatenate([fourier_mix(u[..., :FOURIER_W], f_g).astype(h.dtype), rw_l], axis=-1) @ w_out
    out_c = None
    if ctx_out:
        rw_c = rwkv_output(merge_dirs(y_c), prep_c, g2, r_k, gn_g, gn_b).astype(hc.dtype)
        out_c = jnp.concatenate([fourier_mix(uc[..., :FOURIER_W], f_g).astype(hc.dtype), rw_c], axis=-1) @ w_out
    return out, out_c

def conv_ffn(h, w_up, conv_w, conv_b, w_down, rows):
    u = h @ w_up
    if rows is None:
        u = conv1d_centred(u, conv_w[1]) + conv_b
    else:
        u = conv2d_grid(u, conv_w, rows) + conv_b
    gate, val = jnp.split(u, 2, axis=-1)
    return (jax.nn.silu(gate) * val) @ w_down

def first_inputs(seed: int = 0) -> dict:
    key = jax.random.key(seed)
    ks = jax.random.split(key, 27)
    L, D, C, F2 = DEPTH, D_MODEL, RWKV_W, 2 * D_FF

    def nrm(i, shape, s=1.0):
        return s * jax.random.normal(ks[i], shape, jnp.float32)

    def near_one(i, shape):
        return 1.0 + nrm(i, shape, 0.05)

    centre3 = jnp.zeros((3,), jnp.float32).at[1].set(1.0)
    centre33 = jnp.zeros((3, 3), jnp.float32).at[1, 1].set(1.0)
    return {
        "x": nrm(0, (BATCH, SEQ, D)),
        "c": nrm(1, (BATCH, D)),
        "ctx": nrm(2, (BATCH, CTX_LEN, D)),
        "c_ctx": nrm(3, (D,)),
        "ada_w": nrm(4, (L, D, 6 * D), 0.5 * D ** -0.5),
        "ada_b": nrm(5, (L, 6 * D), 0.02),
        "norm1_g": near_one(6, (L, D)),
        "norm2_g": near_one(7, (L, D)),
        "w_in": nrm(8, (L, D, PROJ_W), D ** -0.5),
        "rwkv_conv_w": centre3[None, :, None] + nrm(9, (L, 3, 3 * C), 0.1),
        "decay_w0": -1.0 + nrm(10, (L, N_DIR, C), 1.5),
        "decay_w2": nrm(11, (L, N_DIR, DECAY_RANK, C), 0.1 * DECAY_RANK ** -0.5),
        "iclr_a0": nrm(12, (L, N_DIR, C), 0.5),
        "iclr_a2": nrm(13, (L, N_DIR, ICLR_RANK, C), 0.1 * ICLR_RANK ** -0.5),
        "gate_g2": nrm(14, (L, GATE_RANK, C), GATE_RANK ** -0.5),
        "k_k": 0.85 + nrm(15, (L, C), 0.05),
        "k_a": near_one(16, (L, C)),
        "r_k": nrm(17, (L, N_HEADS, HEAD), 0.1),
        "gn_g": near_one(18, (L, C)),
        "gn_b": nrm(19, (L, C), 0.02),
        "fourier_g": near_one(20, (L, FOURIER_W)),
        "w_out": nrm(21, (L, D, D), D ** -0.5),
        "ffn_w_up": nrm(22, (L, D, F2), D ** -0.5),
        "ffn_conv_w": centre33[None, :, :, None] + nrm(23, (L, 3, 3, F2), 0.1),
        "ffn_conv_b": nrm(24, (L, F2), 0.02),
        "ffn_w_down": nrm(25, (L, D_FF, D), D_FF ** -0.5),
        "final_g": near_one(26, (D,)),
    }

def first_block(x, c, ctx, c_ctx, ada_w, ada_b, norm1_g, norm2_g, w_in, rwkv_conv_w,
              decay_w0, decay_w2, iclr_a0, iclr_a2, gate_g2, k_k, k_a, r_k, gn_g, gn_b,
              fourier_g, w_out, ffn_w_up, ffn_conv_w, ffn_conv_b, ffn_w_down, final_g):
    rows = x.shape[1] // GRID_W
    for l in range(DEPTH):
        last = l == DEPTH - 1
        mod_x = jax.nn.silu(c) @ ada_w[l] + ada_b[l]
        mod_c = jax.nn.silu(c_ctx) @ ada_w[l] + ada_b[l]
        sh1, sc1, g1, sh2, sc2, g2 = [m[:, None, :] for m in jnp.split(mod_x, 6, axis=-1)]
        sh1c, sc1c, g1c, sh2c, sc2c, g2c = jnp.split(mod_c, 6, axis=-1)

        h = modulate(rms_norm(x, norm1_g[l]), sh1, sc1)
        hc = modulate(rms_norm(ctx, norm1_g[l]), sh1c, sc1c)
        y, yc = token_mixer(h, hc, w_in[l], rwkv_conv_w[l], decay_w0[l], decay_w2[l],
                            iclr_a0[l], iclr_a2[l], gate_g2[l], k_k[l], k_a[l], r_k[l],
                            gn_g[l], gn_b[l], fourier_g[l], w_out[l], not last)
        x = x + g1 * y
        h = modulate(rms_norm(x, norm2_g[l]), sh2, sc2)
        x = x + g2 * conv_ffn(h, ffn_w_up[l], ffn_conv_w[l], ffn_conv_b[l], ffn_w_down[l], rows)
        if not last:
            ctx = ctx + g1c * yc
            hc = modulate(rms_norm(ctx, norm2_g[l]), sh2c, sc2c)
            ctx = ctx + g2c * conv_ffn(hc, ffn_w_up[l], ffn_conv_w[l], ffn_conv_b[l],
                                       ffn_w_down[l], None)
    return rms_norm(x, final_g)


N_HEADS_2 = 8
HEAD_DIM = 64
D_ATT = N_HEADS_2 * HEAD_DIM
WIN_ROWS_MAX = 8
WIN_COLS = 16
D_CONV = 512
CONV_WIDTH = 31
N_GROUPS = 4
EXPERTS_PER_GROUP = 8
N_EXPERTS = N_GROUPS * EXPERTS_PER_GROUP
TOP_K_IN_GROUP = 2
D_EXPERT = 512
MOE_BLOCK = 128
NEG_INF = -1e30

Q0 = 0
K0 = Q0 + D_ATT
V0 = K0 + D_ATT
GLU0 = V0 + D_ATT
GA0 = GLU0 + 2 * D_CONV
GB0 = GA0 + D_MODEL
D_IN = GB0 + D_MODEL


def rmsnorm(x, g):
    xf = x.astype(jnp.float32)
    y = xf * lax.rsqrt(jnp.mean(xf * xf, axis=-1, keepdims=True) + NORM_EPS)
    return (y * g.astype(jnp.float32)).astype(x.dtype)

def layernorm(x, g, b):
    xf = x.astype(jnp.float32)
    mu = jnp.mean(xf, axis=-1, keepdims=True)
    var = jnp.mean(jnp.square(xf - mu), axis=-1, keepdims=True)
    y = (xf - mu) * lax.rsqrt(var + NORM_EPS)
    return (y * g.astype(jnp.float32) + b.astype(jnp.float32)).astype(x.dtype)

def modulate_2(h, shift, scale):
    return h * (1 + scale) + shift

def split_heads(t):
    return t.reshape(t.shape[0], t.shape[1], N_HEADS_2, HEAD_DIM)

def latent_neighbourhood_attention(q, k, v, k_ctx, v_ctx, rpb):
    B, N, H, hd = q.shape
    rows = N // GRID_W
    kh = min(WIN_ROWS_MAX, rows)
    scale = hd ** -0.5
    q_rows = q.reshape(B, rows, GRID_W, H, hd).transpose(1, 0, 3, 2, 4)
    k_grid = k.reshape(B, rows, GRID_W, H, hd).transpose(0, 3, 1, 2, 4)
    v_grid = v.reshape(B, rows, GRID_W, H, hd).transpose(0, 3, 1, 2, 4)
    cq = jnp.arange(GRID_W)[:, None]
    ck = jnp.arange(GRID_W)[None, :]
    c_start = jnp.clip(cq - WIN_COLS // 2, 0, GRID_W - WIN_COLS)
    col_mask = (ck >= c_start) & (ck < c_start + WIN_COLS)
    band_mask = jnp.broadcast_to(col_mask[:, None, :], (GRID_W, kh, GRID_W)).reshape(GRID_W, kh * GRID_W)
    dc_idx = jnp.clip(ck - cq + WIN_COLS - 1, 0, 2 * WIN_COLS - 2)
    rpb_cols = rpb[:, :, dc_idx]

    def row_block(args):
        q_r, r = args
        r_start = jnp.clip(r - kh // 2, 0, rows - kh)
        k_blk = lax.dynamic_slice_in_dim(k_grid, r_start, kh, axis=2).reshape(B, H, kh * GRID_W, hd)
        v_blk = lax.dynamic_slice_in_dim(v_grid, r_start, kh, axis=2).reshape(B, H, kh * GRID_W, hd)
        dr_idx = r_start + jnp.arange(kh) - r + WIN_ROWS_MAX - 1
        bias = jnp.take(rpb_cols, dr_idx, axis=1)
        bias = bias.transpose(0, 2, 1, 3).reshape(H, GRID_W, kh * GRID_W).astype(jnp.float32)
        s_loc = jnp.einsum('bhqd,bhkd->bhqk', q_r, k_blk, preferred_element_type=jnp.float32) * scale + bias
        s_loc = jnp.where(band_mask, s_loc, NEG_INF)
        s_ctx = jnp.einsum('bhqd,bhkd->bhqk', q_r, k_ctx, preferred_element_type=jnp.float32) * scale
        p = jax.nn.softmax(jnp.concatenate([s_loc, s_ctx], axis=-1), axis=-1).astype(v.dtype)
        n_loc = kh * GRID_W
        return (jnp.einsum('bhqk,bhkd->bhqd', p[..., :n_loc], v_blk)
                + jnp.einsum('bhqk,bhkd->bhqd', p[..., n_loc:], v_ctx))

    o = lax.map(row_block, (q_rows, jnp.arange(rows)))
    return o.transpose(1, 0, 3, 2, 4).reshape(B, N, H * hd)

def context_attention(q_c, k_c, v_c):
    s = jnp.einsum('bhqd,bhkd->bhqk', q_c, k_c, preferred_element_type=jnp.float32) * (HEAD_DIM ** -0.5)
    p = jax.nn.softmax(s, axis=-1).astype(v_c.dtype)
    o = jnp.einsum('bhqk,bhkd->bhqd', p, v_c)
    return o.transpose(0, 2, 1, 3).reshape(q_c.shape[0], q_c.shape[2], D_ATT)

def conformer_conv(glu_in, conv_w, conv_b, ln_g, ln_b, w_out):
    a, g = jnp.split(glu_in, 2, axis=-1)
    u = a * jax.nn.sigmoid(g)
    y = lax.conv_general_dilated(u, conv_w[:, None, :].astype(u.dtype), window_strides=(1,),
                                 padding=[(CONV_WIDTH // 2, CONV_WIDTH // 2)],
                                 dimension_numbers=('NWC', 'WIO', 'NWC'),
                                 feature_group_count=D_CONV) + conv_b
    y = jax.nn.silu(layernorm(y, ln_g, ln_b))
    return y @ w_out

def merge_branches(proj, att, conv_w, conv_b, ln_g, ln_b, w_att_out, w_conv_out, w_o):
    y_att = att @ w_att_out
    y_conv = conformer_conv(proj[..., GLU0:GA0], conv_w, conv_b, ln_g, ln_b, w_conv_out)
    gate_att = jax.nn.sigmoid(proj[..., GA0:GB0])
    gate_conv = jax.nn.sigmoid(proj[..., GB0:D_IN])
    return (gate_att * y_att + gate_conv * y_conv) @ w_o

def hierarchical_moe(h, w_rg, b_rg, w_re, b_re, w_g, w_u, w_d):
    T, D = h.shape
    hf = h.astype(jnp.float32)
    g_logits = hf @ w_rg.astype(jnp.float32) + b_rg.astype(jnp.float32)
    g_idx = jnp.argmax(g_logits, axis=-1)
    p_group = jnp.take_along_axis(jax.nn.softmax(g_logits, axis=-1), g_idx[:, None], axis=-1)
    e_logits = (hf @ w_re.astype(jnp.float32) + b_re.astype(jnp.float32)).reshape(T, N_GROUPS, EXPERTS_PER_GROUP)
    e_sel = jnp.take_along_axis(e_logits, g_idx[:, None, None], axis=1)[:, 0]
    top_v, top_i = lax.top_k(e_sel, TOP_K_IN_GROUP)
    gate = p_group * jax.nn.softmax(top_v, axis=-1)
    flat_e = (g_idx[:, None] * EXPERTS_PER_GROUP + top_i).reshape(-1)
    flat_tok = jnp.repeat(jnp.arange(T), TOP_K_IN_GROUP)
    flat_w = gate.reshape(-1)
    A = T * TOP_K_IN_GROUP
    order = jnp.argsort(flat_e)
    e_s, tok_s, w_s = flat_e[order], flat_tok[order], flat_w[order]
    counts = jnp.bincount(flat_e, length=N_EXPERTS)
    padded = (counts + MOE_BLOCK - 1) // MOE_BLOCK * MOE_BLOCK
    pad_end = jnp.cumsum(padded)
    pad_start = pad_end - padded
    start = jnp.cumsum(counts) - counts
    dest = pad_start[e_s] + (jnp.arange(A) - start[e_s])
    n_blocks = -(-A // MOE_BLOCK) + N_EXPERTS
    P = n_blocks * MOE_BLOCK
    row_tok = jnp.zeros((P,), jnp.int32).at[dest].set(tok_s.astype(jnp.int32))
    row_w = jnp.zeros((P,), jnp.float32).at[dest].set(w_s)
    block_e = jnp.clip(jnp.searchsorted(pad_end, jnp.arange(n_blocks) * MOE_BLOCK, side='right'), 0, N_EXPERTS - 1)

    def run_block(args):
        tok, e, wt = args
        xb = h[tok]
        y = (jax.nn.silu(xb @ w_g[e]) * (xb @ w_u[e])) @ w_d[e]
        return y.astype(jnp.float32) * wt[:, None]

    ys = lax.map(run_block, (row_tok.reshape(n_blocks, MOE_BLOCK), block_e, row_w.reshape(n_blocks, MOE_BLOCK)))
    out = jnp.zeros((T, D), jnp.float32).at[row_tok].add(ys.reshape(P, D))
    return out.astype(h.dtype)

def second_inputs(seed: int = 0) -> dict:
    key = jax.random.key(seed)
    ks = jax.random.split(key, 25)
    L, D = DEPTH, D_MODEL

    def nrm(k, shape, s):
        return jax.random.normal(k, shape, jnp.float32) * s

    return {
        "x": nrm(ks[0], (BATCH, SEQ, D), 1.0),
        "c": nrm(ks[1], (BATCH, D), 1.0),
        "ctx": nrm(ks[2], (BATCH, CTX_LEN, D), 1.0),
        "c_ctx": nrm(ks[3], (D,), 1.0),
        "w_mod": nrm(ks[4], (L, D, 6 * D), 0.5 * D ** -0.5),
        "b_mod": nrm(ks[5], (L, 6 * D), 0.01),
        "norm_mix": 1.0 + nrm(ks[6], (L, D), 0.02),
        "w_in": nrm(ks[7], (L, D, D_IN), D ** -0.5),
        "rpb": nrm(ks[8], (L, N_HEADS_2, 2 * WIN_ROWS_MAX - 1, 2 * WIN_COLS - 1), 0.1),
        "w_att_out": nrm(ks[9], (L, D_ATT, D), D_ATT ** -0.5),
        "conv_w": nrm(ks[10], (L, CONV_WIDTH, D_CONV), CONV_WIDTH ** -0.5),
        "conv_b": nrm(ks[11], (L, D_CONV), 0.01),
        "conv_ln_g": 1.0 + nrm(ks[12], (L, D_CONV), 0.02),
        "conv_ln_b": nrm(ks[13], (L, D_CONV), 0.01),
        "w_conv_out": nrm(ks[14], (L, D_CONV, D), D_CONV ** -0.5),
        "w_o": nrm(ks[15], (L, D, D), D ** -0.5),
        "norm_ffn": 1.0 + nrm(ks[16], (L, D), 0.02),
        "w_router_group": nrm(ks[17], (L, D, N_GROUPS), D ** -0.5),
        "b_router_group": nrm(ks[18], (L, N_GROUPS), 0.01),
        "w_router_expert": nrm(ks[19], (L, D, N_EXPERTS), D ** -0.5),
        "b_router_expert": nrm(ks[20], (L, N_EXPERTS), 0.01),
        "w_exp_gate": nrm(ks[21], (L, N_EXPERTS, D, D_EXPERT), D ** -0.5),
        "w_exp_up": nrm(ks[22], (L, N_EXPERTS, D, D_EXPERT), D ** -0.5),
        "w_exp_down": nrm(ks[23], (L, N_EXPERTS, D_EXPERT, D), D_EXPERT ** -0.5),
        "final_norm": 1.0 + nrm(ks[24], (D,), 0.02),
    }

def second_block(x, c, ctx, c_ctx, w_mod, b_mod, norm_mix, w_in, rpb, w_att_out, conv_w, conv_b,
              conv_ln_g, conv_ln_b, w_conv_out, w_o, norm_ffn, w_router_group, b_router_group,
              w_router_expert, b_router_expert, w_exp_gate, w_exp_up, w_exp_down, final_norm):
    B, N, D = x.shape
    n_ctx = ctx.shape[1]
    for l in range(DEPTH):
        last = l == DEPTH - 1
        m_lat = jax.nn.silu(c) @ w_mod[l] + b_mod[l]
        sh1, sc1, g1, sh2, sc2, g2 = jnp.split(m_lat[:, None, :], 6, axis=-1)
        m_ctx = jax.nn.silu(c_ctx) @ w_mod[l] + b_mod[l]
        sh1c, sc1c, g1c, sh2c, sc2c, g2c = jnp.split(m_ctx, 6, axis=-1)

        h = modulate_2(rmsnorm(x, norm_mix[l]), sh1, sc1)
        hc = modulate_2(rmsnorm(ctx, norm_mix[l]), sh1c, sc1c)
        proj = h @ w_in[l]
        q = split_heads(proj[..., Q0:K0])
        k = split_heads(proj[..., K0:V0])
        v = split_heads(proj[..., V0:GLU0])
        if last:
            kv_c = hc @ w_in[l][:, K0:GLU0]
            proj_c = None
        else:
            proj_c = hc @ w_in[l]
            kv_c = proj_c[..., K0:GLU0]
        k_c = split_heads(kv_c[..., :D_ATT]).transpose(0, 2, 1, 3)
        v_c = split_heads(kv_c[..., D_ATT:]).transpose(0, 2, 1, 3)
        att = latent_neighbourhood_attention(q, k, v, k_c, v_c, rpb[l])
        y = merge_branches(proj, att, conv_w[l], conv_b[l], conv_ln_g[l], conv_ln_b[l],
                           w_att_out[l], w_conv_out[l], w_o[l])
        x_mid = x + g1 * y
        h2 = modulate_2(rmsnorm(x_mid, norm_ffn[l]), sh2, sc2)

        if last:
            tokens = h2.reshape(B * N, D)
        else:
            q_c = split_heads(proj_c[..., Q0:K0]).transpose(0, 2, 1, 3)
            att_c = context_attention(q_c, k_c, v_c)
            y_c = merge_branches(proj_c, att_c, conv_w[l], conv_b[l], conv_ln_g[l], conv_ln_b[l],
                                 w_att_out[l], w_conv_out[l], w_o[l])
            ctx_mid = ctx + g1c * y_c
            h2c = modulate_2(rmsnorm(ctx_mid, norm_ffn[l]), sh2c, sc2c)
            tokens = jnp.concatenate([h2.reshape(B * N, D), h2c.reshape(B * n_ctx, D)], axis=0)
        f = hierarchical_moe(tokens, w_router_group[l], b_router_group[l], w_router_expert[l],
                             b_router_expert[l], w_exp_gate[l], w_exp_up[l], w_exp_down[l])
        x = x_mid + g2 * f[:B * N].reshape(B, N, D)
        if not last:
            ctx = ctx_mid + g2c * f[B * N:].reshape(B, n_ctx, D)
    return rmsnorm(x, final_norm)


def setup_inputs(seed=0):
    out = dict(first_inputs(seed))
    for name, value in second_inputs(seed + 1).items():
        if name != "x":
            out[name + "_2"] = value
    return out


def reference(
    x, c, ctx, c_ctx, ada_w, ada_b, norm1_g, norm2_g, w_in, rwkv_conv_w, decay_w0, decay_w2,
    iclr_a0, iclr_a2, gate_g2, k_k, k_a, r_k, gn_g, gn_b, fourier_g, w_out, ffn_w_up,
    ffn_conv_w, ffn_conv_b, ffn_w_down, final_g, c_2, ctx_2, c_ctx_2, w_mod_2, b_mod_2,
    norm_mix_2, w_in_2, rpb_2, w_att_out_2, conv_w_2, conv_b_2, conv_ln_g_2, conv_ln_b_2,
    w_conv_out_2, w_o_2, norm_ffn_2, w_router_group_2, b_router_group_2, w_router_expert_2,
    b_router_expert_2, w_exp_gate_2, w_exp_up_2, w_exp_down_2, final_norm_2,
):
    x = first_block(
        x, c, ctx, c_ctx, ada_w, ada_b, norm1_g, norm2_g, w_in, rwkv_conv_w, decay_w0, decay_w2,
        iclr_a0, iclr_a2, gate_g2, k_k, k_a, r_k, gn_g, gn_b, fourier_g, w_out, ffn_w_up,
        ffn_conv_w, ffn_conv_b, ffn_w_down, final_g,
    )
    return second_block(
        x, c_2, ctx_2, c_ctx_2, w_mod_2, b_mod_2, norm_mix_2, w_in_2, rpb_2, w_att_out_2,
        conv_w_2, conv_b_2, conv_ln_g_2, conv_ln_b_2, w_conv_out_2, w_o_2, norm_ffn_2,
        w_router_group_2, b_router_group_2, w_router_expert_2, b_router_expert_2, w_exp_gate_2,
        w_exp_up_2, w_exp_down_2, final_norm_2,
    )


_drawn_inputs = setup_inputs


def setup_inputs(seed=0):
    import zlib

    import numpy as np

    out = dict(_drawn_inputs(seed))
    spreads = {}
    factors = {'ctx': 3.136,
     'c_ctx': 5.579,
     'norm1_g': 2.714,
     'norm2_g': 3.098,
     'decay_w2': 8.0,
     'iclr_a2': 5.759,
     'k_k': 8.0,
     'k_a': 5.389,
     'gn_g': 8.0,
     'gn_b': 8.0,
     'fourier_g': 4.579,
     'ffn_conv_b': 6.745,
     'ctx_2': 3.907,
     'b_mod_2': 6.845,
     'norm_mix_2': 8.0,
     'rpb_2': 8.0,
     'conv_b_2': 8.0,
     'conv_ln_g_2': 8.0,
     'conv_ln_b_2': 8.0,
     'norm_ffn_2': 4.977,
     'b_router_group_2': 8.0,
     'b_router_expert_2': 8.0,
     'final_norm_2': 2.832}
    for name, (base, spread) in spreads.items():
        noise = np.random.default_rng([zlib.crc32(name.encode()), seed]).standard_normal(out[name].shape)
        drawn = base * np.exp(spread * noise) if base else spread * noise
        out[name] = jnp.asarray(drawn.astype(out[name].dtype))
    for name, factor in factors.items():
        out[name] = (out[name] * factor).astype(out[name].dtype)
    return out
```

```python
import numpy as np

import concourse.bass as bass
import concourse.mybir as mybir
from concourse.alu_op_type import AluOpType as ALU

ACT = mybir.ActivationFunctionType
F32 = mybir.dt.float32
I32 = mybir.dt.int32
U32 = mybir.dt.uint32
AX = mybir.AxisListType.X
ADD, SUB, MUL, MAX = ALU.add, ALU.subtract, ALU.mult, ALU.max

P = 128
D, KD = 1024, 8
SEQ, CTX = 512, 256
ALL = CTX + SEQ
GRID_W, ROWS = 64, SEQ // 64
CH, KC = 512, 4
HEAD = 64
CHUNK = 64
N_CTX, N_CHUNK = CTX // CHUNK, ALL // CHUNK
D_FF = 2816
KF = D_FF // P
N_EXP, N_GRP, PER_GRP, D_EXP = 32, 4, 8, 512
N_PAIR = SEQ * 2
OVER = 7
N_BLK = N_EXP + OVER
DECAY_SCALE = -float(np.exp(-0.5))
NEG = -1e30
RING, SLOT = 4, 2048


def columns(fields):
    at, out = 0, {}
    for name, n in fields:
        out[name] = at
        at += n
    return out, at


FIELDS = [
    ("norm1_g", 8), ("norm2_g", 8), ("final_g", 8), ("ada_b", 48), ("conv_w", 36), ("w0", 8), ("a0", 8),
    ("k_k", 4), ("k_a", 4), ("r_k", 4), ("gn_g", 4), ("gn_b", 4), ("fourier_g", 4),
    ("ffn_conv_w", 9 * 2 * KF), ("ffn_conv_b", 2 * KF),
    ("b_mod", 48), ("norm_mix", 8), ("norm_ffn", 8), ("final_norm", 8),
    ("conv2_w", 31 * 4), ("conv2_b", 4), ("ln_g", 4), ("ln_b", 4), ("router_b", 36),
    ("eps_norm", 1), ("eps_gn", 1), ("eps_kk", 1), ("zero", 1), ("cc1", 16), ("cc2", 16),
]
COL, N_COL = columns(FIELDS)
CONSTS = [("ident", 128), ("ones", 128), ("head_ones", 128), ("causal", 2 * 128), ("level", 6 * 64),
          ("chunk_start", ALL), ("before", 128), ("eye64", 64), ("pair_mask", 64), ("pair_neg", 64),
          ("expert_id", 32)]
CAT, N_CONST = columns(CONSTS)


def tiled(w, cols):
    k, m = w.shape
    return np.ascontiguousarray(w.reshape(k // P, P, m // cols, cols).transpose(2, 1, 0, 3)).reshape(m // cols, P, -1)


def feature_major(x):
    t, f = x.shape
    return np.ascontiguousarray(x.reshape(t, f // P, P).transpose(2, 1, 0))


def per_partition(v):
    v = np.asarray(v)
    return np.moveaxis(v.reshape(v.shape[:-1] + (v.shape[-1] // P, P)), -1, 0).reshape(P, -1)


def shape_constants():
    c = np.zeros((P, N_CONST), np.float32)
    p = np.arange(P)
    c[:, CAT["ident"]:][:, :128] = np.eye(P)
    c[:, CAT["ones"]:][:, :128] = 1
    c[:, CAT["head_ones"]:][:, :128] = p[:, None] // HEAD == p[None] // HEAD
    s, t = p[:, None] % CHUNK, np.arange(CHUNK)[None]
    causal = np.stack([s < t, s <= t, s > t, s >= t], 1).astype(np.float32)
    c[:, CAT["causal"]:][:, :256] = causal.reshape(P, 256)
    for lv in range(6):
        inner, outer = 1 << lv, 2 << lv
        c[:, CAT["level"] + 64 * lv:][:, :64] = (s // outer == t // outer) & (s // inner != t // inner)
    c[:, CAT["chunk_start"]:][:, :ALL] = (np.arange(ALL) % CHUNK != 0)[None]
    c[:, CAT["before"]:][:, :128] = p[:, None] < p[None]
    c[:, CAT["eye64"]:][:, :64] = s == t
    start = np.clip(t * 0 + p[:, None] % 64 - 8, 0, GRID_W - 16)
    inside = (t >= start) & (t < start + 16)
    c[:, CAT["pair_mask"]:][:, :64] = inside[:, ::-1]
    c[:, CAT["pair_neg"]:][:, :64] = np.where(inside, 0, NEG)[:, ::-1]
    c[:, CAT["expert_id"]:][:, :32] = np.arange(32)[None]
    return c


def blank_table():
    t = np.zeros((P, N_BLK, 2), np.int32)
    t[:, :, 0] = N_PAIR + np.arange(P * N_BLK).reshape(P, N_BLK)
    return t.reshape(P, -1)


def row_ids():
    p, i = np.arange(P)[:, None], np.arange(8)[None]
    tok = p + P * (i // 2)
    return np.stack([2 * tok + i % 2, tok], 2).astype(np.int32).reshape(P, 16)


def fourier_constants():
    t = np.arange(SEQ)
    ang = 2 * np.pi * (np.outer(t, t) % SEQ) / SEQ
    seq = np.stack([np.cos(ang), -np.sin(ang)]) / np.sqrt(SEQ)
    j = np.arange(64)
    a64 = 2 * np.pi * (np.outer(j, j) % 64) / 64
    chan = np.zeros((P, 2, P))
    for g in range(2):
        chan[64 * g:64 * g + 64, 0, 64 * g:64 * g + 64] = np.cos(a64) / 8
        chan[64 * g:64 * g + 64, 1, 64 * g:64 * g + 64] = np.sin(a64) / 8
    seq = seq.reshape(2, 4, P, SEQ).transpose(0, 2, 1, 3)
    return np.ascontiguousarray(seq.reshape(2, P, 4 * SEQ), np.float32), np.ascontiguousarray(chan.reshape(P, 256), np.float32)


def lay_out(i):
    one = {k: np.asarray(v) for k, v in i.items()}
    vec = np.zeros((P, N_COL), np.float32)

    def put(name, a):
        vec[:a.shape[0], COL[name]:COL[name] + a.shape[1]] = a

    for name in ("norm1_g", "norm2_g", "ada_b", "k_k", "k_a", "gn_g", "gn_b", "fourier_g", "ffn_conv_b"):
        put(name, per_partition(one[name][0]))
    put("final_g", per_partition(one["final_g"]))
    put("conv_w", per_partition(one["rwkv_conv_w"][0]))
    put("w0", per_partition(one["decay_w0"][0]))
    put("a0", per_partition(one["iclr_a0"][0]))
    put("r_k", per_partition(one["r_k"][0].reshape(-1)))
    put("ffn_conv_w", per_partition(one["ffn_conv_w"][0].reshape(9, -1)))
    put("b_mod", per_partition(one["b_mod_2"][0]))
    put("norm_mix", per_partition(one["norm_mix_2"][0]))
    put("norm_ffn", per_partition(one["norm_ffn_2"][0]))
    put("final_norm", per_partition(one["final_norm_2"]))
    put("conv2_w", per_partition(one["conv_w_2"][0]))
    put("conv2_b", per_partition(one["conv_b_2"][0]))
    put("ln_g", per_partition(one["conv_ln_g_2"][0]))
    put("ln_b", per_partition(one["conv_ln_b_2"][0]))
    bias = np.concatenate([one["b_router_group_2"][0], one["b_router_expert_2"][0]])
    put("router_b", np.broadcast_to(bias[None], (P, 36)))
    for name, v in (("eps_norm", 1e-6), ("eps_gn", 64e-5), ("eps_kk", 1e-12)):
        vec[:, COL[name]] = v
    for name, a, b in (("cc1", "c", "c_ctx"), ("cc2", "c_2", "c_ctx_2")):
        both = np.stack([one[a][0], one[b]])
        put(name, both.reshape(2, KD, P).transpose(2, 1, 0).reshape(P, 16))

    w_in, w_in2 = one["w_in"][0], one["w_in_2"][0]
    seq_dft, chan_dft = fourier_constants()
    x0 = np.concatenate([one["ctx"][0], one["x"][0]])
    w_up = one["ffn_w_up"][0]
    up = np.stack([w_up[:, :D_FF].reshape(D, KF, P), w_up[:, D_FF:].reshape(D, KF, P)], 2)
    return {
        "vec": vec, "const": shape_constants(), "seq_dft": seq_dft, "chan_dft": chan_dft,
        "x0": feature_major(x0), "ctx2": feature_major(one["ctx_2"][0]),
        "ada1": tiled(one["ada_w"][0], 256), "ada2": tiled(one["w_mod_2"][0], 256),
        "w_in": tiled(w_in, 128), "w_out": tiled(one["w_out"][0], 256),
        "lora": np.concatenate([one["decay_w2"][0].reshape(P, CH), one["iclr_a2"][0].reshape(P, CH)], 1),
        "gate_g2": np.ascontiguousarray(one["gate_g2"][0]),
        "w_up": tiled(np.ascontiguousarray(up.reshape(D, 2 * D_FF)), 256),
        "w_down": np.ascontiguousarray(one["ffn_w_down"][0].reshape(2, 11, P, 8, P).transpose(3, 0, 2, 1, 4)).reshape(16, P, 11 * P),
        "w_in2_q": tiled(w_in2[:, :1024], 256),
        "w_in2_v": tiled(w_in2[:, 1024:1536], 256),
        "w_in2_g": tiled(w_in2[:, 1536:], 256),
        "rpb": np.pad(one["rpb_2"][0][:, :, ::-1].reshape(-1), 64),
        "w_att": tiled(one["w_att_out_2"][0], 512), "w_conv": tiled(one["w_conv_out_2"][0], 512),
        "w_o": tiled(one["w_o_2"][0], 256),
        "w_router": tiled(np.concatenate([one["w_router_group_2"][0], one["w_router_expert_2"][0]], 1), 36)[0],
        "blank": blank_table(), "ids": row_ids(),
        "w_gate": one["w_exp_gate_2"][0].reshape(N_EXP, P, KD * D_EXP),
        "w_upe": one["w_exp_up_2"][0].reshape(N_EXP, P, KD * D_EXP),
        "w_downe": one["w_exp_down_2"][0].reshape(N_EXP, P, 4 * D),
    }


class Core:

    def __init__(self, nc, d, out):
        self.nc, self.d, self.out = nc, d, out
        self.mem = nc.alloc_sbuf_tensor("mem", [P, 53100], F32)
        self.bank = [nc.alloc_psum_tensor(f"bank{i}", [P, 512], F32) for i in range(8)]
        self.vec = self.mem[:, 0:N_COL]
        self.const = self.mem[:, N_COL:N_COL + N_CONST]
        at = N_COL + N_CONST
        self.mod = [self.mem[:, at + 96 * b:at + 96 * b + 96].rearrange("p (m t) -> p m t", t=2) for b in range(2)]
        at += 192
        self.small = self.mem[:, at:at + 64]
        at += 64
        self.ring_at = at
        at += RING * SLOT
        self.decay_at = at
        at += 96
        self.free_at = at
        self.w_loaded = [nc.alloc_semaphore(f"weights_loaded_{i}") for i in range(RING)]
        self.freed = {}
        self.stream = []
        self.sent = 0
        self.named = {}
        self.live = []

    def sem(self, name):
        s = self.named.pop(name, None) or self.nc.alloc_semaphore(name)
        self.live.append(s)
        return s

    def retire(self):
        self.nc.clear_and_free_semaphores(self.live)
        self.nc.all_engine_barrier()
        self.live = []
        self.freed = {g: None for g in self.freed}

    def v(self, name, i=0, n=1):
        return self.vec[:, COL[name] + i:COL[name] + i + n]

    def c(self, name, i=0, n=128):
        return self.const[:, CAT[name] + i:CAT[name] + i + n]

    def at(self, words, n):
        assert self.free_at + words + n <= 53100, (self.free_at + words + n)
        return self.mem[:, self.free_at + words:self.free_at + words + n]

    def slot(self, g, n=SLOT):
        a = self.ring_at + (g % RING) * SLOT
        return self.mem[:, a:a + n]

    def weights_ready(self, pe, g):
        pe.wait_ge(self.w_loaded[g % RING], 16 * (g // RING + 1))

    def frees(self, g0, n, sem, per=1):
        for g in range(n):
            self.freed[g0 + g] = (sem, per * (g + 1))

    def frees_later(self, g0, n, name, per):
        self.named[name] = self.nc.alloc_semaphore(name)
        self.frees(g0, n, self.named[name], per)

    def send_weights(self, sp, until):
        while self.sent < min(until, len(self.stream)):
            g = self.sent
            if g >= RING:
                if g - RING not in self.freed:
                    break
                if self.freed[g - RING]:
                    sp.wait_ge(*self.freed[g - RING])
            src = self.stream[g]
            sp.dma_start(self.slot(g, src.shape[1]), src).then_inc(self.w_loaded[g % RING], 16)
            self.sent += 1


def load_stage(k):
    nc, landed = k.nc, k.sem("parameters_landed")
    with nc.Block("load") as block:
        @block.sync
        def _(sp):
            sp.dma_start(k.vec, k.d["vec"]).then_inc(landed, 16)
            sp.dma_start(k.const, k.d["const"]).then_inc(landed, 16)
            k.send_weights(sp, RING)
            sp.wait_ge(landed, 32)


def mod_stage(k, b, g0, x_load=None):
    nc = k.nc
    silu, silu_done = k.small[:, 32:48], k.sem(f"silu_c_{b}")
    summed, done = k.sem(f"mod_summed_{b}"), k.sem(f"mod_done_{b}")
    k.frees(g0, 24, summed)
    cc = k.v(f"cc{b + 1}", 0, 16)
    with nc.Block(f"mod{b}") as block:
        @block.sync
        def _(sp):
            if x_load:
                sp.dma_start(*x_load[:2]).then_inc(x_load[2], 16)
            k.send_weights(sp, g0 + 24 + RING)

        @block.scalar
        def _(act):
            act.activation(silu, cc, ACT.Silu).then_inc(silu_done, 1)

        @block.tensor
        def _(pe):
            pe.wait_ge(silu_done, 1)
            for g in range(24):
                k.weights_ready(pe, g0 + g)
                w = k.slot(g0 + g).rearrange("p (k m) -> p k m", k=KD)
                for j in range(2):
                    m = 2 * g + j
                    for kt in range(KD):
                        last = pe.matmul(k.bank[0][:, 2 * m:2 * m + 2], w[:, kt, 128 * j:128 * j + 128],
                                         silu[:, 2 * kt:2 * kt + 2], start=kt == 0, stop=kt == KD - 1)
                last.then_inc(summed, 1)

        @block.vector
        def _(dve):
            dve.wait_ge(summed, 24)
            bias = k.v(("ada_b", "b_mod")[b], 0, 48)
            for t in range(2):
                dve.tensor_tensor(k.mod[b][:, :, t], k.bank[0][:, 0:96].rearrange("p (m t) -> p m t", t=2)[:, :, t],
                                  bias, ADD).then_inc(done, 1)
            dve.wait_ge(done, 2)
            for n, a in enumerate((8, 32)):
                dve.tensor_scalar(k.mod[b][:, a:a + 8, :], k.mod[b][:, a:a + 8, :], 1.0, None, ADD).then_inc(done, 1)


def norm_stage(k, name, src, dst, parts, gain, shift, work, ring_to=0, tiles=KD, first=None, after=None):
    nc = k.nc
    width = parts[-1][0] + parts[-1][1]
    squares = k.at(work, 2 * width).rearrange("p (n w) -> p n w", n=2)
    rstd = k.at(work + 2 * width, width)
    gains = k.small[:, 0:2 * tiles].rearrange("p (k n) -> p k n", n=2)
    sq, used, rt, rs, scaled, gained, shifted = (k.sem(f"{name}_{s}") for s in (
        "square_ready", "square_used", "root_ready", "rstd_ready", "scaled", "gain_ready", "shifted"))
    with nc.Block(name) as block:
        @block.sync
        def _(sp):
            if ring_to:
                k.send_weights(sp, ring_to)
            if after:
                sp.wait_ge(shifted if shift else scaled, tiles * len(parts))
                after(sp)

        @block.scalar
        def _(act):
            if first is not None:
                act.wait_ge(*first)
            for kt in range(tiles):
                if kt >= 2:
                    act.wait_ge(used, kt - 1)
                act.activation(squares[:, kt % 2], src[:, kt], ACT.Square).then_inc(sq, 1)
            act.wait_ge(used, tiles)
            for a, n, b in parts:
                act.activation(rstd[:, a:a + n], k.bank[b][:, 0:n], ACT.Sqrt, bias=k.v("eps_norm"),
                               scale=1.0 / (tiles * P)).then_inc(rt, 1)
            if shift:
                for kt in range(tiles):
                    for i, (a, n, b) in enumerate(parts):
                        act.wait_ge(scaled, kt * len(parts) + i + 1)
                        act.activation(dst[:, kt, a:a + n], dst[:, kt, a:a + n], ACT.Identity,
                                       bias=shift(kt, i)).then_inc(shifted, 1)

        @block.tensor
        def _(pe):
            for kt in range(tiles):
                pe.wait_ge(sq, kt + 1)
                for a, n, b in parts:
                    last = pe.matmul(k.bank[b][:, 0:n], k.c("ones"), squares[:, kt % 2, a:a + n],
                                     start=kt == 0, stop=kt == tiles - 1)
                last.then_inc(used, 1)

        @block.vector
        def _(dve):
            for i in range(len(parts)):
                for a, b in gain(i):
                    if b is None:
                        dve.tensor_copy(gains[:, :, i], a).then_inc(gained, 1)
                    else:
                        dve.tensor_tensor(gains[:, :, i], a, b, MUL).then_inc(gained, 1)
            if first is not None:
                dve.wait_ge(*first)
            dve.wait_ge(rt, len(parts))
            dve.reciprocal(rstd, rstd).then_inc(rs, 1)
            dve.wait_ge(rs, 1)
            dve.wait_ge(gained, len(parts))
            for kt in range(tiles):
                for i, (a, n, b) in enumerate(parts):
                    dve.scalar_tensor_tensor(out=dst[:, kt, a:a + n], in0=src[:, kt, a:a + n], scalar=gains[:, kt, i:i + 1],
                                             in1=rstd[:, a:a + n], op0=MUL, op1=MUL).then_inc(scaled, 1)


def in_proj_stage(k, g0, h, u, pad_rkv, bank_of):
    nc = k.nc
    summed, copied, padded = k.sem("in_proj_summed"), k.sem("in_proj_copied"), k.sem("in_proj_padded")
    k.frees(g0, 19, summed)
    with nc.Block("in_proj") as block:
        @block.sync
        def _(sp):
            k.send_weights(sp, g0 + 19 + RING)

        @block.gpsimd
        def _(pool):
            for view in pad_rkv:
                pool.memset(view, 0.0).then_inc(padded, 1)

        @block.tensor
        def _(pe):
            for m in range(19):
                k.weights_ready(pe, g0 + m)
                w = k.slot(g0 + m, 1024).rearrange("p (k m) -> p k m", k=KD)
                if m >= 3:
                    pe.wait_ge(copied, m - 2)
                for n0, n1, b in ((CTX, ALL, 2 * (m % 3)), (0, CTX, 2 * (m % 3) + 1)):
                    if n0 == 0 and not u[m][1]:
                        continue
                    for kt in range(KD):
                        last = pe.matmul(k.bank[b][:, 0:n1 - n0], w[:, kt], h[:, kt, n0:n1],
                                         start=kt == 0, stop=kt == KD - 1)
                last.then_inc(summed, 1)

        @block.scalar
        def _(act):
            for m in range(19):
                act.wait_ge(summed, m + 1)
                lat, ctx = u[m]
                for i, (dst, f) in enumerate(lat):
                    ins = act.activation(dst, k.bank[2 * (m % 3)][:, 0:SEQ], f)
                if ctx:
                    for dst, f in ctx:
                        ins = act.activation(dst, k.bank[2 * (m % 3) + 1][:, 0:CTX], f)
                ins.then_inc(copied, 1)


def conv_stage(k, pads, outs, k_heads, v_tok, store):
    nc = k.nc
    tap0, tap1, conv, sq, summed, rt, rs, kraw, kk, turned, out = (k.sem("conv_" + s) for s in (
        "tap0", "tap1", "done", "square", "summed", "root", "rstd", "kraw", "kk_ready", "v_turned", "v_copied"))
    stored = k.sem("fourier_stored")
    jobs = []
    for i, (pad, dst) in enumerate(zip(pads, outs)):
        for ct in range(KC):
            for a, o, n in (((0, 0, SEQ),) if i == 0 else ((0, 0, CTX), (CTX + 2, CTX, SEQ))):
                jobs.append((pad[:, ct, a:a + n + 2], dst[:, ct, o:o + n], n, 4 * i + ct))
    jobs = jobs[4:12] + jobs[12:] + jobs[:4]
    squares = k.at(0, 2 * ALL).rearrange("p (n w) -> p n w", n=2)
    rstd = k.at(2 * ALL, 2 * ALL).rearrange("p (n w) -> p n w", n=2)
    kf, vf = outs[1], outs[2]
    with nc.Block("conv") as block:
        @block.sync
        def _(sp):
            sp.dma_start(*store).then_inc(stored, 16)
            sp.wait_ge(stored, 16)

        @block.scalar
        def _(act):
            for j, (src, dst, n, t) in enumerate(jobs):
                act.activation(dst, src[:, 0:n], ACT.Identity, scale=k.v("conv_w", t)).then_inc(tap0, 1)
            for ct in range(KC):
                act.wait_ge(kraw, ct + 1)
                if ct >= 2:
                    act.wait_ge(summed, ct - 1)
                act.activation(squares[:, ct % 2], k_heads[:, ct], ACT.Square).then_inc(sq, 1)
            for ct in range(KC):
                act.wait_ge(summed, ct + 1)
                if ct >= 2:
                    act.wait_ge(kk, ct - 1)
                for a, n, b in ((0, CTX, 0), (CTX, SEQ, 1)):
                    ins = act.activation(rstd[:, ct % 2, a:a + n], k.bank[2 * (ct % 4) + b][:, 0:n], ACT.Sqrt,
                                         bias=k.v("eps_kk"))
                ins.then_inc(rt, 1)
            for c in range(N_CHUNK):
                act.wait_ge(turned, c + 1)
                act.activation(v_tok[:, :, c], k.bank[c % 2][:, 0:256].rearrange("p (t i) -> p t i", t=KC),
                               ACT.Copy).then_inc(out, 1)

        @block.vector
        def _(dve):
            for j, (src, dst, n, t) in enumerate(jobs):
                dve.wait_ge(tap0, j + 1)
                dve.scalar_tensor_tensor(out=dst, in0=src[:, 1:n + 1], scalar=k.v("conv_w", 12 + t), in1=dst,
                                         op0=MUL, op1=ADD).then_inc(tap1, 1)
                dve.wait_ge(tap1, j + 1)
                dve.scalar_tensor_tensor(out=dst, in0=src[:, 2:n + 2], scalar=k.v("conv_w", 24 + t), in1=dst,
                                         op0=MUL, op1=ADD).then_inc(conv, 1)
                if j == 7:
                    dve.wait_ge(conv, 8)
                    for ct in range(KC):
                        dve.tensor_scalar(k_heads[:, ct], kf[:, ct], k.v("k_k", ct), None, MUL).then_inc(kraw, 1)
            for ct in range(KC):
                dve.wait_ge(rt, ct + 1)
                dve.reciprocal(rstd[:, ct % 2], rstd[:, ct % 2]).then_inc(rs, 1)
                dve.wait_ge(rs, ct + 1)
                dve.tensor_tensor(k_heads[:, ct], k_heads[:, ct], rstd[:, ct % 2], MUL).then_inc(kk, 1)

        @block.tensor
        def _(pe):
            for ct in range(KC):
                pe.wait_ge(sq, ct + 1)
                for a, n, b in ((0, CTX, 0), (CTX, SEQ, 1)):
                    last = pe.matmul(k.bank[2 * (ct % 4) + b][:, 0:n], k.c("head_ones"), squares[:, ct % 2, a:a + n],
                                     start=True, stop=True)
                last.then_inc(summed, 1)
            pe.wait_ge(conv, 16)
            for c in range(N_CHUNK):
                if c < 2:
                    pe.wait_ge(rt, 1)
                else:
                    pe.wait_ge(out, c - 1)
                for ct in range(KC):
                    for r in (slice(0, 64), slice(64, 128)):
                        last = pe.matmul(k.bank[c % 2][r, 64 * ct:64 * ct + 64], vf[r, ct, 64 * c:64 * c + 64],
                                         k.c("eye64", 0, 64)[r], start=True, stop=True)
                last.then_inc(turned, 1)


def lora_stage(k, wd, ad, lora, sig, a):
    nc = k.nc
    summed, done = k.sem("lora_summed"), k.sem("lora_done")
    with nc.Block("lora") as block:
        @block.tensor
        def _(pe):
            u = 0
            for src, w0, dst in ((wd, 0, sig), (ad, CH, a)):
                for d in range(2):
                    r = slice(64 * d, 64 * d + 64)
                    for ct in range(KC):
                        if u >= 4:
                            pe.wait_ge(done, u - 3)
                        for x, n, b in ((0, CTX, 0), (CTX, SEQ, 1)):
                            last = pe.matmul(k.bank[2 * (u % 4) + b][:, 0:n], lora[r, w0 + P * ct:w0 + P * ct + P],
                                             src[r, x:x + n], start=True, stop=True)
                        last.then_inc(summed, 1)
                        u += 1

        @block.scalar
        def _(act):
            u = 0
            for name, dst in (("w0", sig), ("a0", a)):
                for d in range(2):
                    for ct in range(KC):
                        act.wait_ge(summed, u + 1)
                        for x, n, b in ((0, CTX, 0), (CTX, SEQ, 1)):
                            ins = act.activation(dst[:, d, ct, x:x + n], k.bank[2 * (u % 4) + b][:, 0:n], ACT.Sigmoid,
                                                 bias=k.v(name, 4 * d + ct))
                        ins.then_inc(done, 1)
                        u += 1


def step_of(d, c):
    return c if d == 0 else (N_CTX - 1 - c if c < N_CTX else N_CTX + N_CHUNK - 1 - c)


chunk_at = step_of


def factor_stage(k, A, R, K, B, r, kf, kk, vf, bonus_v, chunk_decay, tmp):
    nc = k.nc
    T1, T2, T3 = tmp[:, 0:ALL], tmp[:, ALL:2 * ALL], tmp[:, 2 * ALL:3 * ALL]
    one_minus, prefix, before, upto, e_before, e_upto, e_inv, a_done, r_done, pc_done, kf1, kd, k_done, prod, ba, \
        b_done, bonus_summed, bonus_done = (k.sem("factor_" + n) for n in (
            "one_minus_k_a", "prefix", "sum_before", "sum_upto", "exp_before", "exp_upto", "exp_inverse", "a", "r",
            "chunk_decay", "k_scale", "k_dir", "k", "bonus_product", "kk_a", "b", "bonus_summed", "bonus"))
    omka = k.small[:, 0:4]
    split = lambda x: x.rearrange("p (c t) -> p c t", t=CHUNK)
    with nc.Block("factors") as block:
        @block.vector
        def _(dve):
            dve.tensor_scalar(omka, k.v("k_a", 0, 4), -1.0, 1.0, MUL, ADD).then_inc(one_minus, 1)
            dve.wait_ge(one_minus, 1)
            for u in range(8):
                d, ct = divmod(u, 4)
                sig, a = A[:, d, ct], B[:, d, ct]
                if u:
                    dve.wait_ge(b_done, u)
                if d == 0:
                    dve.tensor_tensor_scan(T1, k.c("chunk_start", 0, ALL), sig, 0.0, MUL, ADD).then_inc(upto, 1)
                    dve.wait_ge(upto, u + 1)
                    dve.tensor_tensor(T2, T1, sig, SUB).then_inc(before, 1)
                else:
                    dve.tensor_tensor_scan(T1, k.c("chunk_start", 0, ALL), sig, 0.0, MUL, ADD).then_inc(prefix, 1)
                    dve.wait_ge(prefix, u - 3)
                    total = split(T1)[:, :, CHUNK - 1:CHUNK].broadcast_to([P, N_CHUNK, CHUNK])
                    dve.tensor_tensor(split(T2), total, split(T1), SUB).then_inc(before, 1)
                    dve.wait_ge(before, u + 1)
                    dve.tensor_tensor(T1, T2, sig, ADD).then_inc(upto, 1)
                dve.wait_ge(e_before, u + 1)
                dve.tensor_tensor(A[:, d, ct], kk[:, ct], T2, MUL).then_inc(a_done, 1)
                dve.wait_ge(e_upto, u + 1)
                dve.tensor_tensor(R[:, d, ct], r[:, ct], T3[:, CTX:ALL], MUL).then_inc(r_done, 1)
                last = split(T3)[:, :, CHUNK - 1] if d == 0 else split(T3)[:, :, 0]
                if d == 0:
                    dve.tensor_copy(chunk_decay[:, :, u], last).then_inc(pc_done, 1)
                else:
                    dve.tensor_copy(chunk_decay[:, 0:N_CTX, u], last[:, N_CTX - 1::-1])
                    dve.tensor_copy(chunk_decay[:, N_CTX:N_CHUNK, u], last[:, N_CHUNK - 1:N_CTX - 1:-1]).then_inc(pc_done, 1)
                dve.wait_ge(a_done, u + 1)
                dve.tensor_scalar(T2, a, k.v("k_a", ct), omka[:, ct:ct + 1], MUL, ADD).then_inc(kf1, 1)
                dve.wait_ge(kf1, u + 1)
                dve.tensor_tensor(T2, T2, kf[:, ct], MUL).then_inc(kd, 1)
                dve.wait_ge(kd, u + 1)
                dve.wait_ge(e_inv, u + 1)
                dve.tensor_tensor(K[:, d, ct], T2, T1, MUL).then_inc(k_done, 1)
                dve.wait_ge(pc_done, u + 1)
                dve.scalar_tensor_tensor(out=T3[:, CTX:ALL], in0=T2[:, CTX:ALL], scalar=k.v("r_k", ct), in1=r[:, ct],
                                         op0=MUL, op1=MUL).then_inc(prod, 1)
                dve.wait_ge(k_done, u + 1)
                dve.tensor_tensor(T1, T1, a, MUL).then_inc(ba, 1)
                dve.wait_ge(ba, u + 1)
                dve.tensor_tensor(B[:, d, ct], T1, kk[:, ct], MUL).then_inc(b_done, 1)
            dve.wait_ge(b_done, 8)
            dve.wait_ge(bonus_summed, 8)
            for ct in range(KC):
                dve.tensor_tensor(bonus_v[:, ct], k.bank[ct][:, 0:SEQ], vf[:, ct, CTX:ALL], MUL).then_inc(bonus_done, 1)

        @block.scalar
        def _(act):
            for u in range(8):
                act.wait_ge(before, u + 1)
                act.wait_ge(upto, u + 1)
                act.activation(T2, T2, ACT.Exp, scale=DECAY_SCALE).then_inc(e_before, 1)
                if u:
                    act.wait_ge(bonus_summed, u)
                act.activation(T3, T1, ACT.Exp, scale=DECAY_SCALE).then_inc(e_upto, 1)
                act.wait_ge(e_upto, u + 1)
                act.activation(T1, T1, ACT.Exp, scale=-DECAY_SCALE).then_inc(e_inv, 1)

        @block.tensor
        def _(pe):
            for u in range(8):
                d, ct = divmod(u, 4)
                pe.wait_ge(prod, u + 1)
                pe.matmul(k.bank[ct][:, 0:SEQ], k.c("head_ones"), T3[:, CTX:ALL], start=d == 0, stop=d == 1,
                          skip_group_check=True).then_inc(bonus_summed, 1)


def chunk_at(d, n):
    return n if d == 0 else (N_CTX - 1 - n if n < N_CTX else N_CTX + N_CHUNK - 1 - n)


def scan_stage(k, A, R, K, B, v_tok, Y, chunk_decay, work):
    nc = k.nc
    off = [work]

    def buf(n=1):
        off[0] += 512 * n
        x = k.at(off[0] - 512 * n, 512 * n)
        return x.rearrange("p (n c) -> p n c", n=n)

    Mba, Mka, Mbr, Mkr, Tt, KT, BT = buf(), buf(2), buf(2), buf(2), buf(2), buf(2), buf(2)
    T, W, Z, Un, S, St, E = buf(), buf(), buf(), buf(), buf(), buf(), buf(2)
    GA, GB, BW, BT_, BTT, BX, BZ, BU = k.bank
    s = {n: k.sem("scan_" + n) for n in (
        "g_ba", "g_ka", "g_br", "g_kr", "mba", "mka", "mbr", "mkr", "e", "e1", "t", "tt", "w_mm", "w", "t_mm", "tt_mm",
        "k_turned", "kt", "b_turned", "bt", "z_mm", "z", "u_mm", "un", "y_mm", "y", "s_mm", "st", "s")}
    LV = 5
    heads = (slice(0, 64), slice(64, 128))
    pairs = [(q, q // 4, q % 4) for q in range(8)]
    col = lambda q: slice(64 * q, 64 * q + 64)
    tok = lambda x, c, base=0: x[:, :, 64 * (c - base):64 * (c - base) + 64]
    with_r = lambda n: max(0, n - N_CTX)
    causal = k.c("causal", 0, 256).rearrange("p (d x t) -> p d x t", d=2, x=2)
    eye = k.c("eye64", 0, 64).rearrange("p (q t) -> p q t", q=1).broadcast_to([P, 8, 64])
    eight = lambda x: x.rearrange("p (q t) -> p q t", q=8)
    level = lambda l: k.c("level", 64 * (l - 1), 64).rearrange("p (q t) -> p q t", q=1).broadcast_to([P, 8, 64])

    with nc.Block("scan") as block:
        @block.tensor
        def _(pe):
            def products(bank, *terms):
                for q, d, ct in pairs:
                    for r in heads:
                        for i, term in enumerate(terms):
                            a, b = term(q, d, ct, r)
                            last = pe.matmul(bank[r, col(q)], a, b, start=i == 0, stop=i == len(terms) - 1,
                                             skip_group_check=True)
                return last

            def gram(bank, X, Yv, base, p):
                return products(bank, lambda q, d, ct, r: (
                    X[r, d, ct, 64 * chunk_at(d, p):64 * chunk_at(d, p) + 64],
                    Yv[r, d, ct, 64 * (chunk_at(d, p) - base):64 * (chunk_at(d, p) - base) + 64]))

            def level_w(p, l):
                pe.wait_ge(s["e"], 6 * p + l)
                pe.wait_ge(s["t"], LV * p + l - 1)
                if LV * p + l - 2 > 0:
                    pe.wait_ge(s["w"], LV * p + l - 2)
                products(BW, lambda q, d, ct, r: (E[r, l % 2, col(q)], T[r, 0, col(q)])).then_inc(s["w_mm"], 1)

            def level_t(p, l):
                pe.wait_ge(s["w"], LV * p + l - 1)
                pe.wait_ge(s["tt"], 6 * p + l - 1)
                if l < 6:
                    products(BT_, lambda q, d, ct, r: (Tt[r, p % 2, col(q)], W[r, 0, col(q)])).then_inc(s["t_mm"], 1)
                products(BTT, lambda q, d, ct, r: (W[r, 0, col(q)], Tt[r, p % 2, col(q)])).then_inc(s["tt_mm"], 1)

            for it in range(N_CHUNK + 1):
                p, j = it, it - 1
                prep, solve = p < N_CHUNK, j >= 0
                if prep:
                    if p:
                        if with_r(p) > with_r(p - 1):
                            pe.wait_ge(s["mbr"], with_r(p))
                            pe.wait_ge(s["mkr"], with_r(p))
                        else:
                            pe.wait_ge(s["mba"], p)
                            pe.wait_ge(s["mka"], p)
                    gram(GA, B, A, 0, p).then_inc(s["g_ba"], 1)
                    gram(GB, K, A, 0, p).then_inc(s["g_ka"], 1)
                if solve:
                    pe.wait_ge(s["s"], j + 1)
                    pe.wait_ge(s["mka"], j + 1)
                    products(BZ, lambda q, d, ct, r: (A[r, d, ct, 64 * chunk_at(d, j):64 * chunk_at(d, j) + 64], S[r, 0, col(q)]),
                             lambda q, d, ct, r: (Mka[r, j % 2, col(q)], v_tok[r, ct, chunk_at(d, j)])).then_inc(s["z_mm"], 1)
                if prep:
                    pe.wait_ge(s["e"], 6 * p + 1)
                    if p:
                        pe.wait_ge(s["t"], LV * p)
                    products(BT_, lambda q, d, ct, r: (E[r, 1, col(q)], k.c("eye64", 0, 64)[r])).then_inc(s["e1"], 1)
                    if p >= N_CTX:
                        pe.wait_ge(s["mba"], p + 1)
                        gram(GA, B, R, N_CTX, p).then_inc(s["g_br"], 1)
                        pe.wait_ge(s["mka"], p + 1)
                        gram(GB, K, R, N_CTX, p).then_inc(s["g_kr"], 1)
                if solve:
                    pe.wait_ge(s["z"], j + 1)
                    pe.wait_ge(s["tt"], 6 * (j + 1))
                    products(BU, lambda q, d, ct, r: (Tt[r, j % 2, col(q)], Z[r, 0, col(q)])).then_inc(s["u_mm"], 1)
                if prep:
                    level_w(p, 2)
                    if p:
                        pe.wait_ge(s["bt"], p)
                    products(BX, lambda q, d, ct, r: (K[r, d, ct, 64 * chunk_at(d, p):64 * chunk_at(d, p) + 64],
                                                      k.c("eye64", 0, 64)[r])).then_inc(s["k_turned"], 1)
                    level_t(p, 2)
                    level_w(p, 3)
                if solve and j >= N_CTX:
                    pe.wait_ge(s["kt"], min(p + 1, N_CHUNK))
                    pe.wait_ge(s["bt"], j + 1)
                    pe.wait_ge(s["un"], j + 1)
                    pe.wait_ge(s["mkr"], with_r(j + 1))
                    pe.wait_ge(s["mbr"], with_r(j + 1))
                    products(BX, lambda q, d, ct, r: (S[r, 0, col(q)], R[r, d, ct, 64 * (chunk_at(d, j) - N_CTX):64 * (chunk_at(d, j) - N_CTX) + 64]),
                             lambda q, d, ct, r: (v_tok[r, ct, chunk_at(d, j)], Mkr[r, j % 2, col(q)]),
                             lambda q, d, ct, r: (Un[r, 0, col(q)], Mbr[r, j % 2, col(q)])).then_inc(s["y_mm"], 1)
                if prep:
                    level_t(p, 3)
                    level_w(p, 4)
                if solve and j < N_CHUNK - 1:
                    pe.wait_ge(s["un"], j + 1)
                    pe.wait_ge(s["kt"], j + 1)
                    pe.wait_ge(s["bt"], j + 1)
                    pe.wait_ge(s["z"], j + 1)
                    products(BZ, lambda q, d, ct, r: (KT[r, j % 2, col(q)], v_tok[r, ct, chunk_at(d, j)]),
                             lambda q, d, ct, r: (BT[r, j % 2, col(q)], Un[r, 0, col(q)])).then_inc(s["s_mm"], 1)
                if prep:
                    level_t(p, 4)
                    level_w(p, 5)
                    pe.wait_ge(s["kt"], p + 1)
                    if solve and j >= N_CTX:
                        pe.wait_ge(s["y"], with_r(j + 1))
                    products(BX, lambda q, d, ct, r: (B[r, d, ct, 64 * chunk_at(d, p):64 * chunk_at(d, p) + 64],
                                                      k.c("eye64", 0, 64)[r])).then_inc(s["b_turned"], 1)
                    level_t(p, 5)
                    level_w(p, 6)
                    level_t(p, 6)

        @block.gpsimd
        def _(pool):
            for p in range(N_CHUNK):
                pool.wait_ge(s["mba"], p + 1)
                for l in range(1, 7):
                    if l == 1 and p:
                        pool.wait_ge(s["w_mm"], LV * p - 1)
                    if l == 2 and p:
                        pool.wait_ge(s["w_mm"], LV * p)
                    if l == 3:
                        pool.wait_ge(s["e1"], p + 1)
                        pool.wait_ge(s["tt"], 6 * p + 1)
                    if l > 3:
                        pool.wait_ge(s["w_mm"], LV * p + l - 3)
                    pool.tensor_tensor(eight(E[:, l % 2]), eight(Mba[:, 0]), level(l), MUL).then_inc(s["e"], 1)

        @block.scalar
        def _(act):
            for it in range(N_CHUNK + 1):
                p, j = it, it - 1
                prep, solve = p < N_CHUNK, j >= 0

                def copy_w(l):
                    act.wait_ge(s["w_mm"], LV * p + l - 1)
                    act.activation(W[:, 0], BW[:, :], ACT.Copy).then_inc(s["w"], 1)

                if solve:
                    act.wait_ge(s["z_mm"], j + 1)
                    act.activation(Z[:, 0], BZ[:, :], ACT.Copy).then_inc(s["z"], 1)
                    act.wait_ge(s["u_mm"], j + 1)
                    act.activation(Un[:, 0], BU[:, :], ACT.Copy, scale=-1.0).then_inc(s["un"], 1)
                if prep:
                    copy_w(2)
                    act.wait_ge(s["k_turned"], p + 1)
                    act.activation(KT[:, p % 2], BX[:, :], ACT.Copy).then_inc(s["kt"], 1)
                    copy_w(3)
                    copy_w(4)
                    copy_w(5)
                    act.wait_ge(s["b_turned"], p + 1)
                    act.activation(BT[:, p % 2], BX[:, :], ACT.Copy).then_inc(s["bt"], 1)
                    copy_w(6)

        @block.vector
        def _(dve):
            dve.memset(S[:, 0], 0.0).then_inc(s["s"], 1)

            def masked(dst, bank, x, ready, done, n):
                dve.wait_ge(s[ready], n)
                m = causal[:, :, x:x + 1].broadcast_to([P, 2, 4, 64])
                dve.tensor_tensor(dst.rearrange("p (d c t) -> p d c t", d=2, c=4),
                                  bank[:, :].rearrange("p (d c t) -> p d c t", d=2, c=4), m, MUL).then_inc(s[done], 1)

            for it in range(N_CHUNK + 1):
                p, j = it, it - 1
                prep, solve = p < N_CHUNK, j >= 0

                def level_update(l):
                    if l < 6:
                        dve.wait_ge(s["t_mm"], (LV - 1) * p + l - 1)
                        dve.tensor_tensor(T[:, 0], T[:, 0], BT_[:, :], SUB).then_inc(s["t"], 1)
                    dve.wait_ge(s["tt_mm"], LV * p + l - 1)
                    dve.tensor_tensor(Tt[:, p % 2], Tt[:, p % 2], BTT[:, :], SUB).then_inc(s["tt"], 1)

                if prep:
                    if p:
                        dve.wait_ge(s["e"], 6 * p)
                    masked(Mba[:, 0], GA, 0, "g_ba", "mba", p + 1)
                    masked(Mka[:, p % 2], GB, 0, "g_ka", "mka", p + 1)
                    dve.wait_ge(s["e1"], p + 1)
                    dve.tensor_tensor(eight(T[:, 0]), eye, eight(BT_[:, :]), SUB).then_inc(s["t"], 1)
                    dve.wait_ge(s["e"], 6 * p + 1)
                    dve.tensor_tensor(eight(Tt[:, p % 2]), eye, eight(E[:, 1]), SUB).then_inc(s["tt"], 1)
                    if p >= N_CTX:
                        masked(Mbr[:, p % 2], GA, 1, "g_br", "mbr", with_r(p + 1))
                        masked(Mkr[:, p % 2], GB, 1, "g_kr", "mkr", with_r(p + 1))
                    level_update(2)
                if solve and j >= N_CTX:
                    dve.wait_ge(s["y_mm"], with_r(j + 1))
                    for d in range(2):
                        c = chunk_at(d, j) - N_CTX
                        y = Y[:, :, 64 * c:64 * c + 64]
                        part = BX[:, 256 * d:256 * d + 256].rearrange("p (c t) -> p c t", c=4)
                        first = j < N_CTX + (N_CHUNK - N_CTX) // 2
                        ins = dve.tensor_copy(y, part) if first else dve.tensor_tensor(y, y, part, ADD)
                    ins.then_inc(s["y"], 1)
                if prep:
                    level_update(3)
                if solve and j < N_CHUNK - 1:
                    dve.wait_ge(s["s_mm"], j + 1)
                    dve.tensor_tensor(St[:, 0], S[:, 0], BZ[:, :], ADD).then_inc(s["st"], 1)
                    dve.wait_ge(s["st"], j + 1)
                    decay = chunk_decay[:, j, :].rearrange("p (q t) -> p q t", t=1).broadcast_to([P, 8, 64])
                    dve.tensor_tensor(eight(S[:, 0]), eight(St[:, 0]), decay, MUL).then_inc(s["s"], 1)
                if prep:
                    level_update(4)
                    level_update(5)
                    level_update(6)


def rwkv_out_stage(k, Y, bonus_v, gate_in, g2, rw, work, loads, landed):
    nc = k.nc
    centred = k.at(work, 4 * SEQ).rearrange("p (c t) -> p c t", c=4)
    squares = k.at(work + 2048, 4 * SEQ).rearrange("p (c t) -> p c t", c=4)
    rstd = k.at(work + 4096, 4 * SEQ).rearrange("p (c t) -> p c t", c=4)
    s = {n: k.sem("rwkv_out_" + n) for n in ("mean_mm", "centred", "sq", "var_mm", "root", "rstd", "scaled", "based",
                                            "gate_mm", "done")}
    with nc.Block("rwkv_out") as block:
        @block.sync
        def _(sp):
            for dst, src in loads:
                sp.dma_start(dst, src).then_inc(landed, 16)
            sp.wait_ge(landed, 16 * len(loads))

        @block.tensor
        def _(pe):
            for ct in range(KC):
                pe.matmul(k.bank[ct][:, :], k.c("head_ones"), Y[:, ct], start=True, stop=True).then_inc(s["mean_mm"], 1)
            for ct in range(KC):
                pe.wait_ge(s["sq"], ct + 1)
                pe.matmul(k.bank[4 + ct][:, :], k.c("head_ones"), squares[:, ct], start=True, stop=True).then_inc(s["var_mm"], 1)
            pe.wait_ge(landed, 16 * len(loads))
            for ct in range(KC):
                pe.wait_ge(s["centred"], ct + 1)
                pe.matmul(k.bank[ct][:, :], g2[:, P * ct:P * ct + P], gate_in, start=True, stop=True).then_inc(s["gate_mm"], 1)

        @block.scalar
        def _(act):
            for ct in range(KC):
                act.wait_ge(s["centred"], ct + 1)
                act.activation(squares[:, ct], centred[:, ct], ACT.Square).then_inc(s["sq"], 1)
            for ct in range(KC):
                act.wait_ge(s["var_mm"], ct + 1)
                act.activation(rstd[:, ct], k.bank[4 + ct][:, :], ACT.Sqrt, bias=k.v("eps_gn"), scale=1.0 / HEAD).then_inc(s["root"], 1)

        @block.vector
        def _(dve):
            for ct in range(KC):
                dve.wait_ge(s["mean_mm"], ct + 1)
                dve.scalar_tensor_tensor(out=centred[:, ct], in0=k.bank[ct][:, :], scalar=-1.0 / HEAD, in1=Y[:, ct],
                                         op0=MUL, op1=ADD).then_inc(s["centred"], 1)
            for ct in range(KC):
                dve.wait_ge(s["root"], ct + 1)
                dve.reciprocal(rstd[:, ct], rstd[:, ct]).then_inc(s["rstd"], 1)
                dve.wait_ge(s["rstd"], ct + 1)
                dve.scalar_tensor_tensor(out=Y[:, ct], in0=centred[:, ct], scalar=k.v("gn_g", ct), in1=rstd[:, ct],
                                         op0=MUL, op1=MUL).then_inc(s["scaled"], 1)
                dve.wait_ge(s["scaled"], ct + 1)
                dve.scalar_tensor_tensor(out=Y[:, ct], in0=Y[:, ct], scalar=k.v("gn_b", ct), in1=bonus_v[:, ct],
                                         op0=ADD, op1=ADD).then_inc(s["based"], 1)
                dve.wait_ge(s["based"], ct + 1)
                dve.wait_ge(s["gate_mm"], ct + 1)
                dve.tensor_tensor(rw[:, ct], Y[:, ct], k.bank[ct][:, :], MUL).then_inc(s["done"], 1)


def fourier_stage(k, u, seq, chan, mixed, parts):
    nc = k.nc
    chan_mm, chan_out, seq_mm, seq_out = (k.sem("fourier_" + n) for n in ("channels", "channels_out", "tokens", "tokens_out"))
    with nc.Block("fourier") as block:
        @block.tensor
        def _(pe):
            for tt in range(4):
                for ct in range(KC):
                    i = 4 * tt + ct
                    if i >= 4:
                        pe.wait_ge(chan_out, i - 3)
                    pe.matmul(k.bank[i % 4][:, 0:256], u[:, ct, P * tt:P * tt + P], chan, start=True, stop=True).then_inc(chan_mm, 1)
            pe.wait_ge(chan_out, 16)
            for ct in range(KC):
                for i in range(8):
                    last = pe.matmul(k.bank[4 + ct][:, :], parts[:, i % 4, ct, P * (i // 4):P * (i // 4) + P],
                                     seq[:, i // 4, i % 4], start=i == 0, stop=i == 7)
                last.then_inc(seq_mm, 1)

        @block.scalar
        def _(act):
            for i in range(16):
                act.wait_ge(chan_mm, i + 1)
                act.activation(parts[:, i // 4, i % 4], k.bank[i % 4][:, 0:256], ACT.Copy).then_inc(chan_out, 1)
            for ct in range(KC):
                act.wait_ge(seq_mm, ct + 1)
                act.activation(mixed[:, ct], k.bank[4 + ct][:, :], ACT.Copy).then_inc(seq_out, 1)


def residual_stage(k, name, g0, per, tiles_of, n_k, rhs, gate, x, dst, ring_to):
    nc = k.nc
    summed, done = k.sem(name + "_summed"), k.sem(name + "_done")
    with nc.Block(name) as block:
        @block.sync
        def _(sp):
            k.send_weights(sp, ring_to)

        @block.tensor
        def _(pe):
            for m in range(KD):
                if m >= 4:
                    pe.wait_ge(done, m - 3)
                pieces = tiles_of(m)
                n = sum(len(cols) for _, cols in pieces)
                i = 0
                for g, cols in pieces:
                    k.weights_ready(pe, g)
                    for w, kt in cols:
                        last = pe.matmul(k.bank[m % 4][:, :], w, rhs[:, kt], start=i == 0, stop=i == n - 1)
                        i += 1
                    if g != pieces[-1][0]:
                        last.then_inc(summed, 1)
                last.then_inc(summed, 1)

        @block.vector
        def _(dve):
            for m in range(KD):
                dve.wait_ge(summed, per * (m + 1))
                dve.scalar_tensor_tensor(out=dst[:, m], in0=k.bank[m % 4][:, :], scalar=gate(m), in1=x[:, m],
                                         op0=MUL, op1=ADD).then_inc(done, 1)


def ffn_up_stage(k, g0, h, hidden, work):
    nc = k.nc
    NP = 3
    PADW = (ROWS + 2) * (GRID_W + 2)
    pad = k.at(work, NP * 2 * PADW).rearrange("p (n h r c) -> p n h r c", n=NP, h=2, r=ROWS + 2)
    acc = k.at(work + NP * 2 * PADW, 2 * 2 * SEQ).rearrange("p (n h r c) -> p n h r c", n=2, h=2, r=ROWS)
    s = {n: k.sem("ffn_" + n) for n in ("zeroed", "up_mm", "padded", "tap", "tapped", "silu", "hidden")}
    k.frees(g0, KF, s["up_mm"])
    flat = lambda x: x.rearrange("p r c -> p (r c)")
    with nc.Block("ffn_up") as block:
        @block.sync
        def _(sp):
            k.send_weights(sp, g0 + KF + RING)

        @block.gpsimd
        def _(pool):
            pool.memset(k.at(work, NP * 2 * PADW), 0.0).then_inc(s["zeroed"], 1)

        @block.tensor
        def _(pe):
            for m in range(KF):
                k.weights_ready(pe, g0 + m)
                w = k.slot(g0 + m).rearrange("p (k h m) -> p k h m", k=KD, h=2)
                if m >= 3:
                    pe.wait_ge(s["padded"], m - 2)
                for h2 in range(2):
                    for kt in range(KD):
                        last = pe.matmul(k.bank[2 * (m % 3) + h2][:, :], w[:, kt, h2], h[:, kt], start=kt == 0, stop=kt == KD - 1)
                last.then_inc(s["up_mm"], 1)

        @block.scalar
        def _(act):
            act.wait_ge(s["zeroed"], 1)
            for m in range(KF + 1):
                if m < KF:
                    act.wait_ge(s["up_mm"], m + 1)
                    if m >= NP:
                        act.wait_ge(s["tapped"], 2 * (m - NP + 1))
                    for h2 in range(2):
                        ins = act.activation(pad[:, m % NP, h2, 1:ROWS + 1, 1:GRID_W + 1],
                                             k.bank[2 * (m % 3) + h2][:, :].rearrange("p (r c) -> p r c", r=ROWS), ACT.Copy)
                    ins.then_inc(s["padded"], 1)
                if m >= 1:
                    act.wait_ge(s["tapped"], 2 * m - 1)
                    g = flat(acc[:, (m - 1) % 2, 0])
                    act.activation(g, g, ACT.Silu).then_inc(s["silu"], 1)

        @block.vector
        def _(dve):
            n = 0
            for m in range(KF):
                dve.wait_ge(s["padded"], m + 1)
                for h2 in range(2):
                    t = m + KF * h2
                    a = acc[:, m % 2, h2]
                    for i in range(9):
                        src = pad[:, m % NP, h2, i // 3:i // 3 + ROWS, i % 3:i % 3 + GRID_W]
                        w = k.v("ffn_conv_w", i * 2 * KF + t)
                        if i == 0:
                            ins = dve.tensor_scalar(a, src, w, k.v("ffn_conv_b", t), MUL, ADD)
                        else:
                            dve.wait_ge(s["tap"], n)
                            ins = dve.scalar_tensor_tensor(out=a, in0=src, scalar=w, in1=a, op0=MUL, op1=ADD)
                        if i < 8:
                            ins.then_inc(s["tap"], 1)
                            n += 1
                        else:
                            ins.then_inc(s["tapped"], 1)
                dve.wait_ge(s["silu"], m + 1)
                dve.wait_ge(s["tapped"], 2 * m + 2)
                dve.tensor_tensor(hidden[:, m], flat(acc[:, m % 2, 0]), flat(acc[:, m % 2, 1]), MUL).then_inc(s["hidden"], 1)


def block_one(k):
    nc, d = k.nc, k.d
    three = lambda at, n, w: k.at(at, n * w).rearrange("p (n w) -> p n w", n=n)
    four = lambda at, t: k.at(at, 2 * 4 * t).rearrange("p (d c t) -> p d c t", d=2, c=4)
    g_ada, g_in, g_out, g_up, g_down = 0, 24, 43, 47, 69
    x_landed = k.sem("x_landed")
    h, x0 = three(0, KD, ALL), three(6144, KD, ALL)
    mod_stage(k, 0, g_ada, x_load=(k.at(6144, KD * ALL), d["x0"].rearrange("p k t -> p (k t)"), x_landed))
    m1 = k.mod[0]
    norm_stage(k, "norm1", x0, h, [(0, CTX, 0), (CTX, SEQ, 1)],
               gain=lambda i: [(m1[:, 8:16, 1 - i], k.v("norm1_g", 0, 8))],
               shift=lambda kt, i: m1[:, kt, 1 - i:2 - i], work=12288, first=(x_landed, 16))
    kp, vp, rp = three(12288, 4, 772), three(15376, 4, 772), three(18464, 4, 514)
    uf = three(6144, 4, SEQ)
    gd, wd, ad = k.at(29696, SEQ), k.at(30208, ALL), k.at(30976, ALL)
    ID = ACT.Copy
    u = {}
    for ct in range(4):
        u[ct] = ([(uf[:, ct], ID)], None)
        u[4 + ct] = ([(rp[:, ct, 1:1 + SEQ], ID)], None)
        for o, pad in ((8, kp), (12, vp)):
            u[o + ct] = ([(pad[:, ct, CTX + 3:CTX + 3 + SEQ], ID)], [(pad[:, ct, 1:1 + CTX], ID)])
    u[16] = ([(wd[:, CTX:ALL], ACT.Tanh)], [(wd[:, 0:CTX], ACT.Tanh)])
    u[17] = ([(ad[:, CTX:ALL], ID)], [(ad[:, 0:CTX], ID)])
    u[18] = ([(gd, ACT.Sigmoid)], None)
    zeros = [rp[:, :, 0:SEQ + 2:SEQ + 1]] + [p[:, :, a:b] for p in (kp, vp) for a, b in ((0, 1), (CTX + 1, CTX + 3), (771, 772))]
    in_proj_stage(k, g_in, h, u, zeros, None)
    A, R, K, B = four(0, ALL), four(6144, SEQ), four(10240, ALL), four(16384, ALL)
    v_tok = k.at(22528, 3072).rearrange("p (c n i) -> p c n i", c=4, n=N_CHUNK)
    bonus_v, Y, kk = three(25600, 4, SEQ), three(27648, 4, SEQ), three(25600, 4, ALL)
    vf, kf, r = three(32512, 4, ALL), three(35584, 4, ALL), three(38656, 4, SEQ)
    chunk_decay = k.mem[:, k.decay_at:k.decay_at + 96].rearrange("p (n q) -> p n q", q=8)
    uf_dram = nc.dram_tensor("fourier_in", [P, 4 * SEQ], F32, kind="Internal").ap()
    conv_stage(k, (rp, kp, vp), (r, kf, vf), kk, v_tok, (uf_dram, k.at(6144, 2048)))
    lora = k.at(10240, 1024)
    lora_landed = k.sem("lora_landed")
    with nc.Block("lora_load") as block:
        @block.sync
        def _(sp):
            sp.dma_start(lora, d["lora"]).then_inc(lora_landed, 16)
            sp.wait_ge(lora_landed, 16)
    lora_stage(k, wd, ad, lora, A, B)
    factor_stage(k, A, R, K, B, r, kf, kk, vf, bonus_v, chunk_decay, k.at(30208, 2304))
    scan_stage(k, A, R, K, B, v_tok, Y, chunk_decay, 30208)
    cat, g2, x = three(0, 8, SEQ), k.at(14592, CH), three(15104, KD, SEQ)
    landed = k.sem("mix_loads_landed")
    loads = [(g2, d["gate_g2"]), (k.at(4096, 2048), d["seq_dft"][0]), (k.at(6144, 2048), d["seq_dft"][1]),
             (k.at(8192, 256), d["chan_dft"]), (k.at(8448, 2048), uf_dram), (x, d["x0"][:, :, CTX:ALL])]
    rwkv_out_stage(k, Y, bonus_v, gd, g2, cat[:, 4:8], 19200, loads, landed)
    parts = k.at(10496, 4096).rearrange("p (t c m) -> p t c m", t=4, c=4)
    seq = k.at(4096, 4096).rearrange("p (x t n) -> p x t n", x=2, t=4)
    fourier_stage(k, three(8448, 4, SEQ), seq, k.at(8192, 256), cat[:, 0:4], parts)
    norm_stage(k, "fourier_norm", cat[:, 0:4], cat[:, 0:4], [(0, SEQ, 0)],
               gain=lambda i: [(k.v("fourier_g", 0, 4), None)], shift=None, work=19200, tiles=4)
    x1, h2 = three(30208, KD, SEQ), three(35840, KD, SEQ)

    def w256(g0):
        def pieces(m):
            w = k.slot(g0 + m // 2).rearrange("p (k m) -> p k m", k=KD)
            return [(g0 + m // 2, [(w[:, kt, P * (m % 2):P * (m % 2) + P], kt) for kt in range(KD)])]
        return pieces
    k.w256 = w256
    out_summed = k.frees_later(g_out, 4, "w_out_summed", 2)
    residual_stage(k, "w_out", g_out, 1, w256(g_out), KD, cat, lambda m: m1[:, 16 + m, 0:1], x, x1, g_out + 4 + RING)
    norm_stage(k, "norm2", x1, h2, [(0, SEQ, 0)], gain=lambda i: [(m1[:, 32:40, 0], k.v("norm2_g", 0, 8))],
               shift=lambda kt, i: m1[:, 24 + kt, 0:1], work=34304 - 34304)
    hidden = three(0, KF, SEQ)
    ffn_up_stage(k, g_up, h2, hidden, 11264)
    x2 = three(17408, KD, SEQ)
    k.frees_later(g_down, 16, "w_down_summed", 1)

    def down(m):
        out = []
        for half in range(2):
            g = g_down + 2 * m + half
            w = k.slot(g, 11 * P).rearrange("p (k m) -> p k m", k=11)
            out.append((g, [(w[:, i], 11 * half + i) for i in range(11)]))
        return out
    residual_stage(k, "w_down", g_down, 2, down, KF, hidden, lambda m: m1[:, 40 + m, 0:1], x1, x2, g_down + 16 + RING)
    x3 = three(0, KD, SEQ)
    norm_stage(k, "final1", x2, x3, [(0, SEQ, 0)], gain=lambda i: [(k.v("final_g", 0, 8), None)], shift=None, work=35840)
    return x3


def in_proj2_stage(k, g_q, g_v, g_g, h, q, kf, v_tok, upad, sig, gate_a, gate_b, conv):
    nc = k.nc
    s = {n: k.sem("proj2_" + n) for n in ("summed", "copied", "padded", "gated", "tap")}
    K2 = 31
    units, total = [], 0
    for g in range(4):
        units += [(g_q + g, "qk", 2 * g + j) for j in range(2)]
    for g in range(2):
        units += [(g_v + g, "v", t) for t in range(6)]
    for g in range(12):
        units += [(g_g + g, "glu" if g < 4 else "gate", 2 * g + j) for j in range(2)]
    for i, (g, _, _) in enumerate(units):
        k.freed[g] = (s["summed"], i + 1)
    glu_g = [i for i, u in enumerate(units) if u[1] == "glu" and u[2] >= 4]
    with nc.Block("in_proj2") as block:
        @block.sync
        def _(sp):
            k.send_weights(sp, g_g + 12 + RING)

        @block.gpsimd
        def _(pool):
            pool.memset(upad[:, :, 0:15], 0.0).then_inc(s["padded"], 1)
            pool.memset(upad[:, :, SEQ + 15:SEQ + 30], 0.0).then_inc(s["padded"], 1)

        @block.tensor
        def _(pe):
            for i, (g, kind, t) in enumerate(units):
                k.weights_ready(pe, g)
                w = k.slot(g).rearrange("p (k m) -> p k m", k=KD)
                if i >= 3:
                    pe.wait_ge(s["copied"], i - 2)
                b = k.bank[2 * (i % 3)]
                for kt in range(KD):
                    if kind == "v":
                        last = pe.matmul(b[:, 0:256], h[:, kt, P * t:P * t + P], w[:, kt], start=kt == 0, stop=kt == KD - 1)
                    else:
                        last = pe.matmul(b[:, :], w[:, kt, P * (t % 2):P * (t % 2) + P], h[:, kt, CTX:ALL],
                                         start=kt == 0, stop=kt == KD - 1)
                if kind == "qk" and t >= 4:
                    for kt in range(KD):
                        last = pe.matmul(k.bank[2 * (i % 3) + 1][:, 0:CTX], w[:, kt, P * (t % 2):P * (t % 2) + P],
                                         h[:, kt, 0:CTX], start=kt == 0, stop=kt == KD - 1)
                last.then_inc(s["summed"], 1)

        @block.scalar
        def _(act):
            for i, (g, kind, t) in enumerate(units):
                act.wait_ge(s["summed"], i + 1)
                b = k.bank[2 * (i % 3)]
                if kind == "qk" and t < 4:
                    ins = act.activation(q[:, t], b[:, :], ACT.Copy)
                elif kind == "qk":
                    act.activation(kf[:, t - 4, CTX:ALL], b[:, :], ACT.Copy)
                    ins = act.activation(kf[:, t - 4, 0:CTX], k.bank[2 * (i % 3) + 1][:, 0:CTX], ACT.Copy)
                elif kind == "v":
                    half = g - g_v
                    ins = act.activation(v_tok[:, t, 256 * half:256 * half + 256], b[:, 0:256], ACT.Copy)
                elif kind == "glu" and t < 4:
                    ins = act.activation(upad[:, t, 15:15 + SEQ], b[:, :], ACT.Copy)
                elif kind == "glu":
                    ins = act.activation(sig[:, t - 4], b[:, :], ACT.Sigmoid)
                else:
                    dst = gate_a[:, t - 8] if t < 16 else gate_b[:, t - 16]
                    ins = act.activation(dst, b[:, :], ACT.Sigmoid)
                ins.then_inc(s["copied"], 1)

        @block.vector
        def _(dve):
            for ct in range(KC):
                dve.wait_ge(s["copied"], glu_g[ct] + 1)
                u = upad[:, ct, 15:15 + SEQ]
                dve.tensor_tensor(u, u, sig[:, ct], MUL).then_inc(s["gated"], 1)
            dve.wait_ge(s["gated"], 4)
            dve.wait_ge(s["padded"], 2)
            for i in range(K2):
                for ct in range(KC):
                    src, w = upad[:, ct, i:i + SEQ], k.v("conv2_w", 4 * i + ct)
                    if i == 0:
                        ins = dve.tensor_scalar(conv[:, ct], src, w, k.v("conv2_b", ct), MUL, ADD)
                    else:
                        dve.wait_ge(s["tap"], 4 * (i - 1) + ct + 1)
                        ins = dve.scalar_tensor_tensor(out=conv[:, ct], in0=src, scalar=w, in1=conv[:, ct], op0=MUL, op1=ADD)
                    ins.then_inc(s["tap"], 1)


def layer_norm_stage(k, x, work):
    nc = k.nc
    squares = k.at(work, 4 * SEQ).rearrange("p (c t) -> p c t", c=4)
    rstd = k.at(work + 2048, SEQ)
    s = {n: k.sem("ln_" + n) for n in ("mean", "centred", "sq", "var", "root", "rstd", "scaled", "silu")}
    with nc.Block("layer_norm") as block:
        @block.tensor
        def _(pe):
            for ct in range(KC):
                last = pe.matmul(k.bank[0][:, :], k.c("ones"), x[:, ct], start=ct == 0, stop=ct == 3)
            last.then_inc(s["mean"], 1)
            for ct in range(KC):
                pe.wait_ge(s["sq"], ct + 1)
                last = pe.matmul(k.bank[1][:, :], k.c("ones"), squares[:, ct], start=ct == 0, stop=ct == 3)
            last.then_inc(s["var"], 1)

        @block.vector
        def _(dve):
            dve.wait_ge(s["mean"], 1)
            for ct in range(KC):
                dve.scalar_tensor_tensor(out=x[:, ct], in0=k.bank[0][:, :], scalar=-1.0 / CH, in1=x[:, ct],
                                         op0=MUL, op1=ADD).then_inc(s["centred"], 1)
            dve.wait_ge(s["root"], 1)
            dve.reciprocal(rstd, rstd).then_inc(s["rstd"], 1)
            dve.wait_ge(s["rstd"], 1)
            dve.wait_ge(s["sq"], 4)
            for ct in range(KC):
                dve.scalar_tensor_tensor(out=x[:, ct], in0=x[:, ct], scalar=k.v("ln_g", ct), in1=rstd,
                                         op0=MUL, op1=MUL).then_inc(s["scaled"], 1)

        @block.scalar
        def _(act):
            for ct in range(KC):
                act.wait_ge(s["centred"], ct + 1)
                act.activation(squares[:, ct], x[:, ct], ACT.Square).then_inc(s["sq"], 1)
            act.wait_ge(s["var"], 1)
            act.activation(rstd, k.bank[1][:, :], ACT.Sqrt, bias=k.v("eps_norm"), scale=1.0 / CH).then_inc(s["root"], 1)
            for ct in range(KC):
                act.wait_ge(s["scaled"], ct + 1)
                act.activation(x[:, ct], x[:, ct], ACT.Silu, bias=k.v("ln_b", ct)).then_inc(s["silu"], 1)


def attention_stage(k, q, kf, v_tok, att, work_bias, work_s, work_p):
    nc = k.nc
    NS = 14
    bias = k.at(work_bias, 2 * NS * 64).rearrange("p (n s c) -> p n s c", n=2, s=NS)
    sc = k.at(work_s, 2 * ALL).rearrange("p (n w) -> p n w", n=2)
    pt = k.at(work_p, 2 * 6 * SEQ).rearrange("p (n j w) -> p n j w", n=2, j=6)
    col = k.small.rearrange("p (n x) -> p n x", n=2)
    s = {n: k.sem("att_" + n) for n in ("bias_ready", "masked", "s_mm", "s_lat", "s_ctx", "max", "neg", "exp", "inv", "p",
                                       "turned", "pt", "av_mm", "av")}
    landed = [k.sem(f"att_bias_landed_{i}") for i in range(2)]
    rpb = k.d["rpb"]
    N = 32
    SCALE = HEAD ** -0.5
    with nc.Block("attention") as block:
        @block.sync
        def _(sp):
            for hd in range(8):
                if hd >= 2:
                    sp.wait_ge(s["s_lat"], 4 * (hd - 1))
                for par in range(2):
                    off = 64 + hd * 465 + (1 - par) * 31 - 48
                    src = bass.AP(rpb.tensor, off, [[1, 64], [31, NS], [1, 64]])
                    sp.dma_start(bias[64 * par:64 * par + 64, hd % 2], src).then_inc(landed[hd % 2], 16)
            k.send_weights(sp, len(k.stream))

        @block.gpsimd
        def _(pool):
            over = lambda name: k.c(name, 0, 64).rearrange("p (s c) -> p s c", s=1).broadcast_to([P, NS, 64])
            for hd in range(8):
                pool.wait_ge(landed[hd % 2], 32 * (hd // 2 + 1))
                pool.tensor_tensor(bias[:, hd % 2], bias[:, hd % 2], over("pair_mask"), MUL).then_inc(s["masked"], 1)
                pool.wait_ge(s["masked"], hd + 1)
                pool.tensor_tensor(bias[:, hd % 2], bias[:, hd % 2], over("pair_neg"), ADD).then_inc(s["bias_ready"], 1)

        @block.tensor
        def _(pe):
            def scores(u):
                hd, i = divmod(u, 4)
                r, ct = slice(64 * (hd % 2), 64 * (hd % 2) + 64), hd // 2
                if u >= 2:
                    pe.wait_ge(s["s_lat"], u - 1)
                    pe.wait_ge(s["s_ctx"], u - 1)
                b = 2 * (u % 2)
                pe.matmul(k.bank[b][:, :], q[r, ct, P * i:P * i + P], kf[r, ct, CTX:ALL], start=True, stop=True)
                pe.matmul(k.bank[b + 1][:, 0:CTX], q[r, ct, P * i:P * i + P], kf[r, ct, 0:CTX],
                          start=True, stop=True).then_inc(s["s_mm"], 1)

            scores(0)
            for u in range(N):
                hd, i = divmod(u, 4)
                if u + 1 < N:
                    scores(u + 1)
                pe.wait_ge(s["p"], u + 1)
                if u:
                    pe.wait_ge(s["pt"], u)
                for j in range(6):
                    last = pe.transpose(k.bank[4 + j // 4][:, P * (j % 4):P * (j % 4) + P], sc[:, u % 2, P * j:P * j + P],
                                        k.c("ident"))
                last.then_inc(s["turned"], 1)
                if i == 3:
                    pe.wait_ge(s["pt"], u + 1)
                    if hd >= 2:
                        pe.wait_ge(s["av"], hd - 1)
                    r = slice(64 * (hd % 2), 64 * (hd % 2) + 64)
                    for j in range(6):
                        last = pe.matmul(k.bank[6 + hd % 2][r, :], v_tok[:, j, 64 * hd:64 * hd + 64], pt[:, hd % 2, j],
                                         start=j == 0, stop=j == 5)
                    last.then_inc(s["av_mm"], 1)

        @block.scalar
        def _(act):
            def ctx_scores(u):
                act.wait_ge(s["s_mm"], u + 1)
                if u >= 2:
                    act.wait_ge(s["turned"], u - 1)
                act.activation(sc[:, u % 2, 0:CTX], k.bank[2 * (u % 2) + 1][:, 0:CTX], ACT.Copy, scale=SCALE).then_inc(s["s_ctx"], 1)

            ctx_scores(0)
            for u in range(N):
                hd, i = divmod(u, 4)
                act.wait_ge(s["neg"], u + 1)
                c = col[:, u % 2]
                act.activation(sc[:, u % 2], sc[:, u % 2], ACT.Exp, bias=c[:, 1:2], accum_out=c[:, 2:3]).then_inc(s["exp"], 1)
                if u + 1 < N:
                    ctx_scores(u + 1)
                act.wait_ge(s["turned"], u + 1)
                act.activation(pt[:, hd % 2, 0:4, P * i:P * i + P], k.bank[4][:, :].rearrange("p (j w) -> p j w", j=4), ACT.Copy)
                act.activation(pt[:, hd % 2, 4:6, P * i:P * i + P], k.bank[5][:, 0:256].rearrange("p (j w) -> p j w", j=2),
                               ACT.Copy).then_inc(s["pt"], 1)
                if i == 3:
                    act.wait_ge(s["av_mm"], hd + 1)
                    r = slice(64 * (hd % 2), 64 * (hd % 2) + 64)
                    act.activation(att[r, hd // 2], k.bank[6 + hd % 2][r, :], ACT.Copy).then_inc(s["av"], 1)

        @block.vector
        def _(dve):
            def lat_scores(u):
                hd, i = divmod(u, 4)
                dve.wait_ge(s["s_mm"], u + 1)
                if i == 0:
                    dve.wait_ge(s["bias_ready"], hd + 1)
                if u >= 2:
                    dve.wait_ge(s["turned"], u - 1)
                dve.scalar_tensor_tensor(out=sc[:, u % 2, CTX:ALL].rearrange("p (s c) -> p s c", s=ROWS),
                                         in0=k.bank[2 * (u % 2)][:, :].rearrange("p (s c) -> p s c", s=ROWS), scalar=SCALE,
                                         in1=bias[:, hd % 2, 6 - 2 * i:14 - 2 * i, ::-1], op0=MUL, op1=ADD).then_inc(s["s_lat"], 1)

            lat_scores(0)
            for u in range(N):
                c = col[:, u % 2]
                dve.wait_ge(s["s_lat"], u + 1)
                dve.wait_ge(s["s_ctx"], u + 1)
                dve.tensor_reduce(c[:, 0:1], sc[:, u % 2], AX, MAX).then_inc(s["max"], 1)
                dve.wait_ge(s["max"], u + 1)
                dve.tensor_scalar(c[:, 1:2], c[:, 0:1], -1.0, None, MUL).then_inc(s["neg"], 1)
                if u + 1 < N:
                    lat_scores(u + 1)
                dve.wait_ge(s["exp"], u + 1)
                dve.reciprocal(c[:, 3:4], c[:, 2:3]).then_inc(s["inv"], 1)
                dve.wait_ge(s["inv"], u + 1)
                dve.tensor_scalar(sc[:, u % 2], sc[:, u % 2], c[:, 3:4], None, MUL).then_inc(s["p"], 1)


def merge_stage(k, g0, att, conv, gate_a, gate_b, mix):
    nc = k.nc
    s = {n: k.sem("merge_" + n) for n in ("summed", "a", "b", "mix")}
    for g in range(4):
        k.freed[g0 + g] = (s["summed"], 4 * (g // 2 + 1))
    with nc.Block("merge") as block:
        @block.sync
        def _(sp):
            k.send_weights(sp, len(k.stream))

        @block.tensor
        def _(pe):
            for m in range(KD):
                ga = g0 + 2 * (m // 4)
                if m % 4 == 0:
                    k.weights_ready(pe, ga)
                    k.weights_ready(pe, ga + 1)
                if m >= 4:
                    pe.wait_ge(s["b"], m - 3)
                for n, rhs in enumerate((att, conv)):
                    w = k.slot(ga + n).rearrange("p (k m) -> p k m", k=4)
                    for kt in range(4):
                        last = pe.matmul(k.bank[2 * (m % 4) + n][:, :], w[:, kt, P * (m % 4):P * (m % 4) + P], rhs[:, kt],
                                         start=kt == 0, stop=kt == 3)
                last.then_inc(s["summed"], 1)

        @block.vector
        def _(dve):
            for m in range(KD):
                dve.wait_ge(s["summed"], m + 1)
                dve.tensor_tensor(gate_a[:, m], gate_a[:, m], k.bank[2 * (m % 4)][:, :], MUL).then_inc(s["a"], 1)
                dve.tensor_tensor(gate_b[:, m], gate_b[:, m], k.bank[2 * (m % 4) + 1][:, :], MUL).then_inc(s["b"], 1)
                dve.wait_ge(s["a"], m + 1)
                dve.wait_ge(s["b"], m + 1)
                dve.tensor_tensor(mix[:, m], gate_a[:, m], gate_b[:, m], ADD).then_inc(s["mix"], 1)


def route_stage(k, h, weights, table, h_dram, table_dram, w_router, ids, work):
    nc = k.nc
    off = [work]

    def buf(*dims):
        n = int(np.prod(dims))
        off[0] += n
        x = k.at(off[0] - n, n)
        if len(dims) == 2:
            return x.rearrange("p (a b) -> p a b", a=dims[0])
        if len(dims) == 3:
            return x.rearrange("p (a b c) -> p a b c", a=dims[0], b=dims[1])
        return x
    L, tie, one_g, ex, pg = buf(4, 36), buf(4, 8), buf(4, 4), buf(4, 4), buf(4, 1)
    top = [buf(4, 1), buf(4, 1)]
    gmax, least, total = buf(4, 1), buf(4, 1), buf(4, 1)
    picked, masked, part = buf(4, 8), buf(4, 8), buf(4, 4, 8)
    one_e = [buf(4, 8), buf(4, 8)]
    X = [buf(4, 32), buf(4, 32)]
    M, dest, tmp = buf(4, 32), buf(4, 32), buf(4, 32)
    j_tile, count, extra, upto = buf(4, 32), buf(32), buf(32), buf(32)
    slot_f = buf(4, 2)
    slot_i = buf(4, 2).bitcast(I32)
    tok_rows = k.at(work + 2048, 2 * D).rearrange("p (n w) -> p n w", n=2)
    s = {n: k.sem("route_" + n) for n in ("logits", "step", "exped", "rank_in", "rank", "slots", "blank", "scattered",
                                         "loaded", "turned", "rows")}
    rows_out = [k.sem(f"route_rows_out_{i}") for i in range(2)]
    iota = k.c("expert_id", 0, 32)
    n_step = [0]
    with nc.Block("route") as block:
        @block.sync
        def _(sp):
            sp.dma_start(table_dram.rearrange("(p b) t -> p (b t)", p=P), k.blank).then_inc(s["blank"], 16)
            for tt in range(4):
                sp.wait_ge(s["rows"], tt + 1)
                sp.dma_start(h_dram[P * tt:P * tt + P], tok_rows[:, tt % 2]).then_inc(rows_out[tt % 2], 16)
            sp.wait_ge(s["scattered"], 128)
            sp.dma_start(table, table_dram.rearrange("(p b) t -> p (b t)", p=P)).then_inc(s["loaded"], 16)
            sp.wait_ge(s["loaded"], 16)
            for out in rows_out:
                sp.wait_ge(out, 32)

        @block.tensor
        def _(pe):
            for tt in range(4):
                for kt in range(KD):
                    last = pe.matmul(k.bank[0][:, 36 * tt:36 * tt + 36], h[:, kt, P * tt:P * tt + P],
                                     w_router[:, kt], start=kt == 0, stop=kt == KD - 1)
            last.then_inc(s["logits"], 1)
            for tt in range(4):
                if tt:
                    pe.wait_ge(s["rows"], tt)
                for kt in range(KD):
                    last = pe.transpose(k.bank[2 + kt // 4][:, P * (kt % 4):P * (kt % 4) + P], h[:, kt, P * tt:P * tt + P],
                                        k.c("ident"))
                last.then_inc(s["turned"], 1)
            pe.wait_ge(s["rank_in"], 1)
            for tt in range(4):
                for t2 in range(tt + 1):
                    pe.matmul(k.bank[1][:, 32 * tt:32 * tt + 32], k.c("before") if t2 == tt else k.c("ones"), M[:, t2],
                              start=t2 == 0, stop=t2 == tt)
            for t2 in range(4):
                last = pe.matmul(k.bank[1][:, 128:160], k.c("ones"), M[:, t2], start=t2 == 0, stop=t2 == 3)
            last.then_inc(s["rank"], 1)

        @block.scalar
        def _(act):
            for tt in range(4):
                act.wait_ge(s["turned"], tt + 1)
                if tt >= 2:
                    act.wait_ge(rows_out[tt % 2], 16)
                act.activation(tok_rows[:, tt % 2, 0:512], k.bank[2][:, :], ACT.Copy)
                act.activation(tok_rows[:, tt % 2, 512:1024], k.bank[3][:, :], ACT.Copy).then_inc(s["rows"], 1)
            act.wait_ge(s["step"], route_steps["group_shifted"])
            act.activation(ex, ex, ACT.Exp).then_inc(s["exped"], 1)
            act.wait_ge(s["step"], route_steps["pair_shifted"])
            act.activation(top[1], top[1], ACT.Exp).then_inc(s["exped"], 1)

        @block.gpsimd
        def _(pool):
            pool.wait_ge(s["blank"], 16)
            pool.wait_ge(s["slots"], 1)
            for i in range(8):
                pool.indirect_dma_start(table_dram, bass.IndirectOffsetOnAxis(slot_i[:, i // 2, i % 2:i % 2 + 1].bitcast(U32), 0),
                                        ids[:, i], None).then_inc(s["scattered"], 16)

        @block.vector
        def _(dve):
            def step(ins):
                n_step[0] += 1
                ins.then_inc(s["step"], 1)
                dve.wait_ge(s["step"], n_step[0])

            def over(x, n):
                return x.broadcast_to([P, 4, n])

            def first_max(x, n, peak, one):
                step(dve.tensor_reduce(peak, x, AX, MAX))
                t = tie[:, :, 0:n]
                step(dve.tensor_tensor(t, x, over(peak, n), ALU.is_equal))
                ids_n = iota[:, 0:n].rearrange("p (a n) -> p a n", a=1).broadcast_to([P, 4, n])
                step(dve.scalar_tensor_tensor(out=t, in0=t, scalar=-100.0, in1=ids_n, op0=MUL, op1=ADD))
                step(dve.tensor_reduce(least, t, AX, ALU.min))
                step(dve.tensor_tensor(one, t, over(least, n), ALU.is_equal))

            dve.wait_ge(s["logits"], 1)
            b = k.v("router_b", 0, 36).rearrange("p (a n) -> p a n", a=1).broadcast_to([P, 4, 36])
            step(dve.tensor_tensor(L, k.bank[0][:, 0:144].rearrange("p (a n) -> p a n", a=4), b, ADD))
            first_max(L[:, :, 0:4], 4, gmax, one_g)
            step(dve.tensor_tensor(ex, L[:, :, 0:4], over(gmax, 4), SUB))
            assert route_steps["group_shifted"] == n_step[0], n_step[0]
            logits = L[:, :, 4:36].rearrange("p a (g e) -> p a g e", g=4)
            for tt in range(4):
                one = one_g[:, tt, :].rearrange("p (g e) -> p g e", e=1).broadcast_to([P, 4, 8])
                step(dve.tensor_tensor(part[:, tt], logits[:, tt], one, MUL))
            step(dve.tensor_tensor(picked, part[:, :, 0], part[:, :, 1], ADD))
            step(dve.tensor_tensor(masked, part[:, :, 2], part[:, :, 3], ADD))
            step(dve.tensor_tensor(picked, picked, masked, ADD))
            first_max(picked, 8, top[0], one_e[0])
            step(dve.scalar_tensor_tensor(out=masked, in0=one_e[0], scalar=NEG, in1=picked, op0=MUL, op1=ADD))
            first_max(masked, 8, top[1], one_e[1])
            step(dve.tensor_tensor(top[1], top[1], top[0], SUB))
            assert route_steps["pair_shifted"] == n_step[0], n_step[0]
            for i in range(2):
                for tt in range(4):
                    g = one_g[:, tt, :].rearrange("p (g e) -> p g e", e=1).broadcast_to([P, 4, 8])
                    e = one_e[i][:, tt, :].rearrange("p (g e) -> p g e", g=1).broadcast_to([P, 4, 8])
                    step(dve.tensor_tensor(X[i][:, tt].rearrange("p (g e) -> p g e", g=4), g, e, MUL))
            dve.tensor_tensor(M, X[0], X[1], ADD).then_inc(s["rank_in"], 1)
            dve.wait_ge(s["exped"], 2)
            step(dve.tensor_reduce(total, ex, AX, ADD))
            step(dve.reciprocal(pg, total))
            step(dve.tensor_scalar(total, top[1], 1.0, None, ADD))
            step(dve.reciprocal(total, total))
            step(dve.tensor_tensor(total, total, pg, MUL))
            step(dve.tensor_copy(weights[:, :, 0:1], total))
            step(dve.tensor_tensor(weights[:, :, 1:2], total, top[1], MUL))
            dve.wait_ge(s["rank"], 1)
            step(dve.tensor_copy(dest, k.bank[1][:, 0:128].rearrange("p (a n) -> p a n", a=4)))
            step(dve.tensor_copy(count, k.bank[1][:, 128:160]))
            step(dve.tensor_scalar(j_tile, dest, 128.0, None, ALU.is_ge))
            step(dve.tensor_scalar(extra, count, 128.0, None, ALU.is_gt))
            for t in (256.0, 384.0):
                step(dve.scalar_tensor_tensor(out=j_tile, in0=dest, scalar=t, in1=j_tile, op0=ALU.is_ge, op1=ADD))
                step(dve.scalar_tensor_tensor(out=extra, in0=count, scalar=t, in1=extra, op0=ALU.is_gt, op1=ADD))
            step(dve.tensor_tensor_scan(upto, k.c("ones", 0, 32), extra, 0.0, MUL, ADD))
            step(dve.scalar_tensor_tensor(out=dest, in0=j_tile, scalar=-128.0, in1=dest, op0=MUL, op1=ADD))
            step(dve.tensor_tensor(count, upto, extra, SUB))
            step(dve.scalar_tensor_tensor(out=count, in0=count, scalar=31.0, in1=iota, op0=ADD, op1=SUB))
            flat = count.rearrange("p (a n) -> p a n", a=1).broadcast_to([P, 4, 32])
            step(dve.tensor_tensor(tmp, j_tile, flat, ADD))
            step(dve.scalar_tensor_tensor(out=tmp, in0=j_tile, scalar=0.5, in1=tmp, op0=ALU.is_gt, op1=MUL))
            ids4 = iota.rearrange("p (a n) -> p a n", a=1).broadcast_to([P, 4, 32])
            step(dve.tensor_tensor(tmp, tmp, ids4, ADD))
            step(dve.scalar_tensor_tensor(out=dest, in0=dest, scalar=float(N_BLK), in1=tmp, op0=MUL, op1=ADD))
            for i in range(2):
                step(dve.tensor_tensor(tmp, X[i], dest, MUL))
                step(dve.tensor_reduce(slot_f[:, :, i:i + 1], tmp, AX, ADD))
            for i in range(OVER):
                step(dve.tensor_scalar(tmp[:, 0], upto, float(i), None, ALU.is_le))
                step(dve.tensor_reduce(k.over_f[:, i:i + 1], tmp[:, 0], AX, ADD))
            step(dve.tensor_copy(k.over_f[:, OVER:OVER + 1], upto[:, 31:32]))
            step(dve.tensor_copy(k.over_i, k.over_f))
            dve.tensor_copy(slot_i, slot_f).then_inc(s["slots"], 1)


route_steps = {"group_shifted": 7, "pair_shifted": 26}


def moe_stage(k, table, h_dram, y_dram, at):
    nc, d = k.nc, k.d

    def buf(n, *shape):
        at[0] += n
        return k.mem[:, at[0] - n:at[0]]
    gate_w = [buf(4096).rearrange("p (k n) -> p k n", k=KD) for _ in range(2)]
    up_w = [buf(4096).rearrange("p (k n) -> p k n", k=KD) for _ in range(2)]
    down_w = [buf(4096).rearrange("p (k n) -> p k n", k=4) for _ in range(2)]
    rows = [buf(D) for _ in range(2)]
    y = [buf(D) for _ in range(2)]
    x = buf(D).rearrange("p (k n) -> p k n", k=KD)
    act_g, hid, hid_t = buf(D_EXP), buf(D_EXP), buf(D_EXP).rearrange("p (k n) -> p k n", k=4)
    idx = [buf(2).bitcast(I32) for _ in range(2)]
    s = {n: k.sem("moe_" + n) for n in ("idx", "x_turned", "x", "gate_mm", "up_mm", "silu", "hid", "h_turned", "hid_t",
                                       "down_mm", "y")}
    gu_landed = [k.sem(f"moe_gate_up_landed_{i}") for i in range(2)]
    down_landed = [k.sem(f"moe_down_landed_{i}") for i in range(2)]
    gathered = [k.sem(f"moe_gathered_{i}") for i in range(2)]
    stored = [k.sem(f"moe_stored_{i}") for i in range(2)]
    n_ready = k.sem("moe_count_ready")
    turns = k.sem("moe_pool_turns")
    w_gate, w_up, w_down = d["w_gate"], d["w_upe"], d["w_downe"]
    one = lambda x, e: x[bass.ds(e, 1)].rearrange("a p n -> (a p) n")

    def send(sp, e, n, i, h, first):
        if not first:
            sp.wait_ge(s["up_mm"], n - 1)
        sp.dma_start(gate_w[h].rearrange("p k n -> p (k n)"), one(w_gate, e)).then_inc(gu_landed[h], 16)
        sp.dma_start(up_w[h].rearrange("p k n -> p (k n)"), one(w_up, e)).then_inc(gu_landed[h], 16)
        if not first:
            sp.wait_ge(s["down_mm"], n - 1)
        sp.dma_start(down_w[h].rearrange("p k n -> p (k n)"), one(w_down, e)).then_inc(down_landed[h], 16)

    def gather(pool, n, i, h, first):
        if not first:
            pool.wait_ge(stored[h], 16 * i)
            pool.wait_ge(s["x_turned"], n - 1)
        pool.sem_inc(turns, 1)
        pool.tensor_copy(idx[h].rearrange("p (a t) -> p a t", a=1), table[:, bass.ds(n, 1), :]).then_inc(s["idx"], 1)
        pool.wait_ge(s["idx"], n + 1)
        pool.sem_inc(turns, 1)
        pool.indirect_dma_start(rows[h], None, h_dram,
                                bass.IndirectOffsetOnAxis(idx[h][:, 1:2].bitcast(U32), 0)).then_inc(gathered[h], 16)

    def scatter(pool, n, i, h):
        pool.wait_ge(s["y"], n + 1)
        pool.sem_inc(turns, 1)
        pool.indirect_dma_start(y_dram, bass.IndirectOffsetOnAxis(idx[h][:, 0:1].bitcast(U32), 0), y[h], None,
                                bounds_check=N_PAIR - 1, oob_is_err=False).then_inc(stored[h], 16)

    def turn_x(pe, n, i, h, first):
        pe.wait_ge(gathered[h], 16 * (i + 1))
        if not first:
            pe.wait_ge(s["x"], n)
        for kt in range(KD):
            last = pe.transpose(k.bank[kt // 4][:, P * (kt % 4):P * (kt % 4) + P], rows[h][:, kt:D:KD], k.c("ident"))
        last.then_inc(s["x_turned"], 1)

    def gate_up(pe, n, i, h, first):
        pe.wait_ge(s["x"], n + 1)
        pe.wait_ge(gu_landed[h], 32 * (i + 1))
        if not first:
            pe.wait_ge(s["hid"], n)
        for kt in range(KD):
            last = pe.matmul(k.bank[2][:, :], x[:, kt], gate_w[h][:, kt], start=kt == 0, stop=kt == KD - 1)
        last.then_inc(s["gate_mm"], 1)
        for kt in range(KD):
            last = pe.matmul(k.bank[3][:, :], x[:, kt], up_w[h][:, kt], start=kt == 0, stop=kt == KD - 1)
        last.then_inc(s["up_mm"], 1)

    def turn_hidden(pe, n):
        pe.wait_ge(s["hid"], n + 1)
        for kt in range(4):
            last = pe.transpose(k.bank[4][:, P * kt:P * kt + P], hid[:, kt:D_EXP:4], k.c("ident"))
        last.then_inc(s["h_turned"], 1)

    def down(pe, n, i, h, first):
        pe.wait_ge(s["hid_t"], n + 1)
        pe.wait_ge(down_landed[h], 16 * (i + 1))
        if not first:
            pe.wait_ge(s["y"], n)
        for half in range(2):
            for kt in range(4):
                last = pe.matmul(k.bank[5 + half][:, :], hid_t[:, kt], down_w[h][:, kt, 512 * half:512 * half + 512],
                                 start=kt == 0, stop=kt == 3)
        last.then_inc(s["down_mm"], 1)

    def act_part(act, n, first):
        act.wait_ge(s["x_turned"], n + 1)
        if not first:
            act.wait_ge(s["up_mm"], n)
        act.activation(x[:, 0:4].rearrange("p k n -> p (k n)"), k.bank[0][:, :], ACT.Copy)
        act.activation(x[:, 4:8].rearrange("p k n -> p (k n)"), k.bank[1][:, :], ACT.Copy).then_inc(s["x"], 1)

    def act_silu(act, n, first):
        act.wait_ge(s["gate_mm"], n + 1)
        if not first:
            act.wait_ge(s["hid"], n)
        act.activation(act_g, k.bank[2][:, :], ACT.Silu).then_inc(s["silu"], 1)

    def dve_part(dve, n, i, h, first, first_half):
        dve.wait_ge(s["silu"], n + 1)
        dve.wait_ge(s["up_mm"], n + 1)
        if not first:
            dve.wait_ge(s["h_turned"], n)
        dve.tensor_tensor(hid, act_g, k.bank[3][:, :], MUL).then_inc(s["hid"], 1)
        dve.wait_ge(s["h_turned"], n + 1)
        if not first:
            dve.wait_ge(s["down_mm"], n)
        dve.tensor_copy(hid_t.rearrange("p k n -> p (k n)"), k.bank[4][:, :]).then_inc(s["hid_t"], 1)
        dve.wait_ge(s["down_mm"], n + 1)
        if not first_half:
            dve.wait_ge(stored[h], 16 * i)
        dve.tensor_copy(y[h][:, 0:512], k.bank[5][:, :])
        dve.tensor_copy(y[h][:, 512:1024], k.bank[6][:, :]).then_inc(s["y"], 1)

    def over_blocks(eng, run):
        eng.wait_ge(n_ready, 1)
        for o in range(OVER):
            count = eng.value_load(k.over_i[0:1, OVER:OVER + 1], min_val=0, max_val=OVER)
            with eng.If(count > o):
                run(o)

    LAST = N_EXP - 1
    with nc.Block("moe") as block:
        @block.sync
        def _(sp):
            send(sp, 0, 0, 0, 0, True)
            send(sp, 1, 1, 0, 1, True)
            with sp.Fori(1, N_EXP // 2) as i:
                for h in range(2):
                    send(sp, 2 * i + h, 2 * i + h, i, h, False)

            def over(o):
                n = N_EXP + o
                e = sp.value_load(k.over_i[0:1, o:o + 1], min_val=0, max_val=N_EXP - 1)
                send(sp, e, n, n // 2, n % 2, False)
            over_blocks(sp, over)

        @block.gpsimd
        def _(pool):
            pool.sem_inc(n_ready, 1)
            gather(pool, 0, 0, 0, True)
            gather(pool, 1, 0, 1, True)
            with pool.Fori(1, N_EXP // 2) as i:
                for h in range(2):
                    scatter(pool, 2 * i + h - 2, i - 1, h)
                    gather(pool, 2 * i + h, i, h, False)
            scatter(pool, LAST - 1, N_EXP // 2 - 1, 0)
            scatter(pool, LAST, N_EXP // 2 - 1, 1)

            def over(o):
                n = N_EXP + o
                gather(pool, n, n // 2, n % 2, False)
                scatter(pool, n, n // 2, n % 2)
            over_blocks(pool, over)
            pool.wait_ge(stored[0], 8 * N_EXP)
            pool.wait_ge(stored[1], 8 * N_EXP)
            for o in range(OVER):
                count = pool.value_load(k.over_i[0:1, OVER:OVER + 1], min_val=0, max_val=OVER)
                with pool.If(count > o):
                    pool.wait_ge(stored[o % 2], 8 * N_EXP + 16 * (o // 2 + 1))

        @block.tensor
        def _(pe):
            def block_of(n, i, h, first=False, more=True, i_next=None):
                gate_up(pe, n, i, h, first)
                if more:
                    turn_x(pe, n + 1, i_next, 1 - h, False)
                turn_hidden(pe, n)
                down(pe, n, i, h, first)
            turn_x(pe, 0, 0, 0, True)
            block_of(0, 0, 0, first=True, i_next=0)
            block_of(1, 0, 1, i_next=1)
            with pe.Fori(1, N_EXP // 2 - 1) as i:
                block_of(2 * i, i, 0, i_next=i)
                block_of(2 * i + 1, i, 1, i_next=i + 1)
            i = N_EXP // 2 - 1
            block_of(LAST - 1, i, 0, i_next=i)
            block_of(LAST, i, 1, more=False)

            def over(o):
                n = N_EXP + o
                turn_x(pe, n, n // 2, n % 2, False)
                block_of(n, n // 2, n % 2, more=False)
            over_blocks(pe, over)

        @block.scalar
        def _(act):
            act_part(act, 0, True)
            act_silu(act, 0, True)
            with act.Fori(1, N_EXP) as n:
                act_part(act, n, False)
                act_silu(act, n, False)

            def over(o):
                act_part(act, N_EXP + o, False)
                act_silu(act, N_EXP + o, False)
            over_blocks(act, over)

        @block.vector
        def _(dve):
            dve_part(dve, 0, 0, 0, True, True)
            dve_part(dve, 1, 0, 1, False, True)
            with dve.Fori(1, N_EXP // 2) as i:
                for h in range(2):
                    dve_part(dve, 2 * i + h, i, h, False, False)

            def over(o):
                n = N_EXP + o
                dve_part(dve, n, n // 2, n % 2, False, False)
            over_blocks(dve, over)


def combine_stage(k, y_dram, weights, x, gate, at):
    nc = k.nc
    yr = k.at(at, 8192).rearrange("p (t c w) -> p t c w", t=4, c=2)
    s = {n: k.sem("combine_" + n) for n in ("first", "both", "turned", "done")}
    landed = [k.sem(f"combine_landed_{tt}") for tt in range(4)]
    with nc.Block("combine") as block:
        @block.sync
        def _(sp):
            for tt in range(4):
                src = y_dram[2 * P * tt:2 * P * (tt + 1)].rearrange("(p c) w -> p (c w)", c=2)
                sp.dma_start(yr[:, tt].rearrange("p c w -> p (c w)"), src).then_inc(landed[tt], 16)

        @block.vector
        def _(dve):
            for tt in range(4):
                dve.wait_ge(landed[tt], 16)
                dve.tensor_scalar(yr[:, tt, 0], yr[:, tt, 0], weights[:, tt, 0:1], None, MUL).then_inc(s["first"], 1)
                dve.wait_ge(s["first"], tt + 1)
                dve.scalar_tensor_tensor(out=yr[:, tt, 0], in0=yr[:, tt, 1], scalar=weights[:, tt, 1:2], in1=yr[:, tt, 0],
                                         op0=MUL, op1=ADD).then_inc(s["both"], 1)
            for kt in range(KD):
                dve.wait_ge(s["turned"], kt + 1)
                dve.scalar_tensor_tensor(out=x[:, kt], in0=k.bank[kt % 4][:, :], scalar=gate(kt), in1=x[:, kt],
                                         op0=MUL, op1=ADD).then_inc(s["done"], 1)

        @block.tensor
        def _(pe):
            pe.wait_ge(s["both"], 4)
            for kt in range(KD):
                if kt >= 4:
                    pe.wait_ge(s["done"], kt - 3)
                for tt in range(4):
                    last = pe.transpose(k.bank[kt % 4][:, P * tt:P * tt + P], yr[:, tt, 0, P * kt:P * kt + P], k.c("ident"))
                last.then_inc(s["turned"], 1)


def block_two(k, x):
    nc, d = k.nc, k.d
    three = lambda at, n, w: k.at(at, n * w).rearrange("p (n w) -> p n w", n=n)
    g_ada, g_q, g_v, g_g, g_m, g_o = 85, 109, 113, 115, 127, 131
    k.retire()
    src = three(10240, KD, ALL)
    landed = k.sem("ctx2_landed")
    mod_stage(k, 1, g_ada)
    m2 = k.mod[1]
    with nc.Block("ctx2_load") as block:
        @block.sync
        def _(sp):
            sp.dma_start(src[:, :, 0:CTX], d["ctx2"]).then_inc(landed, 16)
            sp.wait_ge(landed, 16)

        @block.vector
        def _(dve):
            dve.tensor_copy(src[:, :, CTX:ALL], x).then_inc(k.sem("x_copied"), 1)
    hm = three(4096, KD, ALL)
    norm_stage(k, "norm_mix", src, hm, [(0, CTX, 0), (CTX, SEQ, 1)],
               gain=lambda i: [(m2[:, 8:16, 1 - i], k.v("norm_mix", 0, 8))],
               shift=lambda kt, i: m2[:, kt, 1 - i:2 - i], work=16384)
    q, kf, v_tok = three(10240, 4, SEQ), three(12288, 4, ALL), three(15360, 6, 512)
    upad, ga, gb = three(18432, 4, 542), three(20608, 8, SEQ), three(24704, 8, SEQ)
    conv, sig = three(28800, 4, SEQ), three(30848, 4, SEQ)
    in_proj2_stage(k, g_q, g_v, g_g, hm, q, kf, v_tok, upad, sig, ga, gb, conv)
    layer_norm_stage(k, conv, 32896)
    att = three(30848, 4, SEQ)
    attention_stage(k, q, kf, v_tok, att, 4096, 5888, 32896)
    mix = three(32896, 8, SEQ)
    merge_stage(k, g_m, att, conv, ga, gb, mix)
    k.frees_later(g_o, 4, "w_o_summed", 2)
    residual_stage(k, "w_o", g_o, 1, k.w256(g_o), KD, mix, lambda m: m2[:, 16 + m, 0:1], x, x, len(k.stream))
    k.retire()
    h = three(4096, KD, SEQ)
    norm_stage(k, "norm_ffn", x, h, [(0, SEQ, 0)], gain=lambda i: [(m2[:, 32:40, 0], k.v("norm_ffn", 0, 8))],
               shift=lambda kt, i: m2[:, 24 + kt, 0:1], work=8192)
    w_router = three(8192, KD, 36)
    table = k.at(8480, 2 * N_BLK).bitcast(I32).rearrange("p (b t) -> p b t", t=2)
    k.blank = k.at(8560, 2 * N_BLK).bitcast(I32)
    ids = k.at(8640, 16).bitcast(I32).rearrange("p (i t) -> p i t", t=2)
    weights = k.at(8656, 8).rearrange("p (t c) -> p t c", t=4)
    k.over_f, k.over_i = k.at(8664, 8), k.at(8672, 8).bitcast(I32)
    h_dram = nc.dram_tensor("h_rows", [SEQ, D], F32, kind="Internal").ap()
    y_dram = nc.dram_tensor("y_rows", [N_PAIR, D], F32, kind="Internal").ap()
    table_dram = nc.dram_tensor("slot_table", [P * N_BLK, 2], I32, kind="Internal").ap()
    r_landed = k.sem("router_landed")
    with nc.Block("route_load") as block:
        @block.sync
        def _(sp):
            sp.dma_start(k.at(8192, 288), d["w_router"]).then_inc(r_landed, 16)
            sp.dma_start(k.blank, d["blank"]).then_inc(r_landed, 16)
            sp.dma_start(k.at(8640, 16).bitcast(I32), d["ids"]).then_inc(r_landed, 16)
            sp.wait_ge(r_landed, 48)
    route_stage(k, h, weights, table, h_dram, table_dram, w_router, ids, 9000)
    moe_stage(k, table, h_dram, y_dram, [k.free_at + 9000])
    combine_stage(k, y_dram, weights, x, lambda m: m2[:, 40 + m, 0:1], 10240)
    out = three(4096, KD, SEQ)
    norm_stage(k, "final2", x, out, [(0, SEQ, 0)], gain=lambda i: [(k.v("final_norm", 0, 8), None)], shift=None, work=10240)
    return out


def build(nc, d, out, only_first=False):
    k = Core(nc, d, out)
    for name in ("ada1", "w_in", "w_out", "w_up", "w_down", "ada2", "w_in2_q", "w_in2_v", "w_in2_g"):
        k.stream += [d[name][g] for g in range(d[name].shape[0])]
    k.stream += [d[name][g] for g in range(2) for name in ("w_att", "w_conv")]
    k.stream += [d["w_o"][g] for g in range(4)]
    load_stage(k)
    x = block_one(k)
    if not only_first:
        x = block_two(k, x)
    stored = k.sem("result_stored")
    with nc.Block("store") as block:
        @block.sync
        def _(sp):
            sp.dma_start(out, x).then_inc(stored, 16)
            sp.wait_ge(stored, 16)


def kernel(**inputs):
    import concourse.bacc as bacc
    from concourse.bass_utils import run_bass_kernel_spmd

    nc = bacc.Bacc("TRN2", target_bir_lowering=False, num_devices=1)
    arrays = lay_out(inputs)
    d = {name: nc.dram_tensor(f"in_{name}", a.shape, mybir.dt.from_np(a.dtype), kind="ExternalInput").ap() for name, a in arrays.items()}
    out = nc.dram_tensor("out", [P, KD, SEQ], F32, kind="ExternalOutput").ap()
    build(nc, d, out)
    r = run_bass_kernel_spmd(nc, [{f"in_{name}": a for name, a in arrays.items()}], core_ids=[0])
    got = r.results[0]["out"]
    return np.ascontiguousarray(got.transpose(2, 1, 0)).reshape(1, SEQ, D)
```

```python
import numpy as np

import concourse.bass as bass
import concourse.mybir as mybir
from concourse.alu_op_type import AluOpType as ALU

ACT = mybir.ActivationFunctionType
F32 = mybir.dt.float32
I32 = mybir.dt.int32
U32 = mybir.dt.uint32
AX = mybir.AxisListType.X
ADD, SUB, MUL, MAX = ALU.add, ALU.subtract, ALU.mult, ALU.max

P = 128
D, KD = 1024, 8
SEQ, CTX = 512, 256
ALL = CTX + SEQ
GRID_W, ROWS = 64, SEQ // 64
CH, KC = 512, 4
HEAD = 64
CHUNK = 64
N_CTX, N_CHUNK = CTX // CHUNK, ALL // CHUNK
D_FF = 2816
KF = D_FF // P
N_EXP, N_GRP, PER_GRP, D_EXP = 32, 4, 8, 512
N_PAIR = SEQ * 2
OVER = 7
N_BLK = N_EXP + OVER
DECAY_SCALE = -float(np.exp(-0.5))
NEG = -1e30
RING, SLOT = 4, 2048


def columns(fields):
    at, out = 0, {}
    for name, n in fields:
        out[name] = at
        at += n
    return out, at


FIELDS = [
    ("norm1_g", 8), ("norm2_g", 8), ("final_g", 8), ("ada_b", 48), ("conv_w", 36), ("w0", 8), ("a0", 8),
    ("k_k", 4), ("k_a", 4), ("r_k", 4), ("gn_g", 4), ("gn_b", 4), ("fourier_g", 4),
    ("ffn_conv_w", 9 * 2 * KF), ("ffn_conv_b", 2 * KF),
    ("b_mod", 48), ("norm_mix", 8), ("norm_ffn", 8), ("final_norm", 8),
    ("conv2_w", 31 * 4), ("conv2_b", 4), ("ln_g", 4), ("ln_b", 4), ("router_b", 36),
    ("eps_norm", 1), ("eps_gn", 1), ("eps_kk", 1), ("zero", 1), ("cc1", 16), ("cc2", 16),
]
COL, N_COL = columns(FIELDS)
CONSTS = [("ident", 128), ("ones", 128), ("head_ones", 128), ("causal", 2 * 128), ("level", 6 * 64),
          ("chunk_start", ALL), ("before", 128), ("eye64", 64), ("pair_mask", 64), ("pair_neg", 64),
          ("expert_id", 32), ("pick", 31)]
CAT, N_CONST = columns(CONSTS)


def tiled(w, cols):
    k, m = w.shape
    return np.ascontiguousarray(w.reshape(k // P, P, m // cols, cols).transpose(2, 1, 0, 3)).reshape(m // cols, P, -1)


def feature_major(x):
    t, f = x.shape
    return np.ascontiguousarray(x.reshape(t, f // P, P).transpose(2, 1, 0))


def per_partition(v):
    v = np.asarray(v)
    return np.moveaxis(v.reshape(v.shape[:-1] + (v.shape[-1] // P, P)), -1, 0).reshape(P, -1)


def shape_constants():
    c = np.zeros((P, N_CONST), np.float32)
    p = np.arange(P)
    c[:, CAT["ident"]:][:, :128] = np.eye(P)
    c[:, CAT["ones"]:][:, :128] = 1
    c[:, CAT["head_ones"]:][:, :128] = p[:, None] // HEAD == p[None] // HEAD
    s, t = p[:, None] % CHUNK, np.arange(CHUNK)[None]
    causal = np.stack([s < t, s <= t, s > t, s >= t], 1).astype(np.float32)
    c[:, CAT["causal"]:][:, :256] = causal.reshape(P, 256)
    for lv in range(6):
        inner, outer = 1 << lv, 2 << lv
        c[:, CAT["level"] + 64 * lv:][:, :64] = (s // outer == t // outer) & (s // inner != t // inner)
    c[:, CAT["chunk_start"]:][:, :ALL] = (np.arange(ALL) % CHUNK != 0)[None]
    c[:, CAT["before"]:][:, :128] = p[:, None] < p[None]
    c[:, CAT["eye64"]:][:, :64] = s == t
    start = np.clip(t * 0 + p[:, None] % 64 - 8, 0, GRID_W - 16)
    inside = (t >= start) & (t < start + 16)
    c[:, CAT["pair_mask"]:][:, :64] = inside[:, ::-1]
    c[:, CAT["pair_neg"]:][:, :64] = np.where(inside, 0, NEG)[:, ::-1]
    c[:, CAT["expert_id"]:][:, :32] = np.arange(32)[None]
    c[:, CAT["pick"] + 15] = 1
    return c


def blank_table():
    t = np.zeros((P, N_BLK, 2), np.int32)
    t[:, :, 0] = N_PAIR + np.arange(P * N_BLK).reshape(P, N_BLK)
    return t.reshape(P, -1)


def row_ids():
    p, i = np.arange(P)[:, None], np.arange(8)[None]
    tok = p + P * (i // 2)
    return np.stack([2 * tok + i % 2, tok], 2).astype(np.int32).reshape(P, 16)


def fourier_constants():
    t = np.arange(SEQ)
    ang = 2 * np.pi * (np.outer(t, t) % SEQ) / SEQ
    seq = np.stack([np.cos(ang), -np.sin(ang)]) / np.sqrt(SEQ)
    j = np.arange(64)
    a64 = 2 * np.pi * (np.outer(j, j) % 64) / 64
    chan = np.zeros((P, 2, P))
    for g in range(2):
        chan[64 * g:64 * g + 64, 0, 64 * g:64 * g + 64] = np.cos(a64) / 8
        chan[64 * g:64 * g + 64, 1, 64 * g:64 * g + 64] = np.sin(a64) / 8
    seq = seq.reshape(2, 4, P, SEQ).transpose(0, 2, 1, 3)
    return np.ascontiguousarray(seq.reshape(2, P, 4 * SEQ), np.float32), np.ascontiguousarray(chan.reshape(P, 256), np.float32)


def lay_out(i):
    one = {k: np.asarray(v) for k, v in i.items()}
    vec = np.zeros((P, N_COL), np.float32)

    def put(name, a):
        vec[:a.shape[0], COL[name]:COL[name] + a.shape[1]] = a

    for name in ("norm1_g", "norm2_g", "ada_b", "k_k", "k_a", "gn_g", "gn_b", "fourier_g", "ffn_conv_b"):
        put(name, per_partition(one[name][0]))
    put("final_g", per_partition(one["final_g"]))
    put("conv_w", per_partition(one["rwkv_conv_w"][0]))
    put("w0", per_partition(one["decay_w0"][0]))
    put("a0", per_partition(one["iclr_a0"][0]))
    put("r_k", per_partition(one["r_k"][0].reshape(-1)))
    put("ffn_conv_w", per_partition(one["ffn_conv_w"][0].reshape(9, -1)))
    put("b_mod", per_partition(one["b_mod_2"][0]))
    put("norm_mix", per_partition(one["norm_mix_2"][0]))
    put("norm_ffn", per_partition(one["norm_ffn_2"][0]))
    put("final_norm", per_partition(one["final_norm_2"]))
    put("conv2_w", per_partition(one["conv_w_2"][0]))
    put("conv2_b", per_partition(one["conv_b_2"][0]))
    put("ln_g", per_partition(one["conv_ln_g_2"][0]))
    put("ln_b", per_partition(one["conv_ln_b_2"][0]))
    bias = np.concatenate([one["b_router_group_2"][0], one["b_router_expert_2"][0]])
    put("router_b", np.broadcast_to(bias[None], (P, 36)))
    for name, v in (("eps_norm", 1e-6), ("eps_gn", 64e-5), ("eps_kk", 1e-12)):
        vec[:, COL[name]] = v
    for name, a, b in (("cc1", "c", "c_ctx"), ("cc2", "c_2", "c_ctx_2")):
        both = np.stack([one[a][0], one[b]])
        put(name, both.reshape(2, KD, P).transpose(2, 1, 0).reshape(P, 16))

    w_in, w_in2 = one["w_in"][0], one["w_in_2"][0]
    seq_dft, chan_dft = fourier_constants()
    x0 = np.concatenate([one["ctx"][0], one["x"][0]])
    w_up = one["ffn_w_up"][0]
    up = np.stack([w_up[:, :D_FF].reshape(D, KF, P), w_up[:, D_FF:].reshape(D, KF, P)], 2)
    return {
        "vec": vec, "const": shape_constants(), "seq_dft": seq_dft, "chan_dft": chan_dft,
        "x0": feature_major(x0), "ctx2": feature_major(one["ctx_2"][0]),
        "ada1": tiled(one["ada_w"][0], 256), "ada2": tiled(one["w_mod_2"][0], 256),
        "w_in": tiled(w_in, 128), "w_out": tiled(one["w_out"][0], 256),
        "lora": np.concatenate([one["decay_w2"][0].reshape(P, CH), one["iclr_a2"][0].reshape(P, CH)], 1),
        "gate_g2": np.ascontiguousarray(one["gate_g2"][0]),
        "w_up": tiled(np.ascontiguousarray(up.reshape(D, 2 * D_FF)), 256),
        "w_down": np.ascontiguousarray(one["ffn_w_down"][0].reshape(2, 11, P, 8, P).transpose(3, 0, 2, 1, 4)).reshape(16, P, 11 * P),
        "w_in2_q": tiled(w_in2[:, :1024], 256),
        "w_in2_v": tiled(w_in2[:, 1024:1536], 256),
        "w_in2_g": tiled(w_in2[:, 1536:], 256),
        "rpb": np.pad(one["rpb_2"][0][:, :, ::-1].reshape(-1), 64),
        "w_att": tiled(one["w_att_out_2"][0], 512), "w_conv": tiled(one["w_conv_out_2"][0], 512),
        "w_o": tiled(one["w_o_2"][0], 256),
        "w_router": tiled(np.concatenate([one["w_router_group_2"][0], one["w_router_expert_2"][0]], 1), 36)[0],
        "blank": blank_table(), "ids": row_ids(),
        "w_gate": one["w_exp_gate_2"][0].reshape(N_EXP, P, KD * D_EXP),
        "w_upe": one["w_exp_up_2"][0].reshape(N_EXP, P, KD * D_EXP),
        "w_downe": one["w_exp_down_2"][0].reshape(N_EXP, P, 4 * D),
    }


class Core:

    def __init__(self, nc, d, out):
        self.nc, self.d, self.out = nc, d, out
        self.mem = nc.alloc_sbuf_tensor("mem", [P, 53100], F32)
        self.bank = [nc.alloc_psum_tensor(f"bank{i}", [P, 512], F32) for i in range(8)]
        self.vec = self.mem[:, 0:N_COL]
        self.const = self.mem[:, N_COL:N_COL + N_CONST]
        at = N_COL + N_CONST
        self.mod = [self.mem[:, at + 96 * b:at + 96 * b + 96].rearrange("p (m t) -> p m t", t=2) for b in range(2)]
        at += 192
        self.small = self.mem[:, at:at + 64]
        at += 64
        self.silu = [self.mem[:, at + 16 * b:at + 16 * b + 16] for b in range(2)]
        at += 32
        self.ring_at = at
        at += RING * SLOT
        self.decay_at = at
        at += 96
        self.free_at = at
        self.w_loaded = [nc.alloc_semaphore(f"weights_loaded_{i}") for i in range(RING)]
        self.freed = {}
        self.stream = []
        self.place = {}
        self.sent = 0
        self.named = {}
        self.live = []

    def sem(self, name):
        s = self.named.pop(name, None) or self.nc.alloc_semaphore(name)
        self.live.append(s)
        return s

    def retire(self):
        self.nc.clear_and_free_semaphores(self.live)
        self.nc.all_engine_barrier()
        self.live = []
        self.freed = {g: [] for g in self.freed}

    def v(self, name, i=0, n=1):
        return self.vec[:, COL[name] + i:COL[name] + i + n]

    def c(self, name, i=0, n=128):
        return self.const[:, CAT[name] + i:CAT[name] + i + n]

    def at(self, words, n):
        assert self.free_at + words + n <= 53100, (self.free_at + words + n)
        return self.mem[:, self.free_at + words:self.free_at + words + n]

    def slot(self, g, n=SLOT):
        a = self.ring_at + (g % RING) * SLOT
        return self.mem[:, a:a + n]

    def weights_ready(self, pe, g):
        pe.wait_ge(self.w_loaded[g % RING], 16 * (g // RING + 1))

    def put(self, name, tile):
        self.place[name, tile] = len(self.stream)
        self.stream.append(self.d[name][tile])

    def number(self, name, tile):
        return self.place[name, tile]

    def frees(self, numbers, sem, per=1):
        for i, g in enumerate(numbers):
            self.freed[g] = [(sem, per * (i + 1))]

    def frees_later(self, numbers, name, per):
        self.named[name] = self.nc.alloc_semaphore(name)
        self.frees(numbers, self.named[name], per)

    def send_weights(self, sp):
        while self.sent < len(self.stream):
            g = self.sent
            if g >= RING:
                if g - RING not in self.freed:
                    break
                for sem, value in self.freed[g - RING]:
                    sp.wait_ge(sem, value)
            src = self.stream[g]
            sp.dma_start(self.slot(g, src.shape[1]), src).then_inc(self.w_loaded[g % RING], 16)
            self.sent += 1


def load_stage(k):
    nc, landed = k.nc, k.sem("parameters_landed")
    with nc.Block("load") as block:
        @block.sync
        def _(sp):
            sp.dma_start(k.vec, k.d["vec"]).then_inc(landed, 16)
            sp.dma_start(k.const, k.d["const"]).then_inc(landed, 16)
            k.send_weights(sp)
            sp.wait_ge(landed, 32)


def mod_slot(k, dve, name, g, silu, acc, t, step, count):
    n = k.number(name, g)
    dve.wait_ge(k.w_loaded[n % RING], 16 * (n // RING + 1))
    w = k.slot(n).rearrange("p (k m) -> p k m", k=KD)
    for kt in range(KD):
        c = silu[:, 2 * kt + t:2 * kt + t + 1]
        if kt == 0:
            ins = dve.tensor_scalar(acc, w[:, kt], c, None, MUL)
        else:
            dve.wait_ge(step[0], step[1])
            ins = dve.scalar_tensor_tensor(out=acc, in0=w[:, kt], scalar=c, in1=acc, op0=MUL, op1=ADD)
        if kt < KD - 1:
            step[1] += 1
            ins.then_inc(step[0], 1)
        else:
            ins.then_inc(count, 1)


def mod_slot_by_product(k, pool, name, g, silu, acc, tmp, t, step, count):
    n = k.number(name, g)
    pool.wait_ge(k.w_loaded[n % RING], 16 * (n // RING + 1))
    if step[1]:
        pool.wait_ge(count, step[1] // 3)
    w = k.slot(n).rearrange("p (k m) -> p k m", k=KD)
    tmp = tmp.rearrange("p (k m) -> p k m", k=KD)
    c = silu[:, t:2 * KD:2].rearrange("p (k m) -> p k m", m=1).broadcast_to([P, KD, 256])
    pool.tensor_tensor(tmp, w, c, MUL).then_inc(step[0], 1)
    for half in (4, 2, 1):
        step[1] += 1
        pool.wait_ge(step[0], step[1])
        if half > 1:
            pool.tensor_tensor(tmp[:, 0:half], tmp[:, 0:half], tmp[:, half:2 * half], ADD).then_inc(step[0], 1)
        else:
            pool.tensor_tensor(acc, tmp[:, 0], tmp[:, 1], ADD).then_inc(count, 1)


def mod_contract(k, pe, bank, pieces):
    for j, x in enumerate(pieces):
        last = pe.matmul(bank[0:16, :], k.c("pick", 15 - j, 16), x, start=j == 0, stop=j == len(pieces) - 1)
    return last


def mod_turn(k, pe, bank, rows):
    for q in range(4):
        last = pe.matmul(bank[:, 16 * q:16 * q + 16], rows[0:16, P * q:P * q + P], k.c("ident", 0, 16)[0:16],
                         start=True, stop=True)
    return last


def mod_add_bias(k, dve, bank, b, m0, t, j0, n, added, value):
    four = lambda x: x.rearrange("p (j q) -> p j q", q=4)
    mod = k.mod[b][:, :, t]
    sums = bank[:, 0:64].rearrange("p (q j) -> p j q", q=4)[:, j0:j0 + n]
    bias = k.v(("ada_b", "b_mod")[b], m0, 4 * n)
    dve.tensor_tensor(four(mod[:, m0:m0 + 4 * n]), sums, four(bias), ADD).then_inc(added, 1)
    dve.wait_ge(added, value + 1)
    value += 1
    for a in (8, 32):
        if m0 <= a < m0 + 4 * n:
            dve.tensor_scalar(mod[:, a:a + 8], mod[:, a:a + 8], 1.0, None, ADD).then_inc(added, 1)
            value += 1
    return value


def cut(x, n=512):
    return [x[:, i:i + n] for i in range(0, x.shape[1], n)]


def mod_first_stage(k, x_load):
    nc = k.nc
    silu_done, summed, rows_ready, turned, added = (k.sem("mod_" + n) for n in ("silu", "summed", "rows", "turned", "added"))
    acc = [k.at(2048 * t, 2048) for t in range(2)]
    tmp, rows = k.at(12288, 2048), k.at(14336, 512)
    dve_acc, pool_acc = k.sem("mod_dve_acc"), k.sem("mod_pool_acc")
    dve_step, pool_step = [k.sem("mod_dve_step"), 0], [k.sem("mod_pool_step"), 0]
    dve_jobs = [(g, t) for g in range(8) for t in range(2) if t == 0 or g % 2]
    pool_jobs = [(g, 1) for g in range(0, 8, 2)]
    for g in range(8):
        k.freed[k.number("ada1", g)] = [(dve_acc, 1 + max(i for i, j in enumerate(dve_jobs) if j[0] == g))] + (
            [(pool_acc, pool_jobs.index((g, 1)) + 1)] if g % 2 == 0 else [])
    with nc.Block("mod_first") as block:
        @block.sync
        def _(sp):
            sp.dma_start(*x_load[:2]).then_inc(x_load[2], 16)
            k.send_weights(sp)

        @block.scalar
        def _(act):
            act.activation(k.silu[0], k.v("cc1", 0, 16), ACT.Silu).then_inc(silu_done, 1)
            act.activation(k.silu[1], k.v("cc2", 0, 16), ACT.Silu).then_inc(silu_done, 1)
            act.wait_ge(summed, 1)
            act.activation(rows[0:16], k.bank[0][0:16, :], ACT.Copy).then_inc(rows_ready, 1)

        @block.gpsimd
        def _(pool):
            pool.wait_ge(silu_done, 2)
            for g, t in pool_jobs:
                mod_slot_by_product(k, pool, "ada1", g, k.silu[0], acc[t][:, 256 * g:256 * g + 256], tmp, t, pool_step, pool_acc)

        @block.tensor
        def _(pe):
            pe.wait_ge(dve_acc, len(dve_jobs))
            pe.wait_ge(pool_acc, len(pool_jobs))
            mod_contract(k, pe, k.bank[0], cut(acc[0]) + cut(acc[1])).then_inc(summed, 1)
            pe.wait_ge(rows_ready, 1)
            mod_turn(k, pe, k.bank[1], rows).then_inc(turned, 1)

        @block.vector
        def _(dve):
            dve.wait_ge(silu_done, 2)
            for g, t in dve_jobs:
                mod_slot(k, dve, "ada1", g, k.silu[0], acc[t][:, 256 * g:256 * g + 256], t, dve_step, dve_acc)
            dve.wait_ge(turned, 1)
            value = mod_add_bias(k, dve, k.bank[1], 0, 0, 0, 0, 4, added, 0)
            mod_add_bias(k, dve, k.bank[1], 0, 0, 1, 4, 4, added, value)


def norm_stage(k, name, src, dst, parts, gain, shift, work, tiles=KD, first=None, loads=None, mod2=None):
    nc = k.nc
    landed = k.sem(name + "_landed") if loads else None
    if mod2:
        pieces, rows = mod2
        mod_summed, mod_rows, mod_turned, mod_added = (k.sem("mod2_" + n) for n in ("summed", "rows", "turned", "added"))
    width = parts[-1][0] + parts[-1][1]
    squares = k.at(work, 2 * width).rearrange("p (n w) -> p n w", n=2)
    rstd = k.at(work + 2 * width, width)
    gains = k.small[:, 0:2 * tiles].rearrange("p (k n) -> p k n", n=2)
    sq, used, rt, rs, scaled, gained, shifted = (k.sem(f"{name}_{s}") for s in (
        "square_ready", "square_used", "root_ready", "rstd_ready", "scaled", "gain_ready", "shifted"))
    with nc.Block(name) as block:
        @block.sync
        def _(sp):
            for to, src_dram in loads or ():
                sp.dma_start(to, src_dram).then_inc(landed, 16)
            k.send_weights(sp)
            if loads:
                sp.wait_ge(landed, 16 * len(loads))

        @block.scalar
        def _(act):
            if first is not None:
                act.wait_ge(*first)
            for kt in range(tiles):
                if kt >= 2:
                    act.wait_ge(used, kt - 1)
                act.activation(squares[:, kt % 2], src[:, kt], ACT.Square).then_inc(sq, 1)
            act.wait_ge(used, tiles)
            for a, n, b in parts:
                act.activation(rstd[:, a:a + n], k.bank[b][:, 0:n], ACT.Sqrt, bias=k.v("eps_norm"),
                               scale=1.0 / (tiles * P)).then_inc(rt, 1)
            if mod2:
                act.wait_ge(mod_summed, 1)
                act.activation(rows[0:16], k.bank[2][0:16, :], ACT.Copy).then_inc(mod_rows, 1)
            if shift:
                for kt in range(tiles):
                    for i, (a, n, b) in enumerate(parts):
                        act.wait_ge(scaled, kt * len(parts) + i + 1)
                        act.activation(dst[:, kt, a:a + n], dst[:, kt, a:a + n], ACT.Identity,
                                       bias=shift(kt, i)).then_inc(shifted, 1)

        @block.tensor
        def _(pe):
            for kt in range(tiles):
                pe.wait_ge(sq, kt + 1)
                for a, n, b in parts:
                    last = pe.matmul(k.bank[b][:, 0:n], k.c("ones"), squares[:, kt % 2, a:a + n],
                                     start=kt == 0, stop=kt == tiles - 1)
                last.then_inc(used, 1)
            if mod2:
                mod_contract(k, pe, k.bank[2], pieces).then_inc(mod_summed, 1)
                pe.wait_ge(mod_rows, 1)
                mod_turn(k, pe, k.bank[3], rows).then_inc(mod_turned, 1)

        @block.vector
        def _(dve):
            for i in range(len(parts)):
                for a, b in gain(i):
                    if b is None:
                        dve.tensor_copy(gains[:, :, i], a).then_inc(gained, 1)
                    else:
                        dve.tensor_tensor(gains[:, :, i], a, b, MUL).then_inc(gained, 1)
            if first is not None:
                dve.wait_ge(*first)
            dve.wait_ge(rt, len(parts))
            dve.reciprocal(rstd, rstd).then_inc(rs, 1)
            dve.wait_ge(rs, 1)
            dve.wait_ge(gained, len(parts))
            for kt in range(tiles):
                for i, (a, n, b) in enumerate(parts):
                    dve.scalar_tensor_tensor(out=dst[:, kt, a:a + n], in0=src[:, kt, a:a + n], scalar=gains[:, kt, i:i + 1],
                                             in1=rstd[:, a:a + n], op0=MUL, op1=MUL).then_inc(scaled, 1)
            if mod2:
                dve.wait_ge(mod_turned, 1)
                value = mod_add_bias(k, dve, k.bank[3], 1, 0, 0, 0, 12, mod_added, 0)
                mod_add_bias(k, dve, k.bank[3], 1, 0, 1, 12, 4, mod_added, value)


def in_proj_stage(k, h, u, pad_rkv, convs, acc):
    nc = k.nc
    order = [*range(8, 16), *range(4, 8), 16, 17, 18, *range(4)]
    summed, copied, padded = k.sem("in_proj_summed"), k.sem("in_proj_copied"), k.sem("in_proj_padded")
    tap0, tap1, conv = k.sem("conv_tap0"), k.sem("conv_tap1"), k.sem("conv_tap2")
    mod_acc, mod_step = k.sem("mod_acc"), [k.sem("mod_step"), 0]
    mod_summed, mod_rows, mod_turned, mod_added = (k.sem("mod1_" + n) for n in ("summed", "rows", "turned", "added"))
    rows = acc[:, 4096:4608]
    k.frees([k.number("w_in", m) for m in order], summed)
    k.frees([k.number("ada1", g) for g in range(8, 24)], mod_acc)
    with nc.Block("in_proj") as block:
        @block.sync
        def _(sp):
            k.send_weights(sp)

        @block.gpsimd
        def _(pool):
            for view in pad_rkv:
                pool.memset(view, 0.0).then_inc(padded, 1)

        @block.tensor
        def _(pe):
            for i, m in enumerate(order):
                g = k.number("w_in", m)
                k.weights_ready(pe, g)
                w = k.slot(g, 1024).rearrange("p (k m) -> p k m", k=KD)
                if i >= 3:
                    pe.wait_ge(copied, i - 2)
                for n0, n1, b in ((CTX, ALL, 2 * (i % 3)), (0, CTX, 2 * (i % 3) + 1)):
                    if n0 == 0 and not u[m][1]:
                        continue
                    for kt in range(KD):
                        last = pe.matmul(k.bank[b][:, 0:n1 - n0], w[:, kt], h[:, kt, n0:n1],
                                         start=kt == 0, stop=kt == KD - 1)
                last.then_inc(summed, 1)
            pe.wait_ge(mod_acc, 16)
            pe.wait_ge(copied, 19)
            mod_contract(k, pe, k.bank[0], cut(acc[:, 0:4096])).then_inc(mod_summed, 1)
            pe.wait_ge(mod_rows, 1)
            mod_turn(k, pe, k.bank[6], rows).then_inc(mod_turned, 1)

        @block.scalar
        def _(act):
            n = 0
            for i, m in enumerate(order):
                act.wait_ge(summed, i + 1)
                lat, ctx = u[m]
                for dst, f in lat:
                    ins = act.activation(dst, k.bank[2 * (i % 3)][:, 0:SEQ], f)
                if ctx:
                    for dst, f in ctx:
                        ins = act.activation(dst, k.bank[2 * (i % 3) + 1][:, 0:CTX], f)
                ins.then_inc(copied, 1)
                if m in convs:
                    act.wait_ge(copied, i + 1)
                    act.wait_ge(padded, len(pad_rkv))
                    for src, dst, w in convs[m]:
                        act.activation(dst, src[:, 0:dst.shape[1]], ACT.Identity, scale=k.v("conv_w", w)).then_inc(tap0, 1)
            act.wait_ge(mod_summed, 1)
            act.activation(rows[0:16], k.bank[0][0:16, :], ACT.Copy).then_inc(mod_rows, 1)

        @block.vector
        def _(dve):
            n = 0
            for i, m in enumerate(order):
                if i < 16:
                    mod_slot(k, dve, "ada1", 8 + i, k.silu[0], acc[:, 256 * i:256 * i + 256], 0, mod_step, mod_acc)
                for src, dst, w in convs.get(m, ()):
                    n += 1
                    size = dst.shape[1]
                    dve.wait_ge(tap0, n)
                    dve.scalar_tensor_tensor(out=dst, in0=src[:, 1:size + 1], scalar=k.v("conv_w", 12 + w), in1=dst,
                                             op0=MUL, op1=ADD).then_inc(tap1, 1)
                    dve.wait_ge(tap1, n)
                    dve.scalar_tensor_tensor(out=dst, in0=src[:, 2:size + 2], scalar=k.v("conv_w", 24 + w), in1=dst,
                                             op0=MUL, op1=ADD).then_inc(conv, 1)
            dve.wait_ge(mod_turned, 1)
            mod_add_bias(k, dve, k.bank[6], 0, 16, 0, 0, 8, mod_added, 0)


def key_stage(k, kf, vf, kk_out, v_tok, store, lora_load):
    nc = k.nc
    sq, summed, rt, rs, kraw, kk, turned, out, stored, landed = (k.sem("key_" + s) for s in (
        "square", "summed", "root", "rstd", "kraw", "kk_ready", "v_turned", "v_copied", "fourier_stored", "lora_landed"))
    squares = k.at(0, 2 * ALL).rearrange("p (n w) -> p n w", n=2)
    rstd = k.at(2 * ALL, 4 * ALL).rearrange("p (n w) -> p n w", n=4)
    with nc.Block("keys") as block:
        @block.sync
        def _(sp):
            sp.dma_start(*store).then_inc(stored, 16)
            sp.dma_start(*lora_load).then_inc(landed, 16)
            sp.wait_ge(stored, 16)
            sp.wait_ge(landed, 16)

        @block.scalar
        def _(act):
            for ct in range(KC):
                act.wait_ge(kraw, ct + 1)
                if ct >= 2:
                    act.wait_ge(summed, ct - 1)
                act.activation(squares[:, ct % 2], kk_out[:, ct], ACT.Square).then_inc(sq, 1)
            for ct in range(KC):
                act.wait_ge(summed, ct + 1)
                for a, n, b in ((0, CTX, 0), (CTX, SEQ, 1)):
                    ins = act.activation(rstd[:, ct, a:a + n], k.bank[2 * (ct % 3) + b][:, 0:n], ACT.Sqrt,
                                         bias=k.v("eps_kk"))
                ins.then_inc(rt, 1)
            for c in range(N_CHUNK):
                act.wait_ge(turned, c + 1)
                act.activation(v_tok[:, :, c], k.bank[6 + c % 2][:, 0:256].rearrange("p (t i) -> p t i", t=KC),
                               ACT.Copy).then_inc(out, 1)

        @block.vector
        def _(dve):
            for ct in range(KC):
                dve.tensor_scalar(kk_out[:, ct], kf[:, ct], k.v("k_k", ct), None, MUL).then_inc(kraw, 1)
            for ct in range(KC):
                dve.wait_ge(rt, ct + 1)
                dve.reciprocal(rstd[:, ct], rstd[:, ct]).then_inc(rs, 1)
                dve.wait_ge(rs, ct + 1)
                dve.tensor_tensor(kk_out[:, ct], kk_out[:, ct], rstd[:, ct], MUL).then_inc(kk, 1)

        @block.tensor
        def _(pe):
            for ct in range(KC):
                pe.wait_ge(sq, ct + 1)
                if ct == 3:
                    pe.wait_ge(rt, 1)
                for a, n, b in ((0, CTX, 0), (CTX, SEQ, 1)):
                    last = pe.matmul(k.bank[2 * (ct % 3) + b][:, 0:n], k.c("head_ones"), squares[:, ct % 2, a:a + n],
                                     start=True, stop=True)
                last.then_inc(summed, 1)
            for c in range(N_CHUNK):
                if c >= 2:
                    pe.wait_ge(out, c - 1)
                for ct in range(KC):
                    for r in (slice(0, 64), slice(64, 128)):
                        last = pe.matmul(k.bank[6 + c % 2][r, 64 * ct:64 * ct + 64], vf[r, ct, 64 * c:64 * c + 64],
                                         k.c("eye64", 0, 64)[r], start=True, stop=True)
                last.then_inc(turned, 1)


def lora_stage(k, wd, ad, lora, sig, a):
    nc = k.nc
    summed, done = k.sem("lora_summed"), k.sem("lora_done")
    with nc.Block("lora") as block:
        @block.tensor
        def _(pe):
            u = 0
            for src, w0, dst in ((wd, 0, sig), (ad, CH, a)):
                for d in range(2):
                    r = slice(64 * d, 64 * d + 64)
                    for ct in range(KC):
                        if u >= 4:
                            pe.wait_ge(done, u - 3)
                        for x, n, b in ((0, CTX, 0), (CTX, SEQ, 1)):
                            last = pe.matmul(k.bank[2 * (u % 4) + b][:, 0:n], lora[r, w0 + P * ct:w0 + P * ct + P],
                                             src[r, x:x + n], start=True, stop=True)
                        last.then_inc(summed, 1)
                        u += 1

        @block.scalar
        def _(act):
            u = 0
            for name, dst in (("w0", sig), ("a0", a)):
                for d in range(2):
                    for ct in range(KC):
                        act.wait_ge(summed, u + 1)
                        for x, n, b in ((0, CTX, 0), (CTX, SEQ, 1)):
                            ins = act.activation(dst[:, d, ct, x:x + n], k.bank[2 * (u % 4) + b][:, 0:n], ACT.Sigmoid,
                                                 bias=k.v(name, 4 * d + ct))
                        ins.then_inc(done, 1)
                        u += 1


def step_of(d, c):
    return c if d == 0 else (N_CTX - 1 - c if c < N_CTX else N_CTX + N_CHUNK - 1 - c)


chunk_at = step_of


def factor_stage(k, A, R, K, B, r, kf, kk, vf, bonus_v, chunk_decay, tmp):
    nc = k.nc
    T1, T2, T3 = tmp[:, 0:ALL], tmp[:, ALL:2 * ALL], tmp[:, 2 * ALL:3 * ALL]
    one_minus, prefix, before, upto, e_before, e_upto, e_inv, a_done, r_done, pc_done, kf1, kd, k_done, prod, ba, \
        b_done, bonus_summed, bonus_done = (k.sem("factor_" + n) for n in (
            "one_minus_k_a", "prefix", "sum_before", "sum_upto", "exp_before", "exp_upto", "exp_inverse", "a", "r",
            "chunk_decay", "k_scale", "k_dir", "k", "bonus_product", "kk_a", "b", "bonus_summed", "bonus"))
    omka = k.small[:, 0:4]
    split = lambda x: x.rearrange("p (c t) -> p c t", t=CHUNK)
    with nc.Block("factors") as block:
        @block.vector
        def _(dve):
            dve.tensor_scalar(omka, k.v("k_a", 0, 4), -1.0, 1.0, MUL, ADD).then_inc(one_minus, 1)
            dve.wait_ge(one_minus, 1)
            for u in range(8):
                d, ct = divmod(u, 4)
                sig, a = A[:, d, ct], B[:, d, ct]
                if u:
                    dve.wait_ge(b_done, u)
                if d == 0:
                    dve.tensor_tensor_scan(T1, k.c("chunk_start", 0, ALL), sig, 0.0, MUL, ADD).then_inc(upto, 1)
                    dve.wait_ge(upto, u + 1)
                    dve.tensor_tensor(T2, T1, sig, SUB).then_inc(before, 1)
                else:
                    dve.tensor_tensor_scan(T1, k.c("chunk_start", 0, ALL), sig, 0.0, MUL, ADD).then_inc(prefix, 1)
                    dve.wait_ge(prefix, u - 3)
                    total = split(T1)[:, :, CHUNK - 1:CHUNK].broadcast_to([P, N_CHUNK, CHUNK])
                    dve.tensor_tensor(split(T2), total, split(T1), SUB).then_inc(before, 1)
                    dve.wait_ge(before, u + 1)
                    dve.tensor_tensor(T1, T2, sig, ADD).then_inc(upto, 1)
                dve.wait_ge(e_before, u + 1)
                dve.tensor_tensor(A[:, d, ct], kk[:, ct], T2, MUL).then_inc(a_done, 1)
                dve.wait_ge(e_upto, u + 1)
                last = split(T3)[:, :, CHUNK - 1] if d == 0 else split(T3)[:, :, 0]
                if d == 0:
                    dve.tensor_copy(chunk_decay[:, :, u], last).then_inc(pc_done, 1)
                else:
                    dve.tensor_copy(chunk_decay[:, 0:N_CTX, u], last[:, N_CTX - 1::-1])
                    dve.tensor_copy(chunk_decay[:, N_CTX:N_CHUNK, u], last[:, N_CHUNK - 1:N_CTX - 1:-1]).then_inc(pc_done, 1)
                dve.wait_ge(a_done, u + 1)
                dve.tensor_scalar(T2, a, k.v("k_a", ct), omka[:, ct:ct + 1], MUL, ADD).then_inc(kf1, 1)
                dve.wait_ge(kf1, u + 1)
                dve.tensor_tensor(T2, T2, kf[:, ct], MUL).then_inc(kd, 1)
                dve.wait_ge(kd, u + 1)
                dve.wait_ge(e_inv, u + 1)
                dve.tensor_tensor(K[:, d, ct], T2, T1, MUL).then_inc(k_done, 1)
                dve.wait_ge(pc_done, u + 1)
                dve.wait_ge(r_done, u + 1)
                dve.scalar_tensor_tensor(out=T3[:, CTX:ALL], in0=T2[:, CTX:ALL], scalar=k.v("r_k", ct), in1=r[:, ct],
                                         op0=MUL, op1=MUL).then_inc(prod, 1)
                dve.wait_ge(k_done, u + 1)
                dve.tensor_tensor(T1, T1, a, MUL).then_inc(ba, 1)
                dve.wait_ge(ba, u + 1)
                dve.tensor_tensor(B[:, d, ct], T1, kk[:, ct], MUL).then_inc(b_done, 1)
            dve.wait_ge(b_done, 8)
            dve.wait_ge(bonus_summed, 8)
            for ct in range(KC):
                dve.tensor_tensor(bonus_v[:, ct], k.bank[ct][:, 0:SEQ], vf[:, ct, CTX:ALL], MUL).then_inc(bonus_done, 1)

        @block.gpsimd
        def _(pool):
            for u in range(8):
                d, ct = divmod(u, 4)
                pool.wait_ge(e_upto, u + 1)
                pool.tensor_tensor(R[:, d, ct], r[:, ct], T3[:, CTX:ALL], MUL).then_inc(r_done, 1)

        @block.scalar
        def _(act):
            for u in range(8):
                act.wait_ge(before, u + 1)
                act.wait_ge(upto, u + 1)
                act.activation(T2, T2, ACT.Exp, scale=DECAY_SCALE).then_inc(e_before, 1)
                if u:
                    act.wait_ge(bonus_summed, u)
                act.activation(T3, T1, ACT.Exp, scale=DECAY_SCALE).then_inc(e_upto, 1)
                act.wait_ge(e_upto, u + 1)
                act.activation(T1, T1, ACT.Exp, scale=-DECAY_SCALE).then_inc(e_inv, 1)

        @block.tensor
        def _(pe):
            for u in range(8):
                d, ct = divmod(u, 4)
                pe.wait_ge(prod, u + 1)
                pe.matmul(k.bank[ct][:, 0:SEQ], k.c("head_ones"), T3[:, CTX:ALL], start=d == 0, stop=d == 1,
                          skip_group_check=True).then_inc(bonus_summed, 1)


def chunk_at(d, n):
    return n if d == 0 else (N_CTX - 1 - n if n < N_CTX else N_CTX + N_CHUNK - 1 - n)


def scan_stage(k, A, R, K, B, v_tok, Y, chunk_decay, work):
    nc = k.nc
    off = [work]

    def buf(n=1):
        off[0] += 512 * n
        x = k.at(off[0] - 512 * n, 512 * n)
        return x.rearrange("p (n c) -> p n c", n=n)

    Mba, Mka, Mbr, Mkr, Tt, KT, BT = buf(), buf(2), buf(2), buf(2), buf(2), buf(2), buf(2)
    T, W, Z, Un, S, St, E = buf(), buf(), buf(), buf(), buf(), buf(), buf(2)
    GA, GB, BW, BT_, BTT, BX, BZ, BU = k.bank
    s = {n: k.sem("scan_" + n) for n in (
        "g_ba", "g_ka", "g_br", "g_kr", "mba", "mka", "mbr", "mkr", "e", "e1", "t", "tt", "w_mm", "w", "t_mm", "tt_mm",
        "k_turned", "kt", "b_turned", "bt", "z_mm", "z", "u_mm", "un", "y_mm", "y", "s_mm", "st", "s")}
    LV = 5
    heads = (slice(0, 64), slice(64, 128))
    pairs = [(q, q // 4, q % 4) for q in range(8)]
    col = lambda q: slice(64 * q, 64 * q + 64)
    tok = lambda x, c, base=0: x[:, :, 64 * (c - base):64 * (c - base) + 64]
    with_r = lambda n: max(0, n - N_CTX)
    causal = k.c("causal", 0, 256).rearrange("p (d x t) -> p d x t", d=2, x=2)
    eye = k.c("eye64", 0, 64).rearrange("p (q t) -> p q t", q=1).broadcast_to([P, 8, 64])
    eight = lambda x: x.rearrange("p (q t) -> p q t", q=8)
    level = lambda l: k.c("level", 64 * (l - 1), 64).rearrange("p (q t) -> p q t", q=1).broadcast_to([P, 8, 64])

    with nc.Block("scan") as block:
        @block.tensor
        def _(pe):
            def products(bank, *terms):
                for q, d, ct in pairs:
                    for r in heads:
                        for i, term in enumerate(terms):
                            a, b = term(q, d, ct, r)
                            last = pe.matmul(bank[r, col(q)], a, b, start=i == 0, stop=i == len(terms) - 1,
                                             skip_group_check=True)
                return last

            def gram(bank, X, Yv, base, p):
                return products(bank, lambda q, d, ct, r: (
                    X[r, d, ct, 64 * chunk_at(d, p):64 * chunk_at(d, p) + 64],
                    Yv[r, d, ct, 64 * (chunk_at(d, p) - base):64 * (chunk_at(d, p) - base) + 64]))

            def level_w(p, l):
                pe.wait_ge(s["e"], 6 * p + l)
                pe.wait_ge(s["t"], LV * p + l - 1)
                if LV * p + l - 2 > 0:
                    pe.wait_ge(s["w"], LV * p + l - 2)
                products(BW, lambda q, d, ct, r: (E[r, l % 2, col(q)], T[r, 0, col(q)])).then_inc(s["w_mm"], 1)

            def level_t(p, l):
                pe.wait_ge(s["w"], LV * p + l - 1)
                pe.wait_ge(s["tt"], 6 * p + l - 1)
                if l < 6:
                    products(BT_, lambda q, d, ct, r: (Tt[r, p % 2, col(q)], W[r, 0, col(q)])).then_inc(s["t_mm"], 1)
                products(BTT, lambda q, d, ct, r: (W[r, 0, col(q)], Tt[r, p % 2, col(q)])).then_inc(s["tt_mm"], 1)

            for it in range(N_CHUNK + 1):
                p, j = it, it - 1
                prep, solve = p < N_CHUNK, j >= 0
                if prep:
                    if p:
                        if with_r(p) > with_r(p - 1):
                            pe.wait_ge(s["mbr"], with_r(p))
                            pe.wait_ge(s["mkr"], with_r(p))
                        else:
                            pe.wait_ge(s["mba"], p)
                            pe.wait_ge(s["mka"], p)
                    gram(GA, B, A, 0, p).then_inc(s["g_ba"], 1)
                    gram(GB, K, A, 0, p).then_inc(s["g_ka"], 1)
                if solve:
                    pe.wait_ge(s["s"], j + 1)
                    pe.wait_ge(s["mka"], j + 1)
                    products(BZ, lambda q, d, ct, r: (A[r, d, ct, 64 * chunk_at(d, j):64 * chunk_at(d, j) + 64], S[r, 0, col(q)]),
                             lambda q, d, ct, r: (Mka[r, j % 2, col(q)], v_tok[r, ct, chunk_at(d, j)])).then_inc(s["z_mm"], 1)
                if prep:
                    pe.wait_ge(s["e"], 6 * p + 1)
                    if p:
                        pe.wait_ge(s["t"], LV * p)
                    products(BT_, lambda q, d, ct, r: (E[r, 1, col(q)], k.c("eye64", 0, 64)[r])).then_inc(s["e1"], 1)
                    if p >= N_CTX:
                        pe.wait_ge(s["mba"], p + 1)
                        gram(GA, B, R, N_CTX, p).then_inc(s["g_br"], 1)
                        pe.wait_ge(s["mka"], p + 1)
                        gram(GB, K, R, N_CTX, p).then_inc(s["g_kr"], 1)
                if solve:
                    pe.wait_ge(s["z"], j + 1)
                    pe.wait_ge(s["tt"], 6 * (j + 1))
                    products(BU, lambda q, d, ct, r: (Tt[r, j % 2, col(q)], Z[r, 0, col(q)])).then_inc(s["u_mm"], 1)
                if prep:
                    level_w(p, 2)
                    if p:
                        pe.wait_ge(s["bt"], p)
                    products(BX, lambda q, d, ct, r: (K[r, d, ct, 64 * chunk_at(d, p):64 * chunk_at(d, p) + 64],
                                                      k.c("eye64", 0, 64)[r])).then_inc(s["k_turned"], 1)
                    level_t(p, 2)
                    level_w(p, 3)
                if solve and j >= N_CTX:
                    pe.wait_ge(s["kt"], min(p + 1, N_CHUNK))
                    pe.wait_ge(s["bt"], j + 1)
                    pe.wait_ge(s["un"], j + 1)
                    pe.wait_ge(s["mkr"], with_r(j + 1))
                    pe.wait_ge(s["mbr"], with_r(j + 1))
                    products(BX, lambda q, d, ct, r: (S[r, 0, col(q)], R[r, d, ct, 64 * (chunk_at(d, j) - N_CTX):64 * (chunk_at(d, j) - N_CTX) + 64]),
                             lambda q, d, ct, r: (v_tok[r, ct, chunk_at(d, j)], Mkr[r, j % 2, col(q)]),
                             lambda q, d, ct, r: (Un[r, 0, col(q)], Mbr[r, j % 2, col(q)])).then_inc(s["y_mm"], 1)
                if prep:
                    level_t(p, 3)
                    level_w(p, 4)
                if solve and j < N_CHUNK - 1:
                    pe.wait_ge(s["un"], j + 1)
                    pe.wait_ge(s["kt"], j + 1)
                    pe.wait_ge(s["bt"], j + 1)
                    pe.wait_ge(s["z"], j + 1)
                    products(BZ, lambda q, d, ct, r: (KT[r, j % 2, col(q)], v_tok[r, ct, chunk_at(d, j)]),
                             lambda q, d, ct, r: (BT[r, j % 2, col(q)], Un[r, 0, col(q)])).then_inc(s["s_mm"], 1)
                if prep:
                    level_t(p, 4)
                    level_w(p, 5)
                    pe.wait_ge(s["kt"], p + 1)
                    if solve and j >= N_CTX:
                        pe.wait_ge(s["y"], with_r(j + 1))
                    products(BX, lambda q, d, ct, r: (B[r, d, ct, 64 * chunk_at(d, p):64 * chunk_at(d, p) + 64],
                                                      k.c("eye64", 0, 64)[r])).then_inc(s["b_turned"], 1)
                    level_t(p, 5)
                    level_w(p, 6)
                    level_t(p, 6)

        @block.gpsimd
        def _(pool):
            for p in range(N_CHUNK):
                pool.wait_ge(s["mba"], p + 1)
                for l in range(1, 7):
                    if l == 1 and p:
                        pool.wait_ge(s["w_mm"], LV * p - 1)
                    if l == 2 and p:
                        pool.wait_ge(s["w_mm"], LV * p)
                    if l == 3:
                        pool.wait_ge(s["e1"], p + 1)
                        pool.wait_ge(s["tt"], 6 * p + 1)
                    if l > 3:
                        pool.wait_ge(s["w_mm"], LV * p + l - 3)
                    pool.tensor_tensor(eight(E[:, l % 2]), eight(Mba[:, 0]), level(l), MUL).then_inc(s["e"], 1)

        @block.scalar
        def _(act):
            for it in range(N_CHUNK + 1):
                p, j = it, it - 1
                prep, solve = p < N_CHUNK, j >= 0

                def copy_w(l):
                    act.wait_ge(s["w_mm"], LV * p + l - 1)
                    act.activation(W[:, 0], BW[:, :], ACT.Copy).then_inc(s["w"], 1)

                if solve:
                    act.wait_ge(s["z_mm"], j + 1)
                    act.activation(Z[:, 0], BZ[:, :], ACT.Copy).then_inc(s["z"], 1)
                    act.wait_ge(s["u_mm"], j + 1)
                    act.activation(Un[:, 0], BU[:, :], ACT.Copy, scale=-1.0).then_inc(s["un"], 1)
                if prep:
                    copy_w(2)
                    act.wait_ge(s["k_turned"], p + 1)
                    act.activation(KT[:, p % 2], BX[:, :], ACT.Copy).then_inc(s["kt"], 1)
                    copy_w(3)
                    copy_w(4)
                    copy_w(5)
                    act.wait_ge(s["b_turned"], p + 1)
                    act.activation(BT[:, p % 2], BX[:, :], ACT.Copy).then_inc(s["bt"], 1)
                    copy_w(6)

        @block.vector
        def _(dve):
            dve.memset(S[:, 0], 0.0).then_inc(s["s"], 1)

            def masked(dst, bank, x, ready, done, n):
                dve.wait_ge(s[ready], n)
                m = causal[:, :, x:x + 1].broadcast_to([P, 2, 4, 64])
                dve.tensor_tensor(dst.rearrange("p (d c t) -> p d c t", d=2, c=4),
                                  bank[:, :].rearrange("p (d c t) -> p d c t", d=2, c=4), m, MUL).then_inc(s[done], 1)

            for it in range(N_CHUNK + 1):
                p, j = it, it - 1
                prep, solve = p < N_CHUNK, j >= 0

                def level_update(l):
                    if l < 6:
                        dve.wait_ge(s["t_mm"], (LV - 1) * p + l - 1)
                        dve.tensor_tensor(T[:, 0], T[:, 0], BT_[:, :], SUB).then_inc(s["t"], 1)
                    dve.wait_ge(s["tt_mm"], LV * p + l - 1)
                    dve.tensor_tensor(Tt[:, p % 2], Tt[:, p % 2], BTT[:, :], SUB).then_inc(s["tt"], 1)

                if prep:
                    if p:
                        dve.wait_ge(s["e"], 6 * p)
                    masked(Mba[:, 0], GA, 0, "g_ba", "mba", p + 1)
                    masked(Mka[:, p % 2], GB, 0, "g_ka", "mka", p + 1)
                    dve.wait_ge(s["e1"], p + 1)
                    dve.tensor_tensor(eight(T[:, 0]), eye, eight(BT_[:, :]), SUB).then_inc(s["t"], 1)
                    dve.wait_ge(s["e"], 6 * p + 1)
                    dve.tensor_tensor(eight(Tt[:, p % 2]), eye, eight(E[:, 1]), SUB).then_inc(s["tt"], 1)
                    if p >= N_CTX:
                        masked(Mbr[:, p % 2], GA, 1, "g_br", "mbr", with_r(p + 1))
                        masked(Mkr[:, p % 2], GB, 1, "g_kr", "mkr", with_r(p + 1))
                    level_update(2)
                if solve and j >= N_CTX:
                    dve.wait_ge(s["y_mm"], with_r(j + 1))
                    for d in range(2):
                        c = chunk_at(d, j) - N_CTX
                        y = Y[:, :, 64 * c:64 * c + 64]
                        part = BX[:, 256 * d:256 * d + 256].rearrange("p (c t) -> p c t", c=4)
                        first = j < N_CTX + (N_CHUNK - N_CTX) // 2
                        ins = dve.tensor_copy(y, part) if first else dve.tensor_tensor(y, y, part, ADD)
                    ins.then_inc(s["y"], 1)
                if prep:
                    level_update(3)
                if solve and j < N_CHUNK - 1:
                    dve.wait_ge(s["s_mm"], j + 1)
                    dve.tensor_tensor(St[:, 0], S[:, 0], BZ[:, :], ADD).then_inc(s["st"], 1)
                    dve.wait_ge(s["st"], j + 1)
                    decay = chunk_decay[:, j, :].rearrange("p (q t) -> p q t", t=1).broadcast_to([P, 8, 64])
                    dve.tensor_tensor(eight(S[:, 0]), eight(St[:, 0]), decay, MUL).then_inc(s["s"], 1)
                if prep:
                    level_update(4)
                    level_update(5)
                    level_update(6)


def rwkv_out_stage(k, Y, bonus_v, gate_in, g2, rw, work, loads, landed):
    nc = k.nc
    centred = k.at(work, 4 * SEQ).rearrange("p (c t) -> p c t", c=4)
    squares = k.at(work + 2048, 4 * SEQ).rearrange("p (c t) -> p c t", c=4)
    rstd = k.at(work + 4096, 4 * SEQ).rearrange("p (c t) -> p c t", c=4)
    s = {n: k.sem("rwkv_out_" + n) for n in ("mean_mm", "centred", "sq", "var_mm", "root", "rstd", "scaled", "based",
                                            "gate_mm", "done")}
    with nc.Block("rwkv_out") as block:
        @block.sync
        def _(sp):
            for dst, src in loads:
                sp.dma_start(dst, src).then_inc(landed, 16)
            sp.wait_ge(landed, 16 * len(loads))

        @block.tensor
        def _(pe):
            for ct in range(KC):
                pe.matmul(k.bank[ct][:, :], k.c("head_ones"), Y[:, ct], start=True, stop=True).then_inc(s["mean_mm"], 1)
            for ct in range(KC):
                pe.wait_ge(s["sq"], ct + 1)
                pe.matmul(k.bank[4 + ct][:, :], k.c("head_ones"), squares[:, ct], start=True, stop=True).then_inc(s["var_mm"], 1)
            pe.wait_ge(landed, 16 * len(loads))
            for ct in range(KC):
                pe.wait_ge(s["centred"], ct + 1)
                pe.matmul(k.bank[ct][:, :], g2[:, P * ct:P * ct + P], gate_in, start=True, stop=True).then_inc(s["gate_mm"], 1)

        @block.scalar
        def _(act):
            for ct in range(KC):
                act.wait_ge(s["centred"], ct + 1)
                act.activation(squares[:, ct], centred[:, ct], ACT.Square).then_inc(s["sq"], 1)
            for ct in range(KC):
                act.wait_ge(s["var_mm"], ct + 1)
                act.activation(rstd[:, ct], k.bank[4 + ct][:, :], ACT.Sqrt, bias=k.v("eps_gn"), scale=1.0 / HEAD).then_inc(s["root"], 1)

        @block.vector
        def _(dve):
            for ct in range(KC):
                dve.wait_ge(s["mean_mm"], ct + 1)
                dve.scalar_tensor_tensor(out=centred[:, ct], in0=k.bank[ct][:, :], scalar=-1.0 / HEAD, in1=Y[:, ct],
                                         op0=MUL, op1=ADD).then_inc(s["centred"], 1)
            for ct in range(KC):
                dve.wait_ge(s["root"], ct + 1)
                dve.reciprocal(rstd[:, ct], rstd[:, ct]).then_inc(s["rstd"], 1)
                dve.wait_ge(s["rstd"], ct + 1)
                dve.scalar_tensor_tensor(out=Y[:, ct], in0=centred[:, ct], scalar=k.v("gn_g", ct), in1=rstd[:, ct],
                                         op0=MUL, op1=MUL).then_inc(s["scaled"], 1)
                dve.wait_ge(s["scaled"], ct + 1)
                dve.scalar_tensor_tensor(out=Y[:, ct], in0=Y[:, ct], scalar=k.v("gn_b", ct), in1=bonus_v[:, ct],
                                         op0=ADD, op1=ADD).then_inc(s["based"], 1)
                dve.wait_ge(s["based"], ct + 1)
                dve.wait_ge(s["gate_mm"], ct + 1)
                dve.tensor_tensor(rw[:, ct], Y[:, ct], k.bank[ct][:, :], MUL).then_inc(s["done"], 1)


def fourier_stage(k, u, seq, chan, mixed, parts):
    nc = k.nc
    chan_mm, chan_out, seq_mm, seq_out = (k.sem("fourier_" + n) for n in ("channels", "channels_out", "tokens", "tokens_out"))
    with nc.Block("fourier") as block:
        @block.tensor
        def _(pe):
            for tt in range(4):
                for ct in range(KC):
                    i = 4 * tt + ct
                    if i >= 4:
                        pe.wait_ge(chan_out, i - 3)
                    pe.matmul(k.bank[i % 4][:, 0:256], u[:, ct, P * tt:P * tt + P], chan, start=True, stop=True).then_inc(chan_mm, 1)
            pe.wait_ge(chan_out, 16)
            for ct in range(KC):
                for i in range(8):
                    last = pe.matmul(k.bank[4 + ct][:, :], parts[:, i % 4, ct, P * (i // 4):P * (i // 4) + P],
                                     seq[:, i // 4, i % 4], start=i == 0, stop=i == 7)
                last.then_inc(seq_mm, 1)

        @block.scalar
        def _(act):
            for i in range(16):
                act.wait_ge(chan_mm, i + 1)
                act.activation(parts[:, i // 4, i % 4], k.bank[i % 4][:, 0:256], ACT.Copy).then_inc(chan_out, 1)
            for ct in range(KC):
                act.wait_ge(seq_mm, ct + 1)
                act.activation(mixed[:, ct], k.bank[4 + ct][:, :], ACT.Copy).then_inc(seq_out, 1)


def residual_stage(k, name, per, tiles_of, rhs, gate, x, dst, mod=None):
    nc = k.nc
    summed, done = k.sem(name + "_summed"), k.sem(name + "_done")
    if mod:
        mod_acc, mod_step = k.sem("mod2_acc"), [k.sem("mod2_step"), 0]
        for g in range(24):
            k.freed[k.number("ada2", g)] = [(mod_acc, g + 1 + min(g + 1, 8))]
    with nc.Block(name) as block:
        @block.sync
        def _(sp):
            k.send_weights(sp)

        @block.tensor
        def _(pe):
            for m in range(KD):
                if m >= 4:
                    pe.wait_ge(done, m - 3)
                pieces = tiles_of(m)
                n = sum(len(cols) for _, cols in pieces)
                i = 0
                for g, cols in pieces:
                    k.weights_ready(pe, g)
                    for w, kt in cols:
                        last = pe.matmul(k.bank[m % 4][:, :], w, rhs[:, kt], start=i == 0, stop=i == n - 1)
                        i += 1
                    if g != pieces[-1][0]:
                        last.then_inc(summed, 1)
                last.then_inc(summed, 1)

        @block.vector
        def _(dve):
            for m in range(KD):
                for g in range(3 * m, 3 * m + 3) if mod else ():
                    for t in range(2 if g < 8 else 1):
                        mod_slot(k, dve, "ada2", g, k.silu[1], mod[t][:, 256 * g:256 * g + 256], t, mod_step, mod_acc)
                dve.wait_ge(summed, per * (m + 1))
                dve.scalar_tensor_tensor(out=dst[:, m], in0=k.bank[m % 4][:, :], scalar=gate(m), in1=x[:, m],
                                         op0=MUL, op1=ADD).then_inc(done, 1)


def halves(k, name):
    def pieces(m):
        g = k.number(name, m // 2)
        w = k.slot(g).rearrange("p (k m) -> p k m", k=KD)
        return [(g, [(w[:, kt, P * (m % 2):P * (m % 2) + P], kt) for kt in range(KD)])]
    return pieces


def ffn_up_stage(k, h, hidden, work):
    nc = k.nc
    NP = 3
    PADW = (ROWS + 2) * (GRID_W + 2)
    pad = k.at(work, NP * 2 * PADW).rearrange("p (n h r c) -> p n h r c", n=NP, h=2, r=ROWS + 2)
    acc = k.at(work + NP * 2 * PADW, 2 * 2 * SEQ).rearrange("p (n h r c) -> p n h r c", n=2, h=2, r=ROWS)
    s = {n: k.sem("ffn_" + n) for n in ("zeroed", "up_mm", "padded", "tap", "tapped", "silu", "hidden")}
    k.frees([k.number("w_up", m) for m in range(KF)], s["up_mm"])
    flat = lambda x: x.rearrange("p r c -> p (r c)")
    with nc.Block("ffn_up") as block:
        @block.sync
        def _(sp):
            k.send_weights(sp)

        @block.gpsimd
        def _(pool):
            pool.memset(k.at(work, NP * 2 * PADW), 0.0).then_inc(s["zeroed"], 1)

        @block.tensor
        def _(pe):
            for m in range(KF):
                g = k.number("w_up", m)
                k.weights_ready(pe, g)
                w = k.slot(g).rearrange("p (k h m) -> p k h m", k=KD, h=2)
                if m >= 3:
                    pe.wait_ge(s["padded"], m - 2)
                for h2 in range(2):
                    for kt in range(KD):
                        last = pe.matmul(k.bank[2 * (m % 3) + h2][:, :], w[:, kt, h2], h[:, kt], start=kt == 0, stop=kt == KD - 1)
                last.then_inc(s["up_mm"], 1)

        @block.scalar
        def _(act):
            act.wait_ge(s["zeroed"], 1)
            for m in range(KF + 1):
                if m < KF:
                    act.wait_ge(s["up_mm"], m + 1)
                    if m >= NP:
                        act.wait_ge(s["tapped"], 2 * (m - NP + 1))
                    for h2 in range(2):
                        ins = act.activation(pad[:, m % NP, h2, 1:ROWS + 1, 1:GRID_W + 1],
                                             k.bank[2 * (m % 3) + h2][:, :].rearrange("p (r c) -> p r c", r=ROWS), ACT.Copy)
                    ins.then_inc(s["padded"], 1)
                if m >= 1:
                    act.wait_ge(s["tapped"], 2 * m - 1)
                    g = flat(acc[:, (m - 1) % 2, 0])
                    act.activation(g, g, ACT.Silu).then_inc(s["silu"], 1)

        @block.vector
        def _(dve):
            n = 0
            for m in range(KF):
                dve.wait_ge(s["padded"], m + 1)
                for h2 in range(2):
                    t = m + KF * h2
                    a = acc[:, m % 2, h2]
                    for i in range(9):
                        src = pad[:, m % NP, h2, i // 3:i // 3 + ROWS, i % 3:i % 3 + GRID_W]
                        w = k.v("ffn_conv_w", i * 2 * KF + t)
                        if i == 0:
                            ins = dve.tensor_scalar(a, src, w, k.v("ffn_conv_b", t), MUL, ADD)
                        else:
                            dve.wait_ge(s["tap"], n)
                            ins = dve.scalar_tensor_tensor(out=a, in0=src, scalar=w, in1=a, op0=MUL, op1=ADD)
                        if i < 8:
                            ins.then_inc(s["tap"], 1)
                            n += 1
                        else:
                            ins.then_inc(s["tapped"], 1)
                dve.wait_ge(s["silu"], m + 1)
                dve.wait_ge(s["tapped"], 2 * m + 2)
                dve.tensor_tensor(hidden[:, m], flat(acc[:, m % 2, 0]), flat(acc[:, m % 2, 1]), MUL).then_inc(s["hidden"], 1)


def block_one(k):
    nc, d = k.nc, k.d
    three = lambda at, n, w: k.at(at, n * w).rearrange("p (n w) -> p n w", n=n)
    four = lambda at, t: k.at(at, 2 * 4 * t).rearrange("p (d c t) -> p d c t", d=2, c=4)
    x_landed = k.sem("x_landed")
    h, x0 = three(0, KD, ALL), three(6144, KD, ALL)
    mod_first_stage(k, (k.at(6144, KD * ALL), d["x0"].rearrange("p k t -> p (k t)"), x_landed))
    m1 = k.mod[0]
    norm_stage(k, "norm1", x0, h, [(0, CTX, 0), (CTX, SEQ, 1)],
               gain=lambda i: [(m1[:, 8:16, 1 - i], k.v("norm1_g", 0, 8))],
               shift=lambda kt, i: m1[:, kt, 1 - i:2 - i], work=12288, first=(x_landed, 16))
    kp, vp, rp = three(12288, 4, 772), three(15376, 4, 772), three(18464, 4, 514)
    uf = three(6144, 4, SEQ)
    gd, wd, ad = k.at(29696, SEQ), k.at(30208, ALL), k.at(30976, ALL)
    ID = ACT.Copy
    u = {}
    for ct in range(4):
        u[ct] = ([(uf[:, ct], ID)], None)
        u[4 + ct] = ([(rp[:, ct, 1:1 + SEQ], ID)], None)
        for o, pad in ((8, kp), (12, vp)):
            u[o + ct] = ([(pad[:, ct, CTX + 3:CTX + 3 + SEQ], ID)], [(pad[:, ct, 1:1 + CTX], ID)])
    u[16] = ([(wd[:, CTX:ALL], ACT.Tanh)], [(wd[:, 0:CTX], ACT.Tanh)])
    u[17] = ([(ad[:, CTX:ALL], ID)], [(ad[:, 0:CTX], ID)])
    u[18] = ([(gd, ACT.Sigmoid)], None)
    zeros = [rp[:, :, 0:SEQ + 2:SEQ + 1]] + [p[:, :, a:b] for p in (kp, vp) for a, b in ((0, 1), (CTX + 1, CTX + 3), (771, 772))]
    vf, kf, r = three(32512, 4, ALL), three(35584, 4, ALL), three(38656, 4, SEQ)
    convs = {}
    for ct in range(4):
        convs[4 + ct] = [(rp[:, ct], r[:, ct], ct)]
        for m, pad, dst, w in ((8, kp, kf, 4), (12, vp, vf, 8)):
            convs[m + ct] = [(pad[:, ct, 0:CTX + 2], dst[:, ct, 0:CTX], w + ct),
                             (pad[:, ct, CTX + 2:CTX + SEQ + 4], dst[:, ct, CTX:ALL], w + ct)]
    in_proj_stage(k, h, u, zeros, convs, k.at(8192, 4608))
    A, R, K, B = four(0, ALL), four(6144, SEQ), four(10240, ALL), four(16384, ALL)
    v_tok = k.at(22528, 3072).rearrange("p (c n i) -> p c n i", c=4, n=N_CHUNK)
    bonus_v, Y, kk = three(25600, 4, SEQ), three(27648, 4, SEQ), three(25600, 4, ALL)
    chunk_decay = k.mem[:, k.decay_at:k.decay_at + 96].rearrange("p (n q) -> p n q", q=8)
    uf_dram = nc.dram_tensor("fourier_in", [P, 4 * SEQ], F32, kind="Internal").ap()
    lora = k.at(10240, 1024)
    key_stage(k, kf, vf, kk, v_tok, (uf_dram, k.at(6144, 2048)), (lora, d["lora"]))
    lora_stage(k, wd, ad, lora, A, B)
    factor_stage(k, A, R, K, B, r, kf, kk, vf, bonus_v, chunk_decay, k.at(30208, 2304))
    scan_stage(k, A, R, K, B, v_tok, Y, chunk_decay, 30208)
    cat, g2, x = three(0, 8, SEQ), k.at(14592, CH), three(15104, KD, SEQ)
    landed = k.sem("mix_loads_landed")
    loads = [(g2, d["gate_g2"]), (k.at(4096, 2048), d["seq_dft"][0]), (k.at(6144, 2048), d["seq_dft"][1]),
             (k.at(8192, 256), d["chan_dft"]), (k.at(8448, 2048), uf_dram), (x, d["x0"][:, :, CTX:ALL])]
    rwkv_out_stage(k, Y, bonus_v, gd, g2, cat[:, 4:8], 19200, loads, landed)
    parts = k.at(10496, 4096).rearrange("p (t c m) -> p t c m", t=4, c=4)
    seq = k.at(4096, 4096).rearrange("p (x t n) -> p x t n", x=2, t=4)
    fourier_stage(k, three(8448, 4, SEQ), seq, k.at(8192, 256), cat[:, 0:4], parts)
    norm_stage(k, "fourier_norm", cat[:, 0:4], cat[:, 0:4], [(0, SEQ, 0)],
               gain=lambda i: [(k.v("fourier_g", 0, 4), None)], shift=None, work=19200, tiles=4)
    x1, h2 = three(30208, KD, SEQ), three(35840, KD, SEQ)

    k.frees_later([k.number("w_out", g) for g in range(4)], "w_out_summed", 2)
    residual_stage(k, "w_out", 1, halves(k, "w_out"), cat, lambda m: m1[:, 16 + m, 0:1], x, x1)
    norm_stage(k, "norm2", x1, h2, [(0, SEQ, 0)], gain=lambda i: [(m1[:, 32:40, 0], k.v("norm2_g", 0, 8))],
               shift=lambda kt, i: m1[:, 24 + kt, 0:1], work=0)
    hidden = three(0, KF, SEQ)
    mod_sums = [k.at(21504, 6144), k.at(27648, 2048)]
    ffn_up_stage(k, h2, hidden, 11264)
    x2 = three(17408, KD, SEQ)
    k.frees_later([k.number("w_down", g) for g in range(16)], "w_down_summed", 1)

    def down(m):
        out = []
        for half in range(2):
            g = k.number("w_down", 2 * m + half)
            w = k.slot(g, 11 * P).rearrange("p (k m) -> p k m", k=11)
            out.append((g, [(w[:, i], 11 * half + i) for i in range(11)]))
        return out
    residual_stage(k, "w_down", 2, down, hidden, lambda m: m1[:, 40 + m, 0:1], x1, x2, mod=mod_sums)
    src = three(0, KD, ALL)
    norm_stage(k, "final1", x2, src[:, :, CTX:ALL], [(0, SEQ, 0)], gain=lambda i: [(k.v("final_g", 0, 8), None)],
               shift=None, work=35840, loads=[(src[:, :, 0:CTX], d["ctx2"])], mod2=(cut(mod_sums[0]) + cut(mod_sums[1]), k.at(34304, 512)))
    return src


def in_proj2_stage(k, h, q, kf, v_tok, upad, sig, gate_a, gate_b, conv):
    nc = k.nc
    s = {n: k.sem("proj2_" + n) for n in ("summed", "copied", "padded", "gated", "tap")}
    K2 = 31
    units, total = [], 0
    for g in range(4):
        units += [(k.number("w_in2_q", g), "qk", 2 * g + j) for j in range(2)]
    for g in range(2):
        units += [(k.number("w_in2_v", g), "v", t) for t in range(6)]
    for g in range(12):
        units += [(k.number("w_in2_g", g), "glu" if g < 4 else "gate", 2 * g + j) for j in range(2)]
    for i, (g, _, _) in enumerate(units):
        k.freed[g] = [(s["summed"], i + 1)]
    glu_g = [i for i, u in enumerate(units) if u[1] == "glu" and u[2] >= 4]
    with nc.Block("in_proj2") as block:
        @block.sync
        def _(sp):
            k.send_weights(sp)

        @block.gpsimd
        def _(pool):
            pool.memset(upad[:, :, 0:15], 0.0).then_inc(s["padded"], 1)
            pool.memset(upad[:, :, SEQ + 15:SEQ + 30], 0.0).then_inc(s["padded"], 1)

        @block.tensor
        def _(pe):
            for i, (g, kind, t) in enumerate(units):
                k.weights_ready(pe, g)
                w = k.slot(g).rearrange("p (k m) -> p k m", k=KD)
                if i >= 3:
                    pe.wait_ge(s["copied"], i - 2)
                b = k.bank[2 * (i % 3)]
                for kt in range(KD):
                    if kind == "v":
                        last = pe.matmul(b[:, 0:256], h[:, kt, P * t:P * t + P], w[:, kt], start=kt == 0, stop=kt == KD - 1)
                    else:
                        last = pe.matmul(b[:, :], w[:, kt, P * (t % 2):P * (t % 2) + P], h[:, kt, CTX:ALL],
                                         start=kt == 0, stop=kt == KD - 1)
                if kind == "qk" and t >= 4:
                    for kt in range(KD):
                        last = pe.matmul(k.bank[2 * (i % 3) + 1][:, 0:CTX], w[:, kt, P * (t % 2):P * (t % 2) + P],
                                         h[:, kt, 0:CTX], start=kt == 0, stop=kt == KD - 1)
                last.then_inc(s["summed"], 1)

        @block.scalar
        def _(act):
            for i, (g, kind, t) in enumerate(units):
                act.wait_ge(s["summed"], i + 1)
                b = k.bank[2 * (i % 3)]
                if kind == "qk" and t < 4:
                    ins = act.activation(q[:, t], b[:, :], ACT.Copy)
                elif kind == "qk":
                    act.activation(kf[:, t - 4, CTX:ALL], b[:, :], ACT.Copy)
                    ins = act.activation(kf[:, t - 4, 0:CTX], k.bank[2 * (i % 3) + 1][:, 0:CTX], ACT.Copy)
                elif kind == "v":
                    half = g - k.number("w_in2_v", 0)
                    ins = act.activation(v_tok[:, t, 256 * half:256 * half + 256], b[:, 0:256], ACT.Copy)
                elif kind == "glu" and t < 4:
                    ins = act.activation(upad[:, t, 15:15 + SEQ], b[:, :], ACT.Copy)
                elif kind == "glu":
                    ins = act.activation(sig[:, t - 4], b[:, :], ACT.Sigmoid)
                else:
                    dst = gate_a[:, t - 8] if t < 16 else gate_b[:, t - 16]
                    ins = act.activation(dst, b[:, :], ACT.Sigmoid)
                ins.then_inc(s["copied"], 1)

        @block.vector
        def _(dve):
            for ct in range(KC):
                dve.wait_ge(s["copied"], glu_g[ct] + 1)
                u = upad[:, ct, 15:15 + SEQ]
                dve.tensor_tensor(u, u, sig[:, ct], MUL).then_inc(s["gated"], 1)
            dve.wait_ge(s["gated"], 4)
            dve.wait_ge(s["padded"], 2)
            for i in range(K2):
                for ct in range(KC):
                    src, w = upad[:, ct, i:i + SEQ], k.v("conv2_w", 4 * i + ct)
                    if i == 0:
                        ins = dve.tensor_scalar(conv[:, ct], src, w, k.v("conv2_b", ct), MUL, ADD)
                    else:
                        dve.wait_ge(s["tap"], 4 * (i - 1) + ct + 1)
                        ins = dve.scalar_tensor_tensor(out=conv[:, ct], in0=src, scalar=w, in1=conv[:, ct], op0=MUL, op1=ADD)
                    ins.then_inc(s["tap"], 1)


def layer_norm_stage(k, x, work):
    nc = k.nc
    squares = k.at(work, 4 * SEQ).rearrange("p (c t) -> p c t", c=4)
    rstd = k.at(work + 2048, SEQ)
    s = {n: k.sem("ln_" + n) for n in ("mean", "centred", "sq", "var", "root", "rstd", "scaled", "silu")}
    with nc.Block("layer_norm") as block:
        @block.tensor
        def _(pe):
            for ct in range(KC):
                last = pe.matmul(k.bank[0][:, :], k.c("ones"), x[:, ct], start=ct == 0, stop=ct == 3)
            last.then_inc(s["mean"], 1)
            for ct in range(KC):
                pe.wait_ge(s["sq"], ct + 1)
                last = pe.matmul(k.bank[1][:, :], k.c("ones"), squares[:, ct], start=ct == 0, stop=ct == 3)
            last.then_inc(s["var"], 1)

        @block.vector
        def _(dve):
            dve.wait_ge(s["mean"], 1)
            for ct in range(KC):
                dve.scalar_tensor_tensor(out=x[:, ct], in0=k.bank[0][:, :], scalar=-1.0 / CH, in1=x[:, ct],
                                         op0=MUL, op1=ADD).then_inc(s["centred"], 1)
            dve.wait_ge(s["root"], 1)
            dve.reciprocal(rstd, rstd).then_inc(s["rstd"], 1)
            dve.wait_ge(s["rstd"], 1)
            dve.wait_ge(s["sq"], 4)
            for ct in range(KC):
                dve.scalar_tensor_tensor(out=x[:, ct], in0=x[:, ct], scalar=k.v("ln_g", ct), in1=rstd,
                                         op0=MUL, op1=MUL).then_inc(s["scaled"], 1)

        @block.scalar
        def _(act):
            for ct in range(KC):
                act.wait_ge(s["centred"], ct + 1)
                act.activation(squares[:, ct], x[:, ct], ACT.Square).then_inc(s["sq"], 1)
            act.wait_ge(s["var"], 1)
            act.activation(rstd, k.bank[1][:, :], ACT.Sqrt, bias=k.v("eps_norm"), scale=1.0 / CH).then_inc(s["root"], 1)
            for ct in range(KC):
                act.wait_ge(s["scaled"], ct + 1)
                act.activation(x[:, ct], x[:, ct], ACT.Silu, bias=k.v("ln_b", ct)).then_inc(s["silu"], 1)


def attention_stage(k, q, kf, v_tok, att, work_bias, work_s, work_p):
    nc = k.nc
    NS = 14
    bias = k.at(work_bias, 2 * NS * 64).rearrange("p (n s c) -> p n s c", n=2, s=NS)
    sc = k.at(work_s, 2 * ALL).rearrange("p (n w) -> p n w", n=2)
    pt = k.at(work_p, 2 * 6 * SEQ).rearrange("p (n j w) -> p n j w", n=2, j=6)
    col = k.small.rearrange("p (n x) -> p n x", n=2)
    s = {n: k.sem("att_" + n) for n in ("bias_ready", "masked", "s_mm", "s_lat", "s_ctx", "max", "neg", "exp", "inv", "p",
                                       "turned", "pt", "av_mm", "av")}
    landed = [k.sem(f"att_bias_landed_{i}") for i in range(2)]
    rpb = k.d["rpb"]
    N = 32
    SCALE = HEAD ** -0.5
    with nc.Block("attention") as block:
        @block.sync
        def _(sp):
            for hd in range(8):
                if hd >= 2:
                    sp.wait_ge(s["s_lat"], 4 * (hd - 1))
                for par in range(2):
                    off = 64 + hd * 465 + (1 - par) * 31 - 48
                    src = bass.AP(rpb.tensor, off, [[1, 64], [31, NS], [1, 64]])
                    sp.dma_start(bias[64 * par:64 * par + 64, hd % 2], src).then_inc(landed[hd % 2], 16)
            k.send_weights(sp)

        @block.gpsimd
        def _(pool):
            over = lambda name: k.c(name, 0, 64).rearrange("p (s c) -> p s c", s=1).broadcast_to([P, NS, 64])
            for hd in range(8):
                pool.wait_ge(landed[hd % 2], 32 * (hd // 2 + 1))
                pool.tensor_tensor(bias[:, hd % 2], bias[:, hd % 2], over("pair_mask"), MUL).then_inc(s["masked"], 1)
                pool.wait_ge(s["masked"], hd + 1)
                pool.tensor_tensor(bias[:, hd % 2], bias[:, hd % 2], over("pair_neg"), ADD).then_inc(s["bias_ready"], 1)

        @block.tensor
        def _(pe):
            def scores(u):
                hd, i = divmod(u, 4)
                r, ct = slice(64 * (hd % 2), 64 * (hd % 2) + 64), hd // 2
                if u >= 2:
                    pe.wait_ge(s["s_lat"], u - 1)
                    pe.wait_ge(s["s_ctx"], u - 1)
                b = 2 * (u % 2)
                pe.matmul(k.bank[b][:, :], q[r, ct, P * i:P * i + P], kf[r, ct, CTX:ALL], start=True, stop=True)
                pe.matmul(k.bank[b + 1][:, 0:CTX], q[r, ct, P * i:P * i + P], kf[r, ct, 0:CTX],
                          start=True, stop=True).then_inc(s["s_mm"], 1)

            scores(0)
            for u in range(N):
                hd, i = divmod(u, 4)
                if u + 1 < N:
                    scores(u + 1)
                pe.wait_ge(s["p"], u + 1)
                if u:
                    pe.wait_ge(s["pt"], u)
                for j in range(6):
                    last = pe.transpose(k.bank[4 + j // 4][:, P * (j % 4):P * (j % 4) + P], sc[:, u % 2, P * j:P * j + P],
                                        k.c("ident"))
                last.then_inc(s["turned"], 1)
                if i == 3:
                    pe.wait_ge(s["pt"], u + 1)
                    if hd >= 2:
                        pe.wait_ge(s["av"], hd - 1)
                    r = slice(64 * (hd % 2), 64 * (hd % 2) + 64)
                    for j in range(6):
                        last = pe.matmul(k.bank[6 + hd % 2][r, :], v_tok[:, j, 64 * hd:64 * hd + 64], pt[:, hd % 2, j],
                                         start=j == 0, stop=j == 5)
                    last.then_inc(s["av_mm"], 1)

        @block.scalar
        def _(act):
            def ctx_scores(u):
                act.wait_ge(s["s_mm"], u + 1)
                if u >= 2:
                    act.wait_ge(s["turned"], u - 1)
                act.activation(sc[:, u % 2, 0:CTX], k.bank[2 * (u % 2) + 1][:, 0:CTX], ACT.Copy, scale=SCALE).then_inc(s["s_ctx"], 1)

            ctx_scores(0)
            for u in range(N):
                hd, i = divmod(u, 4)
                act.wait_ge(s["neg"], u + 1)
                c = col[:, u % 2]
                act.activation(sc[:, u % 2], sc[:, u % 2], ACT.Exp, bias=c[:, 1:2], accum_out=c[:, 2:3]).then_inc(s["exp"], 1)
                if u + 1 < N:
                    ctx_scores(u + 1)
                act.wait_ge(s["turned"], u + 1)
                act.activation(pt[:, hd % 2, 0:4, P * i:P * i + P], k.bank[4][:, :].rearrange("p (j w) -> p j w", j=4), ACT.Copy)
                act.activation(pt[:, hd % 2, 4:6, P * i:P * i + P], k.bank[5][:, 0:256].rearrange("p (j w) -> p j w", j=2),
                               ACT.Copy).then_inc(s["pt"], 1)
                if i == 3:
                    act.wait_ge(s["av_mm"], hd + 1)
                    r = slice(64 * (hd % 2), 64 * (hd % 2) + 64)
                    act.activation(att[r, hd // 2], k.bank[6 + hd % 2][r, :], ACT.Copy).then_inc(s["av"], 1)

        @block.vector
        def _(dve):
            def lat_scores(u):
                hd, i = divmod(u, 4)
                dve.wait_ge(s["s_mm"], u + 1)
                if i == 0:
                    dve.wait_ge(s["bias_ready"], hd + 1)
                if u >= 2:
                    dve.wait_ge(s["turned"], u - 1)
                dve.scalar_tensor_tensor(out=sc[:, u % 2, CTX:ALL].rearrange("p (s c) -> p s c", s=ROWS),
                                         in0=k.bank[2 * (u % 2)][:, :].rearrange("p (s c) -> p s c", s=ROWS), scalar=SCALE,
                                         in1=bias[:, hd % 2, 6 - 2 * i:14 - 2 * i, ::-1], op0=MUL, op1=ADD).then_inc(s["s_lat"], 1)

            lat_scores(0)
            for u in range(N):
                c = col[:, u % 2]
                dve.wait_ge(s["s_lat"], u + 1)
                dve.wait_ge(s["s_ctx"], u + 1)
                dve.tensor_reduce(c[:, 0:1], sc[:, u % 2], AX, MAX).then_inc(s["max"], 1)
                dve.wait_ge(s["max"], u + 1)
                dve.tensor_scalar(c[:, 1:2], c[:, 0:1], -1.0, None, MUL).then_inc(s["neg"], 1)
                if u + 1 < N:
                    lat_scores(u + 1)
                dve.wait_ge(s["exp"], u + 1)
                dve.reciprocal(c[:, 3:4], c[:, 2:3]).then_inc(s["inv"], 1)
                dve.wait_ge(s["inv"], u + 1)
                dve.tensor_scalar(sc[:, u % 2], sc[:, u % 2], c[:, 3:4], None, MUL).then_inc(s["p"], 1)


def merge_stage(k, att, conv, gate_a, gate_b, mix):
    nc = k.nc
    s = {n: k.sem("merge_" + n) for n in ("summed", "a", "b", "mix")}
    for g in range(2):
        for name in ("w_att", "w_conv"):
            k.freed[k.number(name, g)] = [(s["summed"], 4 * (g + 1))]
    with nc.Block("merge") as block:
        @block.sync
        def _(sp):
            k.send_weights(sp)

        @block.tensor
        def _(pe):
            for m in range(KD):
                ga = k.number("w_att", m // 4)
                if m % 4 == 0:
                    k.weights_ready(pe, ga)
                    k.weights_ready(pe, ga + 1)
                if m >= 4:
                    pe.wait_ge(s["b"], m - 3)
                for n, rhs in enumerate((att, conv)):
                    w = k.slot(ga + n).rearrange("p (k m) -> p k m", k=4)
                    for kt in range(4):
                        last = pe.matmul(k.bank[2 * (m % 4) + n][:, :], w[:, kt, P * (m % 4):P * (m % 4) + P], rhs[:, kt],
                                         start=kt == 0, stop=kt == 3)
                last.then_inc(s["summed"], 1)

        @block.vector
        def _(dve):
            for m in range(KD):
                dve.wait_ge(s["summed"], m + 1)
                dve.tensor_tensor(gate_a[:, m], gate_a[:, m], k.bank[2 * (m % 4)][:, :], MUL).then_inc(s["a"], 1)
                dve.tensor_tensor(gate_b[:, m], gate_b[:, m], k.bank[2 * (m % 4) + 1][:, :], MUL).then_inc(s["b"], 1)
                dve.wait_ge(s["a"], m + 1)
                dve.wait_ge(s["b"], m + 1)
                dve.tensor_tensor(mix[:, m], gate_a[:, m], gate_b[:, m], ADD).then_inc(s["mix"], 1)


def route_stage(k, h, weights, table, h_dram, table_dram, w_router, ids, work):
    nc = k.nc
    off = [work]

    def buf(*dims):
        n = int(np.prod(dims))
        off[0] += n
        x = k.at(off[0] - n, n)
        if len(dims) == 2:
            return x.rearrange("p (a b) -> p a b", a=dims[0])
        if len(dims) == 3:
            return x.rearrange("p (a b c) -> p a b c", a=dims[0], b=dims[1])
        return x
    L, tie, one_g, ex, pg = buf(4, 36), buf(4, 8), buf(4, 4), buf(4, 4), buf(4, 1)
    top = [buf(4, 1), buf(4, 1)]
    gmax, least, total = buf(4, 1), buf(4, 1), buf(4, 1)
    picked, masked, part = buf(4, 8), buf(4, 8), buf(4, 4, 8)
    one_e = [buf(4, 8), buf(4, 8)]
    X = [buf(4, 32), buf(4, 32)]
    M, dest, tmp = buf(4, 32), buf(4, 32), buf(4, 32)
    j_tile, count, extra, upto = buf(4, 32), buf(32), buf(32), buf(32)
    slot_f = buf(4, 2)
    slot_i = buf(4, 2).bitcast(I32)
    tok_rows = k.at(work + 2048, 2 * D).rearrange("p (n w) -> p n w", n=2)
    s = {n: k.sem("route_" + n) for n in ("logits", "step", "exped", "rank_in", "rank", "slots", "blank", "scattered",
                                         "loaded", "turned", "rows")}
    rows_out = [k.sem(f"route_rows_out_{i}") for i in range(2)]
    iota = k.c("expert_id", 0, 32)
    n_step = [0]
    with nc.Block("route") as block:
        @block.sync
        def _(sp):
            sp.dma_start(table_dram.rearrange("(p b) t -> p (b t)", p=P), k.blank).then_inc(s["blank"], 16)
            for tt in range(4):
                sp.wait_ge(s["rows"], tt + 1)
                sp.dma_start(h_dram[P * tt:P * tt + P], tok_rows[:, tt % 2]).then_inc(rows_out[tt % 2], 16)
            sp.wait_ge(s["scattered"], 128)
            sp.dma_start(table, table_dram.rearrange("(p b) t -> p (b t)", p=P)).then_inc(s["loaded"], 16)
            sp.wait_ge(s["loaded"], 16)
            for out in rows_out:
                sp.wait_ge(out, 32)

        @block.tensor
        def _(pe):
            for tt in range(4):
                for kt in range(KD):
                    last = pe.matmul(k.bank[0][:, 36 * tt:36 * tt + 36], h[:, kt, P * tt:P * tt + P],
                                     w_router[:, kt], start=kt == 0, stop=kt == KD - 1)
            last.then_inc(s["logits"], 1)
            for tt in range(4):
                if tt:
                    pe.wait_ge(s["rows"], tt)
                for kt in range(KD):
                    last = pe.transpose(k.bank[2 + kt // 4][:, P * (kt % 4):P * (kt % 4) + P], h[:, kt, P * tt:P * tt + P],
                                        k.c("ident"))
                last.then_inc(s["turned"], 1)
            pe.wait_ge(s["rank_in"], 1)
            for tt in range(4):
                for t2 in range(tt + 1):
                    pe.matmul(k.bank[1][:, 32 * tt:32 * tt + 32], k.c("before") if t2 == tt else k.c("ones"), M[:, t2],
                              start=t2 == 0, stop=t2 == tt)
            for t2 in range(4):
                last = pe.matmul(k.bank[1][:, 128:160], k.c("ones"), M[:, t2], start=t2 == 0, stop=t2 == 3)
            last.then_inc(s["rank"], 1)

        @block.scalar
        def _(act):
            for tt in range(4):
                act.wait_ge(s["turned"], tt + 1)
                if tt >= 2:
                    act.wait_ge(rows_out[tt % 2], 16)
                act.activation(tok_rows[:, tt % 2, 0:512], k.bank[2][:, :], ACT.Copy)
                act.activation(tok_rows[:, tt % 2, 512:1024], k.bank[3][:, :], ACT.Copy).then_inc(s["rows"], 1)
            act.wait_ge(s["step"], route_steps["group_shifted"])
            act.activation(ex, ex, ACT.Exp).then_inc(s["exped"], 1)
            act.wait_ge(s["step"], route_steps["pair_shifted"])
            act.activation(top[1], top[1], ACT.Exp).then_inc(s["exped"], 1)

        @block.gpsimd
        def _(pool):
            pool.wait_ge(s["blank"], 16)
            pool.wait_ge(s["slots"], 1)
            for i in range(8):
                pool.indirect_dma_start(table_dram, bass.IndirectOffsetOnAxis(slot_i[:, i // 2, i % 2:i % 2 + 1].bitcast(U32), 0),
                                        ids[:, i], None).then_inc(s["scattered"], 16)

        @block.vector
        def _(dve):
            def step(ins):
                n_step[0] += 1
                ins.then_inc(s["step"], 1)
                dve.wait_ge(s["step"], n_step[0])

            def over(x, n):
                return x.broadcast_to([P, 4, n])

            def first_max(x, n, peak, one):
                step(dve.tensor_reduce(peak, x, AX, MAX))
                t = tie[:, :, 0:n]
                step(dve.tensor_tensor(t, x, over(peak, n), ALU.is_equal))
                ids_n = iota[:, 0:n].rearrange("p (a n) -> p a n", a=1).broadcast_to([P, 4, n])
                step(dve.scalar_tensor_tensor(out=t, in0=t, scalar=-100.0, in1=ids_n, op0=MUL, op1=ADD))
                step(dve.tensor_reduce(least, t, AX, ALU.min))
                step(dve.tensor_tensor(one, t, over(least, n), ALU.is_equal))

            dve.wait_ge(s["logits"], 1)
            b = k.v("router_b", 0, 36).rearrange("p (a n) -> p a n", a=1).broadcast_to([P, 4, 36])
            step(dve.tensor_tensor(L, k.bank[0][:, 0:144].rearrange("p (a n) -> p a n", a=4), b, ADD))
            first_max(L[:, :, 0:4], 4, gmax, one_g)
            step(dve.tensor_tensor(ex, L[:, :, 0:4], over(gmax, 4), SUB))
            assert route_steps["group_shifted"] == n_step[0], n_step[0]
            logits = L[:, :, 4:36].rearrange("p a (g e) -> p a g e", g=4)
            for tt in range(4):
                one = one_g[:, tt, :].rearrange("p (g e) -> p g e", e=1).broadcast_to([P, 4, 8])
                step(dve.tensor_tensor(part[:, tt], logits[:, tt], one, MUL))
            step(dve.tensor_tensor(picked, part[:, :, 0], part[:, :, 1], ADD))
            step(dve.tensor_tensor(masked, part[:, :, 2], part[:, :, 3], ADD))
            step(dve.tensor_tensor(picked, picked, masked, ADD))
            first_max(picked, 8, top[0], one_e[0])
            step(dve.scalar_tensor_tensor(out=masked, in0=one_e[0], scalar=NEG, in1=picked, op0=MUL, op1=ADD))
            first_max(masked, 8, top[1], one_e[1])
            step(dve.tensor_tensor(top[1], top[1], top[0], SUB))
            assert route_steps["pair_shifted"] == n_step[0], n_step[0]
            for i in range(2):
                for tt in range(4):
                    g = one_g[:, tt, :].rearrange("p (g e) -> p g e", e=1).broadcast_to([P, 4, 8])
                    e = one_e[i][:, tt, :].rearrange("p (g e) -> p g e", g=1).broadcast_to([P, 4, 8])
                    step(dve.tensor_tensor(X[i][:, tt].rearrange("p (g e) -> p g e", g=4), g, e, MUL))
            dve.tensor_tensor(M, X[0], X[1], ADD).then_inc(s["rank_in"], 1)
            dve.wait_ge(s["exped"], 2)
            step(dve.tensor_reduce(total, ex, AX, ADD))
            step(dve.reciprocal(pg, total))
            step(dve.tensor_scalar(total, top[1], 1.0, None, ADD))
            step(dve.reciprocal(total, total))
            step(dve.tensor_tensor(total, total, pg, MUL))
            step(dve.tensor_copy(weights[:, :, 0:1], total))
            step(dve.tensor_tensor(weights[:, :, 1:2], total, top[1], MUL))
            dve.wait_ge(s["rank"], 1)
            step(dve.tensor_copy(dest, k.bank[1][:, 0:128].rearrange("p (a n) -> p a n", a=4)))
            step(dve.tensor_copy(count, k.bank[1][:, 128:160]))
            step(dve.tensor_scalar(j_tile, dest, 128.0, None, ALU.is_ge))
            step(dve.tensor_scalar(extra, count, 128.0, None, ALU.is_gt))
            for t in (256.0, 384.0):
                step(dve.scalar_tensor_tensor(out=j_tile, in0=dest, scalar=t, in1=j_tile, op0=ALU.is_ge, op1=ADD))
                step(dve.scalar_tensor_tensor(out=extra, in0=count, scalar=t, in1=extra, op0=ALU.is_gt, op1=ADD))
            step(dve.tensor_tensor_scan(upto, k.c("ones", 0, 32), extra, 0.0, MUL, ADD))
            step(dve.scalar_tensor_tensor(out=dest, in0=j_tile, scalar=-128.0, in1=dest, op0=MUL, op1=ADD))
            step(dve.tensor_tensor(count, upto, extra, SUB))
            step(dve.scalar_tensor_tensor(out=count, in0=count, scalar=31.0, in1=iota, op0=ADD, op1=SUB))
            flat = count.rearrange("p (a n) -> p a n", a=1).broadcast_to([P, 4, 32])
            step(dve.tensor_tensor(tmp, j_tile, flat, ADD))
            step(dve.scalar_tensor_tensor(out=tmp, in0=j_tile, scalar=0.5, in1=tmp, op0=ALU.is_gt, op1=MUL))
            ids4 = iota.rearrange("p (a n) -> p a n", a=1).broadcast_to([P, 4, 32])
            step(dve.tensor_tensor(tmp, tmp, ids4, ADD))
            step(dve.scalar_tensor_tensor(out=dest, in0=dest, scalar=float(N_BLK), in1=tmp, op0=MUL, op1=ADD))
            for i in range(2):
                step(dve.tensor_tensor(tmp, X[i], dest, MUL))
                step(dve.tensor_reduce(slot_f[:, :, i:i + 1], tmp, AX, ADD))
            for i in range(OVER):
                step(dve.tensor_scalar(tmp[:, 0], upto, float(i), None, ALU.is_le))
                step(dve.tensor_reduce(k.over_f[:, i:i + 1], tmp[:, 0], AX, ADD))
            step(dve.tensor_copy(k.over_f[:, OVER:OVER + 1], upto[:, 31:32]))
            step(dve.tensor_copy(k.over_i, k.over_f))
            dve.tensor_copy(slot_i, slot_f).then_inc(s["slots"], 1)


route_steps = {"group_shifted": 7, "pair_shifted": 26}


def moe_stage(k, table, h_dram, y_dram, at):
    nc, d = k.nc, k.d

    def buf(n, *shape):
        at[0] += n
        return k.mem[:, at[0] - n:at[0]]
    gate_w = [buf(4096).rearrange("p (k n) -> p k n", k=KD) for _ in range(2)]
    up_w = [buf(4096).rearrange("p (k n) -> p k n", k=KD) for _ in range(2)]
    down_w = [buf(4096).rearrange("p (k n) -> p k n", k=4) for _ in range(2)]
    rows = [buf(D) for _ in range(2)]
    y = [buf(D) for _ in range(2)]
    x = buf(D).rearrange("p (k n) -> p k n", k=KD)
    act_g, hid, hid_t = buf(D_EXP), buf(D_EXP), buf(D_EXP).rearrange("p (k n) -> p k n", k=4)
    idx = [buf(2).bitcast(I32) for _ in range(2)]
    s = {n: k.sem("moe_" + n) for n in ("idx", "x_turned", "x", "gate_mm", "up_mm", "silu", "hid", "h_turned", "hid_t",
                                       "down_mm", "y")}
    gu_landed = [k.sem(f"moe_gate_up_landed_{i}") for i in range(2)]
    down_landed = [k.sem(f"moe_down_landed_{i}") for i in range(2)]
    gathered = [k.sem(f"moe_gathered_{i}") for i in range(2)]
    stored = [k.sem(f"moe_stored_{i}") for i in range(2)]
    n_ready = k.sem("moe_count_ready")
    turns = k.sem("moe_pool_turns")
    w_gate, w_up, w_down = d["w_gate"], d["w_upe"], d["w_downe"]
    one = lambda x, e: x[bass.ds(e, 1)].rearrange("a p n -> (a p) n")

    def send(sp, e, n, i, h, first):
        if not first:
            sp.wait_ge(s["up_mm"], n - 1)
        sp.dma_start(gate_w[h].rearrange("p k n -> p (k n)"), one(w_gate, e)).then_inc(gu_landed[h], 16)
        sp.dma_start(up_w[h].rearrange("p k n -> p (k n)"), one(w_up, e)).then_inc(gu_landed[h], 16)
        if not first:
            sp.wait_ge(s["down_mm"], n - 1)
        sp.dma_start(down_w[h].rearrange("p k n -> p (k n)"), one(w_down, e)).then_inc(down_landed[h], 16)

    def gather(pool, n, i, h, first):
        if not first:
            pool.wait_ge(stored[h], 16 * i)
            pool.wait_ge(s["x_turned"], n - 1)
        pool.sem_inc(turns, 1)
        pool.tensor_copy(idx[h].rearrange("p (a t) -> p a t", a=1), table[:, bass.ds(n, 1), :]).then_inc(s["idx"], 1)
        pool.wait_ge(s["idx"], n + 1)
        pool.sem_inc(turns, 1)
        pool.indirect_dma_start(rows[h], None, h_dram,
                                bass.IndirectOffsetOnAxis(idx[h][:, 1:2].bitcast(U32), 0)).then_inc(gathered[h], 16)

    def scatter(pool, n, i, h):
        pool.wait_ge(s["y"], n + 1)
        pool.sem_inc(turns, 1)
        pool.indirect_dma_start(y_dram, bass.IndirectOffsetOnAxis(idx[h][:, 0:1].bitcast(U32), 0), y[h], None,
                                bounds_check=N_PAIR - 1, oob_is_err=False).then_inc(stored[h], 16)

    def turn_x(pe, n, i, h, first):
        pe.wait_ge(gathered[h], 16 * (i + 1))
        if not first:
            pe.wait_ge(s["x"], n)
        for kt in range(KD):
            last = pe.transpose(k.bank[kt // 4][:, P * (kt % 4):P * (kt % 4) + P], rows[h][:, kt:D:KD], k.c("ident"))
        last.then_inc(s["x_turned"], 1)

    def gate_up(pe, n, i, h, first):
        pe.wait_ge(s["x"], n + 1)
        pe.wait_ge(gu_landed[h], 32 * (i + 1))
        if not first:
            pe.wait_ge(s["hid"], n)
        for kt in range(KD):
            last = pe.matmul(k.bank[2][:, :], x[:, kt], gate_w[h][:, kt], start=kt == 0, stop=kt == KD - 1)
        last.then_inc(s["gate_mm"], 1)
        for kt in range(KD):
            last = pe.matmul(k.bank[3][:, :], x[:, kt], up_w[h][:, kt], start=kt == 0, stop=kt == KD - 1)
        last.then_inc(s["up_mm"], 1)

    def turn_hidden(pe, n):
        pe.wait_ge(s["hid"], n + 1)
        for kt in range(4):
            last = pe.transpose(k.bank[4][:, P * kt:P * kt + P], hid[:, kt:D_EXP:4], k.c("ident"))
        last.then_inc(s["h_turned"], 1)

    def down(pe, n, i, h, first):
        pe.wait_ge(s["hid_t"], n + 1)
        pe.wait_ge(down_landed[h], 16 * (i + 1))
        if not first:
            pe.wait_ge(s["y"], n)
        for half in range(2):
            for kt in range(4):
                last = pe.matmul(k.bank[5 + half][:, :], hid_t[:, kt], down_w[h][:, kt, 512 * half:512 * half + 512],
                                 start=kt == 0, stop=kt == 3)
        last.then_inc(s["down_mm"], 1)

    def act_part(act, n, first):
        act.wait_ge(s["x_turned"], n + 1)
        if not first:
            act.wait_ge(s["up_mm"], n)
        act.activation(x[:, 0:4].rearrange("p k n -> p (k n)"), k.bank[0][:, :], ACT.Copy)
        act.activation(x[:, 4:8].rearrange("p k n -> p (k n)"), k.bank[1][:, :], ACT.Copy).then_inc(s["x"], 1)

    def act_silu(act, n, first):
        act.wait_ge(s["gate_mm"], n + 1)
        if not first:
            act.wait_ge(s["hid"], n)
        act.activation(act_g, k.bank[2][:, :], ACT.Silu).then_inc(s["silu"], 1)

    def dve_part(dve, n, i, h, first, first_half):
        dve.wait_ge(s["silu"], n + 1)
        dve.wait_ge(s["up_mm"], n + 1)
        if not first:
            dve.wait_ge(s["h_turned"], n)
        dve.tensor_tensor(hid, act_g, k.bank[3][:, :], MUL).then_inc(s["hid"], 1)
        dve.wait_ge(s["h_turned"], n + 1)
        if not first:
            dve.wait_ge(s["down_mm"], n)
        dve.tensor_copy(hid_t.rearrange("p k n -> p (k n)"), k.bank[4][:, :]).then_inc(s["hid_t"], 1)
        dve.wait_ge(s["down_mm"], n + 1)
        if not first_half:
            dve.wait_ge(stored[h], 16 * i)
        dve.tensor_copy(y[h][:, 0:512], k.bank[5][:, :])
        dve.tensor_copy(y[h][:, 512:1024], k.bank[6][:, :]).then_inc(s["y"], 1)

    def over_blocks(eng, run):
        eng.wait_ge(n_ready, 1)
        for o in range(OVER):
            count = eng.value_load(k.over_i[0:1, OVER:OVER + 1], min_val=0, max_val=OVER)
            with eng.If(count > o):
                run(o)

    LAST = N_EXP - 1
    with nc.Block("moe") as block:
        @block.sync
        def _(sp):
            send(sp, 0, 0, 0, 0, True)
            send(sp, 1, 1, 0, 1, True)
            with sp.Fori(1, N_EXP // 2) as i:
                for h in range(2):
                    send(sp, 2 * i + h, 2 * i + h, i, h, False)

            def over(o):
                n = N_EXP + o
                e = sp.value_load(k.over_i[0:1, o:o + 1], min_val=0, max_val=N_EXP - 1)
                send(sp, e, n, n // 2, n % 2, False)
            over_blocks(sp, over)

        @block.gpsimd
        def _(pool):
            pool.sem_inc(n_ready, 1)
            gather(pool, 0, 0, 0, True)
            gather(pool, 1, 0, 1, True)
            with pool.Fori(1, N_EXP // 2) as i:
                for h in range(2):
                    scatter(pool, 2 * i + h - 2, i - 1, h)
                    gather(pool, 2 * i + h, i, h, False)
            scatter(pool, LAST - 1, N_EXP // 2 - 1, 0)
            scatter(pool, LAST, N_EXP // 2 - 1, 1)

            def over(o):
                n = N_EXP + o
                gather(pool, n, n // 2, n % 2, False)
                scatter(pool, n, n // 2, n % 2)
            over_blocks(pool, over)
            pool.wait_ge(stored[0], 8 * N_EXP)
            pool.wait_ge(stored[1], 8 * N_EXP)
            for o in range(OVER):
                count = pool.value_load(k.over_i[0:1, OVER:OVER + 1], min_val=0, max_val=OVER)
                with pool.If(count > o):
                    pool.wait_ge(stored[o % 2], 8 * N_EXP + 16 * (o // 2 + 1))

        @block.tensor
        def _(pe):
            def block_of(n, i, h, first=False, more=True, i_next=None):
                gate_up(pe, n, i, h, first)
                if more:
                    turn_x(pe, n + 1, i_next, 1 - h, False)
                turn_hidden(pe, n)
                down(pe, n, i, h, first)
            turn_x(pe, 0, 0, 0, True)
            block_of(0, 0, 0, first=True, i_next=0)
            block_of(1, 0, 1, i_next=1)
            with pe.Fori(1, N_EXP // 2 - 1) as i:
                block_of(2 * i, i, 0, i_next=i)
                block_of(2 * i + 1, i, 1, i_next=i + 1)
            i = N_EXP // 2 - 1
            block_of(LAST - 1, i, 0, i_next=i)
            block_of(LAST, i, 1, more=False)

            def over(o):
                n = N_EXP + o
                turn_x(pe, n, n // 2, n % 2, False)
                block_of(n, n // 2, n % 2, more=False)
            over_blocks(pe, over)

        @block.scalar
        def _(act):
            act_part(act, 0, True)
            act_silu(act, 0, True)
            with act.Fori(1, N_EXP) as n:
                act_part(act, n, False)
                act_silu(act, n, False)

            def over(o):
                act_part(act, N_EXP + o, False)
                act_silu(act, N_EXP + o, False)
            over_blocks(act, over)

        @block.vector
        def _(dve):
            dve_part(dve, 0, 0, 0, True, True)
            dve_part(dve, 1, 0, 1, False, True)
            with dve.Fori(1, N_EXP // 2) as i:
                for h in range(2):
                    dve_part(dve, 2 * i + h, i, h, False, False)

            def over(o):
                n = N_EXP + o
                dve_part(dve, n, n // 2, n % 2, False, False)
            over_blocks(dve, over)


def combine_stage(k, y_dram, weights, x, gate, at):
    nc = k.nc
    yr = k.at(at, 8192).rearrange("p (t c w) -> p t c w", t=4, c=2)
    s = {n: k.sem("combine_" + n) for n in ("first", "both", "turned", "done")}
    landed = [k.sem(f"combine_landed_{tt}") for tt in range(4)]
    with nc.Block("combine") as block:
        @block.sync
        def _(sp):
            for tt in range(4):
                src = y_dram[2 * P * tt:2 * P * (tt + 1)].rearrange("(p c) w -> p (c w)", c=2)
                sp.dma_start(yr[:, tt].rearrange("p c w -> p (c w)"), src).then_inc(landed[tt], 16)

        @block.vector
        def _(dve):
            for tt in range(4):
                dve.wait_ge(landed[tt], 16)
                dve.tensor_scalar(yr[:, tt, 0], yr[:, tt, 0], weights[:, tt, 0:1], None, MUL).then_inc(s["first"], 1)
                dve.wait_ge(s["first"], tt + 1)
                dve.scalar_tensor_tensor(out=yr[:, tt, 0], in0=yr[:, tt, 1], scalar=weights[:, tt, 1:2], in1=yr[:, tt, 0],
                                         op0=MUL, op1=ADD).then_inc(s["both"], 1)
            for kt in range(KD):
                dve.wait_ge(s["turned"], kt + 1)
                dve.scalar_tensor_tensor(out=x[:, kt], in0=k.bank[kt % 4][:, :], scalar=gate(kt), in1=x[:, kt],
                                         op0=MUL, op1=ADD).then_inc(s["done"], 1)

        @block.tensor
        def _(pe):
            pe.wait_ge(s["both"], 4)
            for kt in range(KD):
                if kt >= 4:
                    pe.wait_ge(s["done"], kt - 3)
                for tt in range(4):
                    last = pe.transpose(k.bank[kt % 4][:, P * tt:P * tt + P], yr[:, tt, 0, P * kt:P * kt + P], k.c("ident"))
                last.then_inc(s["turned"], 1)


def block_two(k, src):
    nc, d = k.nc, k.d
    three = lambda at, n, w: k.at(at, n * w).rearrange("p (n w) -> p n w", n=n)
    k.retire()
    x = src[:, :, CTX:ALL]
    m2 = k.mod[1]
    hm = three(6144, KD, ALL)
    norm_stage(k, "norm_mix", src, hm, [(0, CTX, 0), (CTX, SEQ, 1)],
               gain=lambda i: [(m2[:, 8:16, 1 - i], k.v("norm_mix", 0, 8))],
               shift=lambda kt, i: m2[:, kt, 1 - i:2 - i], work=18432)
    q, kf, v_tok = three(12288, 4, SEQ), three(14336, 4, ALL), three(17408, 6, 512)
    upad, ga, gb = three(20480, 4, 542), three(22656, 8, SEQ), three(26752, 8, SEQ)
    conv, sig = three(30848, 4, SEQ), three(32896, 4, SEQ)
    in_proj2_stage(k, hm, q, kf, v_tok, upad, sig, ga, gb, conv)
    layer_norm_stage(k, conv, 34944)
    att = three(32896, 4, SEQ)
    attention_stage(k, q, kf, v_tok, att, 6144, 7936, 34944)
    mix = three(34944, 8, SEQ)
    x4 = three(6144, KD, SEQ)
    merge_stage(k, att, conv, ga, gb, mix)
    k.frees_later([k.number("w_o", g) for g in range(4)], "w_o_summed", 2)
    residual_stage(k, "w_o", 1, halves(k, "w_o"), mix, lambda m: m2[:, 16 + m, 0:1], x, x4)
    k.retire()
    h, x = three(0, KD, SEQ), x4
    w_router = three(4096, KD, 36)
    table = k.at(4384, 2 * N_BLK).bitcast(I32).rearrange("p (b t) -> p b t", t=2)
    k.blank = k.at(4464, 2 * N_BLK).bitcast(I32)
    ids = k.at(4544, 16).bitcast(I32).rearrange("p (i t) -> p i t", t=2)
    weights = k.at(4560, 8).rearrange("p (t c) -> p t c", t=4)
    k.over_f, k.over_i = k.at(4568, 8), k.at(4576, 8).bitcast(I32)
    h_dram = nc.dram_tensor("h_rows", [SEQ, D], F32, kind="Internal").ap()
    y_dram = nc.dram_tensor("y_rows", [N_PAIR, D], F32, kind="Internal").ap()
    table_dram = nc.dram_tensor("slot_table", [P * N_BLK, 2], I32, kind="Internal").ap()
    norm_stage(k, "norm_ffn", x, h, [(0, SEQ, 0)], gain=lambda i: [(m2[:, 32:40, 0], k.v("norm_ffn", 0, 8))],
               shift=lambda kt, i: m2[:, 24 + kt, 0:1], work=10240,
               loads=[(k.at(4096, 288), d["w_router"]), (k.blank, d["blank"]), (k.at(4544, 16).bitcast(I32), d["ids"])])
    route_stage(k, h, weights, table, h_dram, table_dram, w_router, ids, 10240)
    moe_stage(k, table, h_dram, y_dram, [k.free_at + 10240])
    combine_stage(k, y_dram, weights, x, lambda m: m2[:, 40 + m, 0:1], 10240)
    out = three(0, KD, SEQ)
    norm_stage(k, "final2", x, out, [(0, SEQ, 0)], gain=lambda i: [(k.v("final_norm", 0, 8), None)], shift=None, work=10240)
    return out


def order_of_use(k):
    for g in range(8):
        k.put("ada1", g)
    order = [*range(8, 16), *range(4, 8), 16, 17, 18, *range(4)]
    for i, m in enumerate(order):
        k.put("w_in", m)
        if i < 16:
            k.put("ada1", 8 + i)
    for g in range(4):
        k.put("w_out", g)
    for m in range(KF):
        k.put("w_up", m)
    for m in range(KD):
        k.put("w_down", 2 * m)
        k.put("ada2", 3 * m)
        k.put("w_down", 2 * m + 1)
        k.put("ada2", 3 * m + 1)
        k.put("ada2", 3 * m + 2)
    for name, n in (("w_in2_q", 4), ("w_in2_v", 2), ("w_in2_g", 12)):
        for g in range(n):
            k.put(name, g)
    for g in range(2):
        k.put("w_att", g)
        k.put("w_conv", g)
    for g in range(4):
        k.put("w_o", g)


def build(nc, d, out, only_first=False):
    k = Core(nc, d, out)
    order_of_use(k)
    load_stage(k)
    x = block_one(k)
    if not only_first:
        x = block_two(k, x)
    stored = k.sem("result_stored")
    with nc.Block("store") as block:
        @block.sync
        def _(sp):
            sp.dma_start(out, x).then_inc(stored, 16)
            sp.wait_ge(stored, 16)


def kernel(**inputs):
    import concourse.bacc as bacc
    from concourse.bass_utils import run_bass_kernel_spmd

    nc = bacc.Bacc("TRN2", target_bir_lowering=False, num_devices=1)
    arrays = lay_out(inputs)
    d = {name: nc.dram_tensor(f"in_{name}", a.shape, mybir.dt.from_np(a.dtype), kind="ExternalInput").ap() for name, a in arrays.items()}
    out = nc.dram_tensor("out", [P, KD, SEQ], F32, kind="ExternalOutput").ap()
    build(nc, d, out)
    r = run_bass_kernel_spmd(nc, [{f"in_{name}": a for name, a in arrays.items()}], core_ids=[0])
    got = r.results[0]["out"]
    return np.ascontiguousarray(got.transpose(2, 1, 0)).reshape(1, SEQ, D)
```

```python
import numpy as np

import concourse.bass as bass
import concourse.mybir as mybir
from concourse.alu_op_type import AluOpType as ALU

ACT = mybir.ActivationFunctionType
F32 = mybir.dt.float32
I32 = mybir.dt.int32
U32 = mybir.dt.uint32
AX = mybir.AxisListType.X
ADD, SUB, MUL, MAX = ALU.add, ALU.subtract, ALU.mult, ALU.max

P = 128
D, KD = 1024, 8
SEQ, CTX = 512, 256
ALL = CTX + SEQ
GRID_W, ROWS = 64, SEQ // 64
CH, KC = 512, 4
HEAD = 64
CHUNK = 64
N_CTX, N_CHUNK = CTX // CHUNK, ALL // CHUNK
D_FF = 2816
KF = D_FF // P
N_EXP, N_GRP, PER_GRP, D_EXP = 32, 4, 8, 512
N_PAIR = SEQ * 2
OVER = 7
N_BLK = N_EXP + OVER
DECAY_SCALE = -float(np.exp(-0.5))
NEG = -1e30
MOD_BESIDE = [range(0, 3), range(3, 6), range(6, 10), range(10, 14), range(14, 18), range(18, 21), range(21, 24), ()]
RING, SLOT = 4, 2048


def columns(fields):
    at, out = 0, {}
    for name, n in fields:
        out[name] = at
        at += n
    return out, at


FIELDS = [
    ("norm1_g", 8), ("norm2_g", 8), ("final_g", 8), ("ada_b", 48), ("conv_w", 36), ("w0", 8), ("a0", 8),
    ("k_k", 4), ("k_a", 4), ("r_k", 4), ("gn_g", 4), ("gn_b", 4), ("fourier_g", 4),
    ("ffn_conv_w", 9 * 2 * KF), ("ffn_conv_b", 2 * KF),
    ("b_mod", 48), ("norm_mix", 8), ("norm_ffn", 8), ("final_norm", 8),
    ("conv2_w", 31 * 4), ("conv2_b", 4), ("ln_g", 4), ("ln_b", 4), ("router_b", 36),
    ("eps_norm", 1), ("eps_gn", 1), ("eps_kk", 1), ("zero", 1), ("cc1", 16), ("cc2", 16),
]
COL, N_COL = columns(FIELDS)
CONSTS = [("ident", 128), ("ones", 128), ("head_ones", 128), ("causal", 2 * 128), ("level", 6 * 64),
          ("chunk_start", ALL), ("before", 128), ("pair_mask", 64), ("pair_neg", 64),
          ("expert_id", 32), ("pick", 31)]
CAT, N_CONST = columns(CONSTS)


def tiled(w, cols):
    k, m = w.shape
    return np.ascontiguousarray(w.reshape(k // P, P, m // cols, cols).transpose(2, 1, 0, 3)).reshape(m // cols, P, -1)


def feature_major(x):
    t, f = x.shape
    return np.ascontiguousarray(x.reshape(t, f // P, P).transpose(2, 1, 0))


def per_partition(v):
    v = np.asarray(v)
    return np.moveaxis(v.reshape(v.shape[:-1] + (v.shape[-1] // P, P)), -1, 0).reshape(P, -1)


def shape_constants():
    c = np.zeros((P, N_CONST), np.float32)
    p = np.arange(P)
    c[:, CAT["ident"]:][:, :128] = np.eye(P)
    c[:, CAT["ones"]:][:, :128] = 1
    c[:, CAT["head_ones"]:][:, :128] = p[:, None] // HEAD == p[None] // HEAD
    s, t = p[:, None] % CHUNK, np.arange(CHUNK)[None]
    causal = np.stack([s < t, s <= t, s > t, s >= t], 1).astype(np.float32)
    c[:, CAT["causal"]:][:, :256] = causal.reshape(P, 256)
    for lv in range(6):
        inner, outer = 1 << lv, 2 << lv
        c[:, CAT["level"] + 64 * lv:][:, :64] = (s // outer == t // outer) & (s // inner != t // inner)
    c[:, CAT["chunk_start"]:][:, :ALL] = (np.arange(ALL) % CHUNK != 0)[None]
    c[:, CAT["before"]:][:, :128] = p[:, None] < p[None]
    start = np.clip(t * 0 + p[:, None] % 64 - 8, 0, GRID_W - 16)
    inside = (t >= start) & (t < start + 16)
    c[:, CAT["pair_mask"]:][:, :64] = inside[:, ::-1]
    c[:, CAT["pair_neg"]:][:, :64] = np.where(inside, 0, NEG)[:, ::-1]
    c[:, CAT["expert_id"]:][:, :32] = np.arange(32)[None]
    c[:, CAT["pick"] + 15] = 1
    return c


def blank_table():
    t = np.zeros((P, N_BLK, 2), np.int32)
    t[:, :, 0] = N_PAIR + np.arange(P * N_BLK).reshape(P, N_BLK)
    return t.reshape(P, -1)


def row_ids():
    p, i = np.arange(P)[:, None], np.arange(8)[None]
    tok = p + P * (i // 2)
    return np.stack([2 * tok + i % 2, tok], 2).astype(np.int32).reshape(P, 16)


def fourier_constants():
    t = np.arange(SEQ)
    ang = 2 * np.pi * (np.outer(t, t) % SEQ) / SEQ
    seq = np.stack([np.cos(ang), -np.sin(ang)]) / np.sqrt(SEQ)
    j = np.arange(64)
    a64 = 2 * np.pi * (np.outer(j, j) % 64) / 64
    chan = np.zeros((P, 2, P))
    for g in range(2):
        chan[64 * g:64 * g + 64, 0, 64 * g:64 * g + 64] = np.cos(a64) / 8
        chan[64 * g:64 * g + 64, 1, 64 * g:64 * g + 64] = np.sin(a64) / 8
    seq = seq.reshape(2, 4, P, SEQ).transpose(0, 2, 1, 3)
    return np.ascontiguousarray(seq.reshape(2, P, 4 * SEQ), np.float32), np.ascontiguousarray(chan.reshape(P, 256), np.float32)


def lay_out(i):
    one = {k: np.asarray(v) for k, v in i.items()}
    vec = np.zeros((P, N_COL), np.float32)

    def put(name, a):
        vec[:a.shape[0], COL[name]:COL[name] + a.shape[1]] = a

    for name in ("norm1_g", "norm2_g", "ada_b", "k_k", "k_a", "gn_g", "gn_b", "fourier_g", "ffn_conv_b"):
        put(name, per_partition(one[name][0]))
    put("final_g", per_partition(one["final_g"]))
    put("conv_w", per_partition(one["rwkv_conv_w"][0]))
    put("w0", per_partition(one["decay_w0"][0]))
    put("a0", per_partition(one["iclr_a0"][0]))
    put("r_k", per_partition(one["r_k"][0].reshape(-1)))
    put("ffn_conv_w", per_partition(one["ffn_conv_w"][0].reshape(9, -1)))
    put("b_mod", per_partition(one["b_mod_2"][0]))
    put("norm_mix", per_partition(one["norm_mix_2"][0]))
    put("norm_ffn", per_partition(one["norm_ffn_2"][0]))
    put("final_norm", per_partition(one["final_norm_2"]))
    put("conv2_w", per_partition(one["conv_w_2"][0]))
    put("conv2_b", per_partition(one["conv_b_2"][0]))
    put("ln_g", per_partition(one["conv_ln_g_2"][0]))
    put("ln_b", per_partition(one["conv_ln_b_2"][0]))
    bias = np.concatenate([one["b_router_group_2"][0], one["b_router_expert_2"][0]])
    put("router_b", np.broadcast_to(bias[None], (P, 36)))
    for name, v in (("eps_norm", 1e-6), ("eps_gn", 64e-5), ("eps_kk", 1e-12)):
        vec[:, COL[name]] = v
    for name, a, b in (("cc1", "c", "c_ctx"), ("cc2", "c_2", "c_ctx_2")):
        both = np.stack([one[a][0], one[b]])
        put(name, both.reshape(2, KD, P).transpose(2, 1, 0).reshape(P, 16))

    w_in, w_in2 = one["w_in"][0], one["w_in_2"][0]
    seq_dft, chan_dft = fourier_constants()
    x0 = np.concatenate([one["ctx"][0], one["x"][0]])
    w_up = one["ffn_w_up"][0]
    up = np.stack([w_up[:, :D_FF].reshape(D, KF, P), w_up[:, D_FF:].reshape(D, KF, P)], 2)
    return {
        "vec": vec, "const": shape_constants(), "seq_dft": seq_dft, "chan_dft": chan_dft,
        "x0": feature_major(x0), "ctx2": feature_major(one["ctx_2"][0]),
        "ada1": tiled(one["ada_w"][0], 256), "ada2": tiled(one["w_mod_2"][0], 256),
        "w_in": tiled(w_in, 128), "w_out": tiled(one["w_out"][0], 256),
        "lora": np.concatenate([one["decay_w2"][0].reshape(P, CH), one["iclr_a2"][0].reshape(P, CH)], 1),
        "gate_g2": np.ascontiguousarray(one["gate_g2"][0]),
        "w_up": tiled(np.ascontiguousarray(up.reshape(D, 2 * D_FF)), 256),
        "w_down": np.ascontiguousarray(one["ffn_w_down"][0].reshape(2, 11, P, 8, P).transpose(3, 0, 2, 1, 4)).reshape(16, P, 11 * P),
        "w_in2_q": tiled(w_in2[:, :1024], 256),
        "w_in2_v": tiled(w_in2[:, 1024:1536], 256),
        "w_in2_g": tiled(w_in2[:, 1536:], 256),
        "rpb": np.pad(one["rpb_2"][0][:, :, ::-1].reshape(-1), 64),
        "w_att": tiled(one["w_att_out_2"][0], 512), "w_conv": tiled(one["w_conv_out_2"][0], 512),
        "w_o": tiled(one["w_o_2"][0], 256),
        "w_router": tiled(np.concatenate([one["w_router_group_2"][0], one["w_router_expert_2"][0]], 1), 36)[0],
        "blank": blank_table(), "ids": row_ids(),
        "w_gate": one["w_exp_gate_2"][0].reshape(N_EXP, P, KD * D_EXP),
        "w_upe": one["w_exp_up_2"][0].reshape(N_EXP, P, KD * D_EXP),
        "w_downe": one["w_exp_down_2"][0].reshape(N_EXP, P, 4 * D),
    }


class Core:

    def __init__(self, nc, d, out):
        self.nc, self.d, self.out = nc, d, out
        self.mem = nc.alloc_sbuf_tensor("mem", [P, 53100], F32)
        self.bank = [nc.alloc_psum_tensor(f"bank{i}", [P, 512], F32) for i in range(8)]
        self.vec = self.mem[:, 0:N_COL]
        self.const = self.mem[:, N_COL:N_COL + N_CONST]
        at = N_COL + N_CONST
        self.mod = [self.mem[:, at + 96 * b:at + 96 * b + 96].rearrange("p (m t) -> p m t", t=2) for b in range(2)]
        at += 192
        self.small = self.mem[:, at:at + 64]
        at += 64
        self.silu = [self.mem[:, at + 16 * b:at + 16 * b + 16] for b in range(2)]
        at += 32
        self.ring_at = at
        at += RING * SLOT
        self.decay_at = at
        at += 96
        self.free_at = at
        self.w_loaded = [nc.alloc_semaphore(f"weights_loaded_{i}") for i in range(RING)]
        self.freed = {}
        self.stream = []
        self.place = {}
        self.sent = 0
        self.named = {}
        self.live = []

    def sem(self, name):
        s = self.named.pop(name, None) or self.nc.alloc_semaphore(name)
        self.live.append(s)
        return s

    def retire(self):
        self.nc.clear_and_free_semaphores(self.live)
        self.nc.all_engine_barrier()
        self.live = []
        self.freed = {g: [] for g in self.freed}

    def v(self, name, i=0, n=1):
        return self.vec[:, COL[name] + i:COL[name] + i + n]

    def c(self, name, i=0, n=128):
        return self.const[:, CAT[name] + i:CAT[name] + i + n]

    def at(self, words, n):
        assert self.free_at + words + n <= 53100, (self.free_at + words + n)
        return self.mem[:, self.free_at + words:self.free_at + words + n]

    def slot(self, g, n=SLOT):
        a = self.ring_at + (g % RING) * SLOT
        return self.mem[:, a:a + n]

    def weights_ready(self, pe, g):
        pe.wait_ge(self.w_loaded[g % RING], 16 * (g // RING + 1))

    def put(self, name, tile):
        self.place[name, tile] = len(self.stream)
        self.stream.append(self.d[name][tile])

    def number(self, name, tile):
        return self.place[name, tile]

    def frees(self, numbers, sem, per=1):
        for i, g in enumerate(numbers):
            self.freed[g] = [(sem, per * (i + 1))]

    def frees_later(self, numbers, name, per):
        self.named[name] = self.nc.alloc_semaphore(name)
        self.frees(numbers, self.named[name], per)

    def send_weights(self, sp, upto=None):
        while self.sent < (len(self.stream) if upto is None else upto):
            g = self.sent
            if g >= RING:
                if g - RING not in self.freed:
                    break
                for sem, value in self.freed[g - RING]:
                    sp.wait_ge(sem, value)
            src = self.stream[g]
            sp.dma_start(self.slot(g, src.shape[1]), src).then_inc(self.w_loaded[g % RING], 16)
            self.sent += 1


def load_stage(k):
    nc, landed = k.nc, k.sem("parameters_landed")
    with nc.Block("load") as block:
        @block.sync
        def _(sp):
            sp.dma_start(k.vec, k.d["vec"]).then_inc(landed, 16)
            sp.dma_start(k.const, k.d["const"]).then_inc(landed, 16)
            k.send_weights(sp)
            sp.wait_ge(landed, 32)


def mod_slot(k, dve, name, g, silu, acc, t, step, count):
    n = k.number(name, g)
    dve.wait_ge(k.w_loaded[n % RING], 16 * (n // RING + 1))
    w = k.slot(n).rearrange("p (k m) -> p k m", k=KD)
    for kt in range(KD):
        c = silu[:, 2 * kt + t:2 * kt + t + 1]
        if kt == 0:
            ins = dve.tensor_scalar(acc, w[:, kt], c, None, MUL)
        else:
            dve.wait_ge(step[0], step[1])
            ins = dve.scalar_tensor_tensor(out=acc, in0=w[:, kt], scalar=c, in1=acc, op0=MUL, op1=ADD)
        if kt < KD - 1:
            step[1] += 1
            ins.then_inc(step[0], 1)
        else:
            ins.then_inc(count, 1)


def mod_slot_by_product(k, pool, name, g, silu, acc, tmp, t, step, count):
    n = k.number(name, g)
    pool.wait_ge(k.w_loaded[n % RING], 16 * (n // RING + 1))
    if step[1]:
        pool.wait_ge(count, step[1] // 3)
    w = k.slot(n).rearrange("p (k m) -> p k m", k=KD)
    tmp = tmp.rearrange("p (k m) -> p k m", k=KD)
    c = silu[:, t:2 * KD:2].rearrange("p (k m) -> p k m", m=1).broadcast_to([P, KD, 256])
    pool.tensor_tensor(tmp, w, c, MUL).then_inc(step[0], 1)
    for half in (4, 2, 1):
        step[1] += 1
        pool.wait_ge(step[0], step[1])
        if half > 1:
            pool.tensor_tensor(tmp[:, 0:half], tmp[:, 0:half], tmp[:, half:2 * half], ADD).then_inc(step[0], 1)
        else:
            pool.tensor_tensor(acc, tmp[:, 0], tmp[:, 1], ADD).then_inc(count, 1)


def mod_contract(k, pe, bank, pieces):
    for j, x in enumerate(pieces):
        last = pe.matmul(bank[0:16, :], k.c("pick", 15 - j, 16), x, start=j == 0, stop=j == len(pieces) - 1)
    return last


def mod_turn(k, pe, bank, rows):
    for q in range(4):
        last = pe.matmul(bank[:, 16 * q:16 * q + 16], rows[0:16, P * q:P * q + P], k.c("ident", 0, 16)[0:16],
                         start=True, stop=True)
    return last


def mod_add_bias(k, dve, bank, b, m0, t, j0, n, added, value):
    four = lambda x: x.rearrange("p (j q) -> p j q", q=4)
    mod = k.mod[b][:, :, t]
    sums = bank[:, 0:64].rearrange("p (q j) -> p j q", q=4)[:, j0:j0 + n]
    bias = k.v(("ada_b", "b_mod")[b], m0, 4 * n)
    dve.tensor_tensor(four(mod[:, m0:m0 + 4 * n]), sums, four(bias), ADD).then_inc(added, 1)
    dve.wait_ge(added, value + 1)
    value += 1
    for a in (8, 32):
        if m0 <= a < m0 + 4 * n:
            dve.tensor_scalar(mod[:, a:a + 8], mod[:, a:a + 8], 1.0, None, ADD).then_inc(added, 1)
            value += 1
    return value


def cut(x, n=512):
    return [x[:, i:i + n] for i in range(0, x.shape[1], n)]


def mod_first_stage(k, x_load):
    nc = k.nc
    silu_done, summed, rows_ready, turned, added = (k.sem("mod_" + n) for n in ("silu", "summed", "rows", "turned", "added"))
    acc = [k.at(2048 * t, 2048) for t in range(2)]
    tmp, rows = k.at(12288, 2048), k.at(14336, 512)
    dve_acc, pool_acc = k.sem("mod_dve_acc"), k.sem("mod_pool_acc")
    dve_step, pool_step = [k.sem("mod_dve_step"), 0], [k.sem("mod_pool_step"), 0]
    dve_jobs = [(g, t) for g in range(8) for t in range(2) if t == 0 or g % 2]
    pool_jobs = [(g, 1) for g in range(0, 8, 2)]
    for g in range(8):
        k.freed[k.number("ada1", g)] = [(dve_acc, 1 + max(i for i, j in enumerate(dve_jobs) if j[0] == g))] + (
            [(pool_acc, pool_jobs.index((g, 1)) + 1)] if g % 2 == 0 else [])
    with nc.Block("mod_first") as block:
        @block.sync
        def _(sp):
            k.send_weights(sp, 8)
            sp.dma_start(*x_load[:2]).then_inc(x_load[2], 16)
            k.send_weights(sp)

        @block.scalar
        def _(act):
            act.activation(k.silu[0], k.v("cc1", 0, 16), ACT.Silu).then_inc(silu_done, 1)
            act.activation(k.silu[1], k.v("cc2", 0, 16), ACT.Silu).then_inc(silu_done, 1)
            act.wait_ge(summed, 1)
            act.activation(rows[0:16], k.bank[0][0:16, :], ACT.Copy).then_inc(rows_ready, 1)

        @block.gpsimd
        def _(pool):
            pool.wait_ge(silu_done, 2)
            for g, t in pool_jobs:
                mod_slot_by_product(k, pool, "ada1", g, k.silu[0], acc[t][:, 256 * g:256 * g + 256], tmp, t, pool_step, pool_acc)

        @block.tensor
        def _(pe):
            for i in range(4):
                pe.wait_ge(dve_acc, dve_jobs.index((2 * i + 1, 1)) + 1)
                pe.wait_ge(pool_acc, pool_jobs.index((2 * i, 1)) + 1)
                for t in range(2):
                    last = pe.matmul(k.bank[0][0:16, :], k.c("pick", 15 - (4 * t + i), 16), acc[t][:, 512 * i:512 * i + 512],
                                     start=(i, t) == (0, 0), stop=(i, t) == (3, 1))
            last.then_inc(summed, 1)
            pe.wait_ge(rows_ready, 1)
            mod_turn(k, pe, k.bank[1], rows).then_inc(turned, 1)

        @block.vector
        def _(dve):
            dve.wait_ge(silu_done, 2)
            for g, t in dve_jobs:
                mod_slot(k, dve, "ada1", g, k.silu[0], acc[t][:, 256 * g:256 * g + 256], t, dve_step, dve_acc)
            dve.wait_ge(turned, 1)
            value = mod_add_bias(k, dve, k.bank[1], 0, 0, 0, 0, 4, added, 0)
            mod_add_bias(k, dve, k.bank[1], 0, 0, 1, 4, 4, added, value)


def norm_stage(k, name, src, dst, parts, gain, shift, work, tiles=KD, first=None, loads=None, mod2=None, experts=None):
    nc = k.nc
    landed = k.sem(name + "_landed") if loads else None
    if mod2:
        pieces, rows = mod2
        mod_summed, mod_rows, mod_turned, mod_added = (k.sem("mod2_" + n) for n in ("summed", "rows", "turned", "added"))
    width = parts[-1][0] + parts[-1][1]
    squares = k.at(work, 2 * width).rearrange("p (n w) -> p n w", n=2)
    rstd = k.at(work + 2 * width, width)
    gains = k.small[:, 0:2 * tiles].rearrange("p (k n) -> p k n", n=2)
    sq, used, rt, rs, scaled, gained, shifted = (k.sem(f"{name}_{s}") for s in (
        "square_ready", "square_used", "root_ready", "rstd_ready", "scaled", "gain_ready", "shifted"))
    with nc.Block(name) as block:
        @block.sync
        def _(sp):
            for to, src_dram in loads or ():
                sp.dma_start(to, src_dram).then_inc(landed, 16)
            k.send_weights(sp)
            if experts:
                experts.send_gate_up(sp, 0, 0)
                experts.send_down(sp, 0, 0)
            if loads:
                sp.wait_ge(landed, 16 * len(loads))

        @block.scalar
        def _(act):
            if first is not None:
                act.wait_ge(*first)
            for kt in range(tiles):
                if kt >= 2:
                    act.wait_ge(used, kt - 1)
                act.activation(squares[:, kt % 2], src[:, kt], ACT.Square).then_inc(sq, 1)
            act.wait_ge(used, tiles)
            for a, n, b in parts:
                act.activation(rstd[:, a:a + n], k.bank[b][:, 0:n], ACT.Sqrt, bias=k.v("eps_norm"),
                               scale=1.0 / (tiles * P)).then_inc(rt, 1)
            if mod2:
                act.wait_ge(mod_summed, 1)
                act.activation(rows[0:16], k.bank[2][0:16, :], ACT.Copy).then_inc(mod_rows, 1)
            if shift:
                for kt in range(tiles):
                    for i, (a, n, b) in enumerate(parts):
                        act.wait_ge(scaled, kt * len(parts) + i + 1)
                        act.activation(dst[:, kt, a:a + n], dst[:, kt, a:a + n], ACT.Identity,
                                       bias=shift(kt, i)).then_inc(shifted, 1)

        @block.tensor
        def _(pe):
            for kt in range(tiles):
                pe.wait_ge(sq, kt + 1)
                for a, n, b in parts:
                    last = pe.matmul(k.bank[b][:, 0:n], k.c("ones"), squares[:, kt % 2, a:a + n],
                                     start=kt == 0, stop=kt == tiles - 1)
                last.then_inc(used, 1)
            if mod2:
                mod_contract(k, pe, k.bank[2], pieces).then_inc(mod_summed, 1)
                pe.wait_ge(mod_rows, 1)
                mod_turn(k, pe, k.bank[3], rows).then_inc(mod_turned, 1)

        @block.vector
        def _(dve):
            for i in range(len(parts)):
                for a, b in gain(i):
                    if b is None:
                        dve.tensor_copy(gains[:, :, i], a).then_inc(gained, 1)
                    else:
                        dve.tensor_tensor(gains[:, :, i], a, b, MUL).then_inc(gained, 1)
            if first is not None:
                dve.wait_ge(*first)
            dve.wait_ge(rt, len(parts))
            dve.reciprocal(rstd, rstd).then_inc(rs, 1)
            dve.wait_ge(rs, 1)
            dve.wait_ge(gained, len(parts))
            for kt in range(tiles):
                for i, (a, n, b) in enumerate(parts):
                    dve.scalar_tensor_tensor(out=dst[:, kt, a:a + n], in0=src[:, kt, a:a + n], scalar=gains[:, kt, i:i + 1],
                                             in1=rstd[:, a:a + n], op0=MUL, op1=MUL).then_inc(scaled, 1)
            if mod2:
                dve.wait_ge(mod_turned, 1)
                value = mod_add_bias(k, dve, k.bank[3], 1, 0, 0, 0, 12, mod_added, 0)
                mod_add_bias(k, dve, k.bank[3], 1, 0, 1, 12, 4, mod_added, value)


def in_proj_stage(k, h, u, pad_rkv, convs, acc):
    nc = k.nc
    order = [*range(8, 16), *range(4, 8), 16, 17, 18, *range(4)]
    summed, copied, padded = k.sem("in_proj_summed"), k.sem("in_proj_copied"), k.sem("in_proj_padded")
    tap0, tap1, conv = k.sem("conv_tap0"), k.sem("conv_tap1"), k.sem("conv_tap2")
    mod_acc, mod_step = k.sem("mod_acc"), [k.sem("mod_step"), 0]
    mod_summed, mod_rows, mod_turned, mod_added = (k.sem("mod1_" + n) for n in ("summed", "rows", "turned", "added"))
    rows = acc[:, 4096:4608]
    k.frees([k.number("w_in", m) for m in order], summed)
    k.frees([k.number("ada1", g) for g in range(8, 24)], mod_acc)
    with nc.Block("in_proj") as block:
        @block.sync
        def _(sp):
            k.send_weights(sp, k.number("w_out", 0))

        @block.gpsimd
        def _(pool):
            for view in pad_rkv:
                pool.memset(view, 0.0).then_inc(padded, 1)

        @block.tensor
        def _(pe):
            for i, m in enumerate(order):
                g = k.number("w_in", m)
                k.weights_ready(pe, g)
                w = k.slot(g, 1024).rearrange("p (k m) -> p k m", k=KD)
                if i >= 3:
                    pe.wait_ge(copied, i - 2)
                for n0, n1, b in ((CTX, ALL, 2 * (i % 3)), (0, CTX, 2 * (i % 3) + 1)):
                    if n0 == 0 and not u[m][1]:
                        continue
                    for kt in range(KD):
                        last = pe.matmul(k.bank[b][:, 0:n1 - n0], w[:, kt], h[:, kt, n0:n1],
                                         start=kt == 0, stop=kt == KD - 1)
                last.then_inc(summed, 1)
            pe.wait_ge(mod_acc, 16)
            pe.wait_ge(copied, 19)
            mod_contract(k, pe, k.bank[0], cut(acc[:, 0:4096])).then_inc(mod_summed, 1)
            pe.wait_ge(mod_rows, 1)
            mod_turn(k, pe, k.bank[6], rows).then_inc(mod_turned, 1)

        @block.scalar
        def _(act):
            n = 0
            for i, m in enumerate(order):
                act.wait_ge(summed, i + 1)
                lat, ctx = u[m]
                for dst, f in lat:
                    ins = act.activation(dst, k.bank[2 * (i % 3)][:, 0:SEQ], f)
                if ctx:
                    for dst, f in ctx:
                        ins = act.activation(dst, k.bank[2 * (i % 3) + 1][:, 0:CTX], f)
                ins.then_inc(copied, 1)
                if m in convs:
                    act.wait_ge(copied, i + 1)
                    act.wait_ge(padded, len(pad_rkv))
                    for src, dst, w in convs[m]:
                        act.activation(dst, src[:, 0:dst.shape[1]], ACT.Identity, scale=k.v("conv_w", w)).then_inc(tap0, 1)
            act.wait_ge(mod_summed, 1)
            act.activation(rows[0:16], k.bank[0][0:16, :], ACT.Copy).then_inc(mod_rows, 1)

        @block.vector
        def _(dve):
            n = 0
            for i, m in enumerate(order):
                if i < 16:
                    mod_slot(k, dve, "ada1", 8 + i, k.silu[0], acc[:, 256 * i:256 * i + 256], 0, mod_step, mod_acc)
                for src, dst, w in convs.get(m, ()):
                    n += 1
                    size = dst.shape[1]
                    dve.wait_ge(tap0, n)
                    dve.scalar_tensor_tensor(out=dst, in0=src[:, 1:size + 1], scalar=k.v("conv_w", 12 + w), in1=dst,
                                             op0=MUL, op1=ADD).then_inc(tap1, 1)
                    dve.wait_ge(tap1, n)
                    dve.scalar_tensor_tensor(out=dst, in0=src[:, 2:size + 2], scalar=k.v("conv_w", 24 + w), in1=dst,
                                             op0=MUL, op1=ADD).then_inc(conv, 1)
            dve.wait_ge(mod_turned, 1)
            mod_add_bias(k, dve, k.bank[6], 0, 16, 0, 0, 8, mod_added, 0)


def key_stage(k, kf, kk_out, wd, ad, lora, sig, a, scratch, store, lora_load):
    nc = k.nc
    sq, summed, rt, rs, kraw, kk, stored, landed = (k.sem("key_" + s) for s in (
        "square", "summed", "root", "rstd", "kraw", "kk_ready", "fourier_stored", "lora_landed"))
    squares = k.at(scratch, 2 * ALL).rearrange("p (n w) -> p n w", n=2)
    rstd = k.at(scratch + 2 * ALL, 4 * ALL).rearrange("p (n w) -> p n w", n=4)
    lora_summed, lora_done = k.sem("lora_summed"), k.sem("lora_done")
    lora_units = [(src, w0, dst, name, d, ct) for src, w0, dst, name in ((wd, 0, sig, "w0"), (ad, CH, a, "a0"))
                  for d in range(2) for ct in range(KC)]
    with nc.Block("keys") as block:
        @block.sync
        def _(sp):
            sp.dma_start(*store).then_inc(stored, 16)
            sp.dma_start(*lora_load).then_inc(landed, 16)
            sp.wait_ge(stored, 16)
            sp.wait_ge(landed, 16)

        @block.scalar
        def _(act):
            for ct in range(KC):
                act.wait_ge(kraw, ct + 1)
                if ct >= 2:
                    act.wait_ge(summed, ct - 1)
                act.activation(squares[:, ct % 2], kk_out[:, ct], ACT.Square).then_inc(sq, 1)
            for ct in range(KC):
                act.wait_ge(summed, ct + 1)
                for a, n, b in ((0, CTX, 0), (CTX, SEQ, 1)):
                    ins = act.activation(rstd[:, ct, a:a + n], k.bank[2 * (ct % 3) + b][:, 0:n], ACT.Sqrt,
                                         bias=k.v("eps_kk"))
                ins.then_inc(rt, 1)
            for u, (_, _, dst, name, d, ct) in enumerate(lora_units):
                act.wait_ge(lora_summed, u + 1)
                for x, n, b in ((0, CTX, 0), (CTX, SEQ, 1)):
                    ins = act.activation(dst[:, d, ct, x:x + n], k.bank[2 * (u % 4) + b][:, 0:n], ACT.Sigmoid,
                                         bias=k.v(name, 4 * d + ct))
                ins.then_inc(lora_done, 1)

        @block.vector
        def _(dve):
            for ct in range(KC):
                dve.tensor_scalar(kk_out[:, ct], kf[:, ct], k.v("k_k", ct), None, MUL).then_inc(kraw, 1)
            for ct in range(KC):
                dve.wait_ge(rt, ct + 1)
                dve.reciprocal(rstd[:, ct], rstd[:, ct]).then_inc(rs, 1)
                dve.wait_ge(rs, ct + 1)
                dve.tensor_tensor(kk_out[:, ct], kk_out[:, ct], rstd[:, ct], MUL).then_inc(kk, 1)

        @block.tensor
        def _(pe):
            for ct in range(KC):
                pe.wait_ge(sq, ct + 1)
                if ct == 3:
                    pe.wait_ge(rt, 1)
                for a, n, b in ((0, CTX, 0), (CTX, SEQ, 1)):
                    last = pe.matmul(k.bank[2 * (ct % 3) + b][:, 0:n], k.c("head_ones"), squares[:, ct % 2, a:a + n],
                                     start=True, stop=True)
                last.then_inc(summed, 1)
            pe.wait_ge(landed, 16)
            pe.wait_ge(rt, KC)
            for u, (src, w0, _, _, d, ct) in enumerate(lora_units):
                r = slice(64 * d, 64 * d + 64)
                if u >= 4:
                    pe.wait_ge(lora_done, u - 3)
                for x, n, b in ((0, CTX, 0), (CTX, SEQ, 1)):
                    last = pe.matmul(k.bank[2 * (u % 4) + b][:, 0:n], lora[r, w0 + P * ct:w0 + P * ct + P],
                                     src[r, x:x + n], start=True, stop=True)
                last.then_inc(lora_summed, 1)


def factor_stage(k, A, R, K, B, r, kf, kk, vf, bonus_v, chunk_decay, tmp):
    nc = k.nc
    T1, T2, T3 = tmp[:, 0:ALL], tmp[:, ALL:2 * ALL], tmp[:, 2 * ALL:3 * ALL]
    one_minus, prefix, before, upto, e_before, e_upto, e_inv, a_done, r_done, pc_done, kf1, kd, k_done, prod, ba, \
        b_done, bonus_summed, bonus_done = (k.sem("factor_" + n) for n in (
            "one_minus_k_a", "prefix", "sum_before", "sum_upto", "exp_before", "exp_upto", "exp_inverse", "a", "r",
            "chunk_decay", "k_scale", "k_dir", "k", "bonus_product", "kk_a", "b", "bonus_summed", "bonus"))
    omka = k.small[:, 0:4]
    split = lambda x: x.rearrange("p (c t) -> p c t", t=CHUNK)
    with nc.Block("factors") as block:
        @block.vector
        def _(dve):
            dve.tensor_scalar(omka, k.v("k_a", 0, 4), -1.0, 1.0, MUL, ADD).then_inc(one_minus, 1)
            dve.wait_ge(one_minus, 1)
            for u in range(8):
                d, ct = divmod(u, 4)
                sig, a = A[:, d, ct], B[:, d, ct]
                if u:
                    dve.wait_ge(ba, u)
                    dve.wait_ge(k_done, u)
                if d == 0:
                    dve.tensor_tensor_scan(T1, k.c("chunk_start", 0, ALL), sig, 0.0, MUL, ADD).then_inc(upto, 1)
                    dve.wait_ge(upto, u + 1)
                    dve.tensor_tensor(T2, T1, sig, SUB).then_inc(before, 1)
                else:
                    dve.tensor_tensor_scan(T1, k.c("chunk_start", 0, ALL), sig, 0.0, MUL, ADD).then_inc(prefix, 1)
                    dve.wait_ge(prefix, u - 3)
                    total = split(T1)[:, :, CHUNK - 1:CHUNK].broadcast_to([P, N_CHUNK, CHUNK])
                    dve.tensor_tensor(split(T2), total, split(T1), SUB).then_inc(before, 1)
                    dve.wait_ge(before, u + 1)
                    dve.tensor_tensor(T1, T2, sig, ADD).then_inc(upto, 1)
                dve.wait_ge(e_before, u + 1)
                dve.tensor_tensor(A[:, d, ct], kk[:, ct], T2, MUL).then_inc(a_done, 1)
                dve.wait_ge(e_upto, u + 1)
                last = split(T3)[:, :, CHUNK - 1] if d == 0 else split(T3)[:, :, 0]
                if d == 0:
                    dve.tensor_copy(chunk_decay[:, :, u], last).then_inc(pc_done, 1)
                else:
                    dve.tensor_copy(chunk_decay[:, 0:N_CTX, u], last[:, N_CTX - 1::-1])
                    dve.tensor_copy(chunk_decay[:, N_CTX:N_CHUNK, u], last[:, N_CHUNK - 1:N_CTX - 1:-1]).then_inc(pc_done, 1)
                dve.wait_ge(a_done, u + 1)
                dve.tensor_scalar(T2, a, k.v("k_a", ct), omka[:, ct:ct + 1], MUL, ADD).then_inc(kf1, 1)
                dve.wait_ge(kf1, u + 1)
                dve.tensor_tensor(T2, T2, kf[:, ct], MUL).then_inc(kd, 1)
                dve.wait_ge(kd, u + 1)
                dve.wait_ge(e_inv, u + 1)
                dve.tensor_tensor(K[:, d, ct], T2, T1, MUL).then_inc(k_done, 1)
                dve.wait_ge(pc_done, u + 1)
                dve.wait_ge(r_done, u + 1)
                dve.scalar_tensor_tensor(out=T3[:, CTX:ALL], in0=T2[:, CTX:ALL], scalar=k.v("r_k", ct), in1=r[:, ct],
                                         op0=MUL, op1=MUL).then_inc(prod, 1)
            dve.wait_ge(b_done, 8)
            dve.wait_ge(bonus_summed, 8)
            for ct in range(KC):
                dve.tensor_tensor(bonus_v[:, ct], k.bank[ct][:, 0:SEQ], vf[:, ct, CTX:ALL], MUL).then_inc(bonus_done, 1)

        @block.gpsimd
        def _(pool):
            for u in range(8):
                d, ct = divmod(u, 4)
                pool.wait_ge(e_upto, u + 1)
                pool.tensor_tensor(R[:, d, ct], r[:, ct], T3[:, CTX:ALL], MUL).then_inc(r_done, 1)
                pool.wait_ge(e_inv, u + 1)
                pool.wait_ge(kf1, u + 1)
                pool.tensor_tensor(B[:, d, ct], B[:, d, ct], T1, MUL).then_inc(ba, 1)
                pool.wait_ge(ba, u + 1)
                pool.tensor_tensor(B[:, d, ct], B[:, d, ct], kk[:, ct], MUL).then_inc(b_done, 1)

        @block.scalar
        def _(act):
            for u in range(8):
                act.wait_ge(before, u + 1)
                act.wait_ge(upto, u + 1)
                act.activation(T2, T2, ACT.Exp, scale=DECAY_SCALE).then_inc(e_before, 1)
                if u:
                    act.wait_ge(bonus_summed, u)
                act.activation(T3, T1, ACT.Exp, scale=DECAY_SCALE).then_inc(e_upto, 1)
                act.wait_ge(e_upto, u + 1)
                act.activation(T1, T1, ACT.Exp, scale=-DECAY_SCALE).then_inc(e_inv, 1)

        @block.tensor
        def _(pe):
            for u in range(8):
                d, ct = divmod(u, 4)
                pe.wait_ge(prod, u + 1)
                pe.matmul(k.bank[ct][:, 0:SEQ], k.c("head_ones"), T3[:, CTX:ALL], start=d == 0, stop=d == 1,
                          skip_group_check=True).then_inc(bonus_summed, 1)


def chunk_at(d, n):
    return n if d == 0 else (N_CTX - 1 - n if n < N_CTX else N_CTX + N_CHUNK - 1 - n)


def scan_stage(k, A, R, K, B, vf, Y, chunk_decay, work):
    nc = k.nc
    off = [work]

    def buf(n=1):
        off[0] += 512 * n
        x = k.at(off[0] - 512 * n, 512 * n)
        return x.rearrange("p (n c) -> p n c", n=n)

    Mka, Z, S, V = buf(2), buf(), buf(), buf()
    Mba, T, W, Tt0, Tt1, E0, E1 = (k.mem[:, k.ring_at + 1024 * i:k.ring_at + 1024 * (i + 1)] for i in range(7))
    Tt, E = (Tt0, Tt1), (E0, E1)
    both = lambda: buf(4).rearrange("p (n a) c -> p n (a c)", n=2)
    Mr, KB = both(), both()
    UV = buf(2).rearrange("p a c -> p (a c)")
    GA, GB, BW0, BW1, BT_, BTT, BX, BZ = k.bank
    BW, BU, turned = (BW0, BW1), BZ, (BX, BZ)
    s = {n: k.sem("scan_" + n) for n in (
        "g_ba", "g_ka", "g_br", "g_kr", "mba", "mka", "mbr", "mkr", "zeroed", "e", "e1", "t", "tt", "w_mm", "w", "t_mm", "tt_mm",
        "k_turned", "kt", "b_turned", "bt", "v_turned", "v", "z_mm", "z", "u_mm", "un", "y_mm", "y", "s_mm", "st", "s")}
    LV = 5
    heads = (slice(0, 64), slice(64, 128))
    pairs = [(q, q // 4, q % 4) for q in range(8)]
    col = lambda q: slice(64 * q, 64 * q + 64)
    pair_head = lambda x: x.rearrange("p (q h c) -> p q h c", h=2, c=64)
    block_of = lambda q, h: slice(64 * (2 * q + h), 64 * (2 * q + h) + 64)
    with_r = lambda n: max(0, n - N_CTX)
    causal = k.c("causal", 0, 256).rearrange("p (d x t) -> p d x t", d=2, x=2)
    eye = k.c("ident").rearrange("p (q t) -> p q t", q=1).broadcast_to([P, 4, P])
    four = lambda x: x.rearrange("p (q t) -> p q t", q=4)
    of = lambda x, d: x[:, 512 * d:512 * d + 512]
    w_count = lambda p, l, d: 2 * (LV * p + l - 2) + d + 1
    t_count = lambda p, l, d: 2 * (LV * p + l - 1) + d + 1
    t_mm_count = lambda p, l, d: 2 * ((LV - 1) * p + l - 2) + d + 1
    tt_count = lambda p, l, d: 2 * (6 * p + l - 1) + d + 1
    eight = lambda x: x.rearrange("p (q t) -> p q t", q=8)
    level = lambda l: k.c("level", 64 * (l - 1), 64).rearrange("p (q t) -> p q t", q=1).broadcast_to([P, 16, 64])
    sixteen = lambda x: x.rearrange("p (q t) -> p q t", q=16)

    with nc.Block("scan") as block:
        @block.tensor
        def _(pe):
            def products(bank, *terms, crossed=False):
                for q, d, ct in pairs:
                    for h in range(2):
                        for i, term in enumerate(terms):
                            a, b = term(q, d, ct, h)
                            last = pe.matmul(bank[heads[h ^ crossed], col(q)], a, b, start=i == 0, stop=i == len(terms) - 1,
                                             skip_group_check=True)
                return last

            def gram(bank, X, Yv, base, p, crossed=False):
                return products(bank, lambda q, d, ct, h: (
                    X[heads[h], d, ct, 64 * chunk_at(d, p):64 * chunk_at(d, p) + 64],
                    Yv[heads[h], d, ct, 64 * (chunk_at(d, p) - base):64 * (chunk_at(d, p) - base) + 64]), crossed=crossed)

            def turn(x, p):
                for d in range(2):
                    for ct in range(KC):
                        last = pe.transpose(turned[d][0:64, P * ct:P * ct + P], x(d, ct)[:, 64 * chunk_at(d, p):64 * chunk_at(d, p) + 64],
                                            k.c("ident"))
                return last

            def diagonal(bank, d, a, b):
                for q in range(4 * d, 4 * d + 4):
                    last = pe.matmul(bank[:, P * (q % 4):P * (q % 4) + P], a[:, P * q:P * q + P], b[:, P * q:P * q + P],
                                     start=True, stop=True, skip_group_check=True)
                return last

            def level_w(p, l):
                pe.wait_ge(s["e"], 6 * p + l)
                for d in range(2):
                    pe.wait_ge(s["t"], t_count(p, l - 1, d))
                    if w_count(p, l, d) > 2:
                        pe.wait_ge(s["w"], w_count(p, l, d) - 2)
                    diagonal(BW[d], d, E[l % 2], T).then_inc(s["w_mm"], 1)

            def level_t(p, l):
                for d in range(2):
                    pe.wait_ge(s["w"], w_count(p, l, d))
                    pe.wait_ge(s["tt"], tt_count(p, l, d) - 1)
                    if l < 6:
                        pe.wait_ge(s["t"], t_count(p, l, d) - 1)
                        diagonal(BT_, d, Tt[p % 2], W).then_inc(s["t_mm"], 1)
                    diagonal(BTT, d, W, Tt[p % 2]).then_inc(s["tt_mm"], 1)

            for it in range(N_CHUNK + 1):
                p, j = it, it - 1
                prep, solve = p < N_CHUNK, j >= 0
                if prep:
                    if p:
                        if with_r(p) > with_r(p - 1):
                            pe.wait_ge(s["mbr"], with_r(p))
                            pe.wait_ge(s["mkr"], with_r(p))
                        else:
                            pe.wait_ge(s["mba"], p)
                            pe.wait_ge(s["mka"], p)
                    gram(GA, B, A, 0, p).then_inc(s["g_ba"], 1)
                    gram(GB, K, A, 0, p).then_inc(s["g_ka"], 1)
                if solve:
                    pe.wait_ge(s["s"], j + 1)
                    pe.wait_ge(s["mka"], j + 1)
                    pe.wait_ge(s["v"], 2 * (j + 1))
                    products(BZ, lambda q, d, ct, h: (A[heads[h], d, ct, 64 * chunk_at(d, j):64 * chunk_at(d, j) + 64],
                                                      S[heads[h], 0, col(q)]),
                             lambda q, d, ct, h: (Mka[heads[h], j % 2, col(q)], V[heads[h], 0, col(q)])).then_inc(s["z_mm"], 1)
                if prep:
                    pe.wait_ge(s["e"], 6 * p + 1)
                    if p:
                        pe.wait_ge(s["t"], 2 * LV * p)
                        pe.wait_ge(s["tt"], 12 * p)
                    for d, bank in enumerate((BT_, BTT)):
                        for ct in range(KC):
                            q = 4 * d + ct
                            last = pe.transpose(bank[:, P * ct:P * ct + P], E[1][:, P * q:P * q + P], k.c("ident"))
                        last.then_inc(s["e1"], 1)
                    if p >= N_CTX:
                        pe.wait_ge(s["mba"], p + 1)
                        gram(GA, B, R, N_CTX, p).then_inc(s["g_br"], 1)
                        pe.wait_ge(s["mka"], p + 1)
                        gram(GB, K, R, N_CTX, p, crossed=True).then_inc(s["g_kr"], 1)
                if solve:
                    pe.wait_ge(s["z"], j + 1)
                    pe.wait_ge(s["tt"], 12 * (j + 1))
                    for q in range(8):
                        last = pe.matmul(BU[:, col(q)], Tt[j % 2][:, P * q:P * q + P], Z[:, 0, col(q)],
                                         start=True, stop=True, skip_group_check=True)
                    last.then_inc(s["u_mm"], 1)
                if prep:
                    level_w(p, 2)
                    if p:
                        pe.wait_ge(s["v"], 2 * p)
                    if solve:
                        pe.wait_ge(s["un"], j + 1)
                    turn(lambda d, ct: K[:, d, ct], p).then_inc(s["k_turned"], 1)
                    level_t(p, 2)
                    level_w(p, 3)
                if solve and j >= N_CTX:
                    pe.wait_ge(s["kt"], min(p + 1, N_CHUNK))
                    pe.wait_ge(s["bt"], j + 1)
                    pe.wait_ge(s["un"], j + 1)
                    pe.wait_ge(s["mkr"], with_r(j + 1))
                    pe.wait_ge(s["mbr"], with_r(j + 1))
                    products(BX, lambda q, d, ct, h: (S[heads[h], 0, col(q)], R[heads[h], d, ct, 64 * (chunk_at(d, j) - N_CTX):
                                                                                64 * (chunk_at(d, j) - N_CTX) + 64]),
                             lambda q, d, ct, h: (UV[:, block_of(q, h)], Mr[:, j % 2, block_of(q, h)])).then_inc(s["y_mm"], 1)
                if prep:
                    level_t(p, 3)
                    level_w(p, 4)
                if solve and j < N_CHUNK - 1:
                    pe.wait_ge(s["un"], j + 1)
                    pe.wait_ge(s["kt"], j + 1)
                    pe.wait_ge(s["bt"], j + 1)
                    pe.wait_ge(s["kt"], j + 2)
                    products(BZ, lambda q, d, ct, h: (KB[:, j % 2, block_of(q, h)], UV[:, block_of(q, h)])).then_inc(s["s_mm"], 1)
                if prep:
                    level_t(p, 4)
                    level_w(p, 5)
                    pe.wait_ge(s["kt"], p + 1)
                    if solve:
                        pe.wait_ge(s["st"], j + 1)
                    if solve and j >= N_CTX:
                        pe.wait_ge(s["y"], with_r(j + 1))
                    turn(lambda d, ct: B[:, d, ct], p).then_inc(s["b_turned"], 1)
                    level_t(p, 5)
                    level_w(p, 6)
                    pe.wait_ge(s["bt"], p + 1)
                    turn(lambda d, ct: vf[:, ct], p).then_inc(s["v_turned"], 1)
                    level_t(p, 6)

        @block.gpsimd
        def _(pool):
            for p in range(N_CHUNK):
                pool.wait_ge(s["mba"], p + 1)
                for l in range(1, 7):
                    if l <= 2 and p:
                        pool.wait_ge(s["w_mm"], w_count(p - 1, l + 4, 1))
                    if l == 3:
                        pool.wait_ge(s["e1"], 2 * (p + 1))
                        pool.wait_ge(s["tt"], tt_count(p, 1, 1))
                    if l > 3:
                        pool.wait_ge(s["w_mm"], w_count(p, l - 2, 1))
                    pool.tensor_tensor(sixteen(E[l % 2]), sixteen(Mba), level(l), MUL).then_inc(s["e"], 1)

        @block.scalar
        def _(act):
            for it in range(N_CHUNK + 1):
                p, j = it, it - 1
                prep, solve = p < N_CHUNK, j >= 0

                def take_turned(dst, crossed, done):
                    for d in range(2):
                        for h in range(2):
                            ins = act.activation(dst(heads[h ^ crossed], d, h), pair_head(turned[d][0:64, :])[:, :, h], ACT.Copy)
                    ins.then_inc(s[done], 1)
                block_in = lambda x: lambda r, d, h: pair_head(x[r])[:, 4 * d:4 * d + 4, h]

                def copy_w(l):
                    for d in range(2):
                        act.wait_ge(s["w_mm"], w_count(p, l, d))
                        act.activation(of(W, d), BW[d][:, :], ACT.Copy).then_inc(s["w"], 1)

                if solve:
                    act.wait_ge(s["z_mm"], j + 1)
                    act.activation(Z[:, 0], BZ[:, :], ACT.Copy).then_inc(s["z"], 1)
                    act.wait_ge(s["u_mm"], j + 1)
                    for h in range(2):
                        ins = act.activation(pair_head(UV[heads[h]])[:, :, h], eight(BU[heads[h], :]), ACT.Copy, scale=-1.0)
                    ins.then_inc(s["un"], 1)
                if prep:
                    copy_w(2)
                    act.wait_ge(s["k_turned"], p + 1)
                    take_turned(block_in(KB[:, p % 2]), True, "kt")
                    copy_w(3)
                    copy_w(4)
                    copy_w(5)
                    act.wait_ge(s["b_turned"], p + 1)
                    take_turned(block_in(KB[:, p % 2]), False, "bt")
                    copy_w(6)
                    act.wait_ge(s["v_turned"], p + 1)
                    take_turned(block_in(UV), True, "v")
                    take_turned(lambda r, d, h: eight(V[r, 0])[:, 4 * d:4 * d + 4], False, "v")

        @block.vector
        def _(dve):
            dve.memset(S[:, 0], 0.0).then_inc(s["s"], 1)
            dve.memset(Mba, 0.0).then_inc(s["zeroed"], 1)
            dve.wait_ge(s["zeroed"], 1)

            def masked(dst, bank, x, ready, done, n):
                dve.wait_ge(s[ready], n)
                m = causal[:, :, x:x + 1].broadcast_to([P, 2, 4, 64])
                dve.tensor_tensor(dst.rearrange("p (d c t) -> p d c t", d=2, c=4),
                                  bank[:, :].rearrange("p (d c t) -> p d c t", d=2, c=4), m, MUL).then_inc(s[done], 1)

            def masked_blocks(dst, bank, x, crossed, ready, done, n):
                dve.wait_ge(s[ready], n)
                for h in range(2):
                    r = heads[h ^ crossed]
                    m = causal[r, :, x:x + 1].broadcast_to([64, 2, 4, 64])
                    by_d = lambda x: x.rearrange("p (d c) t -> p d c t", d=2)
                    ins = dve.tensor_tensor(by_d(pair_head(dst[r])[:, :, h]), by_d(eight(bank[r, :])), m, MUL)
                ins.then_inc(s[done], 1)

            for it in range(N_CHUNK + 1):
                p, j = it, it - 1
                prep, solve = p < N_CHUNK, j >= 0

                def level_update(l):
                    for d in range(2):
                        if l < 6:
                            dve.wait_ge(s["t_mm"], t_mm_count(p, l, d))
                            dve.tensor_tensor(of(T, d), of(T, d), BT_[:, :], SUB).then_inc(s["t"], 1)
                        dve.wait_ge(s["tt_mm"], w_count(p, l, d))
                        dve.tensor_tensor(of(Tt[p % 2], d), of(Tt[p % 2], d), BTT[:, :], SUB).then_inc(s["tt"], 1)

                if prep:
                    if p:
                        dve.wait_ge(s["e"], 6 * p)
                    masked_blocks(Mba, GA, 0, False, "g_ba", "mba", p + 1)
                    masked(Mka[:, p % 2], GB, 0, "g_ka", "mka", p + 1)
                    for d, bank in enumerate((BT_, BTT)):
                        dve.wait_ge(s["e1"], 2 * p + d + 1)
                        dve.tensor_tensor(four(of(T, d)), eye, four(bank[:, :]), SUB).then_inc(s["t"], 1)
                        dve.tensor_tensor(four(of(Tt[p % 2], d)), eye, four(of(E[1], d)), SUB).then_inc(s["tt"], 1)
                    if p >= N_CTX:
                        masked_blocks(Mr[:, p % 2], GA, 1, False, "g_br", "mbr", with_r(p + 1))
                        masked_blocks(Mr[:, p % 2], GB, 1, True, "g_kr", "mkr", with_r(p + 1))
                    level_update(2)
                if solve and j >= N_CTX:
                    dve.wait_ge(s["y_mm"], with_r(j + 1))
                    for d in range(2):
                        c = chunk_at(d, j) - N_CTX
                        y = Y[:, :, 64 * c:64 * c + 64]
                        part = BX[:, 256 * d:256 * d + 256].rearrange("p (c t) -> p c t", c=4)
                        first = j < N_CTX + (N_CHUNK - N_CTX) // 2
                        ins = dve.tensor_copy(y, part) if first else dve.tensor_tensor(y, y, part, ADD)
                    ins.then_inc(s["y"], 1)
                if prep:
                    level_update(3)
                if solve and j < N_CHUNK - 1:
                    dve.wait_ge(s["s_mm"], j + 1)
                    dve.tensor_tensor(S[:, 0], S[:, 0], BZ[:, :], ADD).then_inc(s["st"], 1)
                    dve.wait_ge(s["st"], j + 1)
                    decay = chunk_decay[:, j, :].rearrange("p (q t) -> p q t", t=1).broadcast_to([P, 8, 64])
                    dve.tensor_tensor(eight(S[:, 0]), eight(S[:, 0]), decay, MUL).then_inc(s["s"], 1)
                if prep:
                    level_update(4)
                    level_update(5)
                    level_update(6)


def rwkv_out_stage(k, Y, bonus_v, gate_in, g2, rw, work, loads, landed):
    nc = k.nc
    centred = k.at(work, 4 * SEQ).rearrange("p (c t) -> p c t", c=4)
    squares = k.at(work + 2048, 4 * SEQ).rearrange("p (c t) -> p c t", c=4)
    rstd = k.at(work + 4096, 4 * SEQ).rearrange("p (c t) -> p c t", c=4)
    s = {n: k.sem("rwkv_out_" + n) for n in ("mean_mm", "centred", "sq", "var_mm", "root", "rstd", "scaled", "based",
                                            "gate_mm", "done")}
    with nc.Block("rwkv_out") as block:
        @block.sync
        def _(sp):
            for dst, src in loads:
                sp.dma_start(dst, src).then_inc(landed, 16)
            k.send_weights(sp)
            sp.wait_ge(landed, 16 * len(loads))

        @block.tensor
        def _(pe):
            for ct in range(KC):
                pe.matmul(k.bank[ct][:, :], k.c("head_ones"), Y[:, ct], start=True, stop=True).then_inc(s["mean_mm"], 1)
            for ct in range(KC):
                pe.wait_ge(s["sq"], ct + 1)
                pe.matmul(k.bank[4 + ct][:, :], k.c("head_ones"), squares[:, ct], start=True, stop=True).then_inc(s["var_mm"], 1)
            pe.wait_ge(landed, 16 * len(loads))
            for ct in range(KC):
                pe.wait_ge(s["centred"], ct + 1)
                pe.matmul(k.bank[ct][:, :], g2[:, P * ct:P * ct + P], gate_in, start=True, stop=True).then_inc(s["gate_mm"], 1)

        @block.scalar
        def _(act):
            for ct in range(KC):
                act.wait_ge(s["centred"], ct + 1)
                act.activation(squares[:, ct], centred[:, ct], ACT.Square).then_inc(s["sq"], 1)
            for ct in range(KC):
                act.wait_ge(s["var_mm"], ct + 1)
                act.activation(rstd[:, ct], k.bank[4 + ct][:, :], ACT.Sqrt, bias=k.v("eps_gn"), scale=1.0 / HEAD).then_inc(s["root"], 1)

        @block.vector
        def _(dve):
            for ct in range(KC):
                dve.wait_ge(s["mean_mm"], ct + 1)
                dve.scalar_tensor_tensor(out=centred[:, ct], in0=k.bank[ct][:, :], scalar=-1.0 / HEAD, in1=Y[:, ct],
                                         op0=MUL, op1=ADD).then_inc(s["centred"], 1)
            for ct in range(KC):
                dve.wait_ge(s["root"], ct + 1)
                dve.reciprocal(rstd[:, ct], rstd[:, ct]).then_inc(s["rstd"], 1)
                dve.wait_ge(s["rstd"], ct + 1)
                dve.scalar_tensor_tensor(out=Y[:, ct], in0=centred[:, ct], scalar=k.v("gn_g", ct), in1=rstd[:, ct],
                                         op0=MUL, op1=MUL).then_inc(s["scaled"], 1)
                dve.wait_ge(s["scaled"], ct + 1)
                dve.scalar_tensor_tensor(out=Y[:, ct], in0=Y[:, ct], scalar=k.v("gn_b", ct), in1=bonus_v[:, ct],
                                         op0=ADD, op1=ADD).then_inc(s["based"], 1)
                dve.wait_ge(s["based"], ct + 1)
                dve.wait_ge(s["gate_mm"], ct + 1)
                dve.tensor_tensor(rw[:, ct], Y[:, ct], k.bank[ct][:, :], MUL).then_inc(s["done"], 1)


def fourier_stage(k, u, seq, chan, mixed, parts):
    nc = k.nc
    chan_mm, chan_out, seq_mm, seq_out = (k.sem("fourier_" + n) for n in ("channels", "channels_out", "tokens", "tokens_out"))
    with nc.Block("fourier") as block:
        @block.tensor
        def _(pe):
            for tt in range(4):
                for ct in range(KC):
                    i = 4 * tt + ct
                    if i >= 4:
                        pe.wait_ge(chan_out, i - 3)
                    pe.matmul(k.bank[i % 4][:, 0:256], u[:, ct, P * tt:P * tt + P], chan, start=True, stop=True).then_inc(chan_mm, 1)
            pe.wait_ge(chan_out, 16)
            for ct in range(KC):
                for i in range(8):
                    last = pe.matmul(k.bank[4 + ct][:, :], parts[:, i % 4, ct, P * (i // 4):P * (i // 4) + P],
                                     seq[:, i // 4, i % 4], start=i == 0, stop=i == 7)
                last.then_inc(seq_mm, 1)

        @block.scalar
        def _(act):
            for i in range(16):
                act.wait_ge(chan_mm, i + 1)
                act.activation(parts[:, i // 4, i % 4], k.bank[i % 4][:, 0:256], ACT.Copy).then_inc(chan_out, 1)
            for ct in range(KC):
                act.wait_ge(seq_mm, ct + 1)
                act.activation(mixed[:, ct], k.bank[4 + ct][:, :], ACT.Copy).then_inc(seq_out, 1)


class Residual:

    def __init__(self, k, name, per, tiles_of, rhs, gate, x, dst, banks=(0, 1, 2, 3), mod=None, rhs_ready=None):
        self.k, self.per, self.tiles_of, self.rhs, self.gate, self.x, self.dst = k, per, tiles_of, rhs, gate, x, dst
        self.banks, self.mod, self.rhs_ready = [k.bank[b] for b in banks], mod, rhs_ready
        self.summed, self.done = k.sem(name + "_summed"), k.sem(name + "_done")
        if mod:
            self.mod_acc, self.mod_step = k.sem("mod2_acc"), [k.sem("mod2_step"), 0]
            for g in range(24):
                k.freed[k.number("ada2", g)] = [(self.mod_acc, g + 1 + min(g + 1, 8))]

    def products(self, pe):
        k = self.k
        for m in range(KD):
            if m >= 4:
                pe.wait_ge(self.done, m - 3)
            pieces = self.tiles_of(m)
            n = sum(len(cols) for _, cols in pieces)
            i = 0
            for g, cols in pieces:
                k.weights_ready(pe, g)
                for w, kt in cols:
                    if self.rhs_ready and m == 0:
                        pe.wait_ge(self.rhs_ready, kt + 1)
                    last = pe.matmul(self.banks[m % 4][:, :], w, self.rhs[:, kt], start=i == 0, stop=i == n - 1)
                    i += 1
                if g != pieces[-1][0]:
                    last.then_inc(self.summed, 1)
            last.then_inc(self.summed, 1)

    def additions(self, dve):
        k, mod = self.k, self.mod
        for m in range(KD):
            dve.wait_ge(self.summed, self.per * (m + 1))
            dve.scalar_tensor_tensor(out=self.dst[:, m], in0=self.banks[m % 4][:, :], scalar=self.gate(m), in1=self.x[:, m],
                                     op0=MUL, op1=ADD).then_inc(self.done, 1)
            for g in MOD_BESIDE[m] if mod else ():
                for t in range(2 if g < 8 else 1):
                    mod_slot(k, dve, "ada2", g, k.silu[1], mod[t][:, 256 * g:256 * g + 256], t, self.mod_step, self.mod_acc)


def residual_stage(k, name, *args):
    nc = k.nc
    r = Residual(k, name, *args)
    with nc.Block(name) as block:
        @block.sync
        def _(sp):
            k.send_weights(sp)

        @block.tensor
        def _(pe):
            r.products(pe)

        @block.vector
        def _(dve):
            r.additions(dve)


def halves(k, name):
    def pieces(m):
        g = k.number(name, m // 2)
        w = k.slot(g).rearrange("p (k m) -> p k m", k=KD)
        return [(g, [(w[:, kt, P * (m % 2):P * (m % 2) + P], kt) for kt in range(KD)])]
    return pieces


def ffn_stage(k, h, hidden, work, down_args, mod):
    nc = k.nc
    NP = 3
    PADW = (ROWS + 2) * (GRID_W + 2)
    pad = k.at(work, NP * 2 * PADW).rearrange("p (n h r c) -> p n h r c", n=NP, h=2, r=ROWS + 2)
    acc = k.at(work + NP * 2 * PADW, 2 * 2 * SEQ).rearrange("p (n h r c) -> p n h r c", n=2, h=2, r=ROWS)
    s = {n: k.sem("ffn_" + n) for n in ("zeroed", "up_mm", "padded", "tap", "tapped", "silu", "hidden")}
    k.frees([k.number("w_up", m) for m in range(KF)], s["up_mm"])
    k.frees_later([k.number("w_down", g) for g in range(16)], "w_down_summed", 1)
    down = Residual(k, "w_down", 2, *down_args, banks=(6, 7, 0, 1), mod=mod, rhs_ready=s["hidden"])
    flat = lambda x: x.rearrange("p r c -> p (r c)")
    with nc.Block("ffn_up") as block:
        @block.sync
        def _(sp):
            k.send_weights(sp)

        @block.gpsimd
        def _(pool):
            pool.memset(k.at(work, NP * 2 * PADW), 0.0).then_inc(s["zeroed"], 1)

        @block.tensor
        def _(pe):
            for m in range(KF):
                g = k.number("w_up", m)
                k.weights_ready(pe, g)
                w = k.slot(g).rearrange("p (k h m) -> p k h m", k=KD, h=2)
                if m >= 3:
                    pe.wait_ge(s["padded"], m - 2)
                for h2 in range(2):
                    for kt in range(KD):
                        last = pe.matmul(k.bank[2 * (m % 3) + h2][:, :], w[:, kt, h2], h[:, kt], start=kt == 0, stop=kt == KD - 1)
                last.then_inc(s["up_mm"], 1)
            pe.wait_ge(s["padded"], KF)
            down.products(pe)

        @block.scalar
        def _(act):
            act.wait_ge(s["zeroed"], 1)
            for m in range(KF + 1):
                if m < KF:
                    act.wait_ge(s["up_mm"], m + 1)
                    if m >= NP:
                        act.wait_ge(s["tapped"], 2 * (m - NP + 1))
                    for h2 in range(2):
                        ins = act.activation(pad[:, m % NP, h2, 1:ROWS + 1, 1:GRID_W + 1],
                                             k.bank[2 * (m % 3) + h2][:, :].rearrange("p (r c) -> p r c", r=ROWS), ACT.Copy)
                    ins.then_inc(s["padded"], 1)
                if m >= 1:
                    act.wait_ge(s["tapped"], 2 * m - 1)
                    g = flat(acc[:, (m - 1) % 2, 0])
                    act.activation(g, g, ACT.Silu).then_inc(s["silu"], 1)

        @block.vector
        def _(dve):
            def product(m):
                dve.wait_ge(s["silu"], m + 1)
                dve.wait_ge(s["tapped"], 2 * m + 2)
                dve.tensor_tensor(hidden[:, m], flat(acc[:, m % 2, 0]), flat(acc[:, m % 2, 1]), MUL).then_inc(s["hidden"], 1)

            for m in range(KF):
                dve.wait_ge(s["padded"], m + 1)
                for i in range(9):
                    for h2 in range(2):
                        t = m + KF * h2
                        a = acc[:, m % 2, h2]
                        src = pad[:, m % NP, h2, i // 3:i // 3 + ROWS, i % 3:i % 3 + GRID_W]
                        w = k.v("ffn_conv_w", i * 2 * KF + t)
                        if i == 0:
                            ins = dve.tensor_scalar(a, src, w, k.v("ffn_conv_b", t), MUL, ADD)
                        else:
                            dve.wait_ge(s["tap"], 16 * m + 2 * i + h2 - 1)
                            ins = dve.scalar_tensor_tensor(out=a, in0=src, scalar=w, in1=a, op0=MUL, op1=ADD)
                        ins.then_inc(s["tap" if i < 8 else "tapped"], 1)
                    if i == 1 and m:
                        product(m - 1)
            product(KF - 1)
            down.additions(dve)


def block_one(k):
    nc, d = k.nc, k.d
    three = lambda at, n, w: k.at(at, n * w).rearrange("p (n w) -> p n w", n=n)
    four = lambda at, t: k.at(at, 2 * 4 * t).rearrange("p (d c t) -> p d c t", d=2, c=4)
    x_landed = k.sem("x_landed")
    h, x0 = three(0, KD, ALL), three(6144, KD, ALL)
    mod_first_stage(k, (k.at(6144, KD * ALL), d["x0"].rearrange("p k t -> p (k t)"), x_landed))
    m1 = k.mod[0]
    norm_stage(k, "norm1", x0, h, [(0, CTX, 0), (CTX, SEQ, 1)],
               gain=lambda i: [(m1[:, 8:16, 1 - i], k.v("norm1_g", 0, 8))],
               shift=lambda kt, i: m1[:, kt, 1 - i:2 - i], work=12288, first=(x_landed, 16))
    kp, vp, rp = three(12288, 4, 772), three(15376, 4, 772), three(18464, 4, 514)
    uf = three(6144, 4, SEQ)
    gd, wd, ad = k.at(29696, SEQ), k.at(30208, ALL), k.at(30976, ALL)
    ID = ACT.Copy
    u = {}
    for ct in range(4):
        u[ct] = ([(uf[:, ct], ID)], None)
        u[4 + ct] = ([(rp[:, ct, 1:1 + SEQ], ID)], None)
        for o, pad in ((8, kp), (12, vp)):
            u[o + ct] = ([(pad[:, ct, CTX + 3:CTX + 3 + SEQ], ID)], [(pad[:, ct, 1:1 + CTX], ID)])
    u[16] = ([(wd[:, CTX:ALL], ACT.Tanh)], [(wd[:, 0:CTX], ACT.Tanh)])
    u[17] = ([(ad[:, CTX:ALL], ID)], [(ad[:, 0:CTX], ID)])
    u[18] = ([(gd, ACT.Sigmoid)], None)
    zeros = [rp[:, :, 0:SEQ + 2:SEQ + 1]] + [p[:, :, a:b] for p in (kp, vp) for a, b in ((0, 1), (CTX + 1, CTX + 3), (771, 772))]
    vf, kf, r = three(22528, 4, ALL), three(35584, 4, ALL), three(38656, 4, SEQ)
    convs = {}
    for ct in range(4):
        convs[4 + ct] = [(rp[:, ct], r[:, ct], ct)]
        for m, pad, dst, w in ((8, kp, kf, 4), (12, vp, vf, 8)):
            convs[m + ct] = [(pad[:, ct, 0:CTX + 2], dst[:, ct, 0:CTX], w + ct),
                             (pad[:, ct, CTX + 2:CTX + SEQ + 4], dst[:, ct, CTX:ALL], w + ct)]
    in_proj_stage(k, h, u, zeros, convs, k.at(8192, 4608))
    A, R, K, B = four(0, ALL), four(6144, SEQ), four(10240, ALL), four(16384, ALL)
    bonus_v, Y, kk = three(25600, 4, SEQ), three(27648, 4, SEQ), three(25600, 4, ALL)
    chunk_decay = k.mem[:, k.decay_at:k.decay_at + 96].rearrange("p (n q) -> p n q", q=8)
    uf_dram = nc.dram_tensor("fourier_in", [P, 4 * SEQ], F32, kind="Internal").ap()
    lora = k.at(10240, 1024)
    key_stage(k, kf, kk, wd, ad, lora, A, B, 11264, (uf_dram, k.at(6144, 2048)), (lora, d["lora"]))
    factor_stage(k, A, R, K, B, r, kf, kk, vf, bonus_v, chunk_decay, k.at(30208, 2304))
    scan_stage(k, A, R, K, B, vf, Y, chunk_decay, 30208)
    cat, g2, x = three(0, 8, SEQ), k.at(14592, CH), three(15104, KD, SEQ)
    landed = k.sem("mix_loads_landed")
    loads = [(g2, d["gate_g2"]), (k.at(4096, 2048), d["seq_dft"][0]), (k.at(6144, 2048), d["seq_dft"][1]),
             (k.at(8192, 256), d["chan_dft"]), (k.at(8448, 2048), uf_dram), (x, d["x0"][:, :, CTX:ALL])]
    rwkv_out_stage(k, Y, bonus_v, gd, g2, cat[:, 4:8], 19200, loads, landed)
    parts = k.at(10496, 4096).rearrange("p (t c m) -> p t c m", t=4, c=4)
    seq = k.at(4096, 4096).rearrange("p (x t n) -> p x t n", x=2, t=4)
    fourier_stage(k, three(8448, 4, SEQ), seq, k.at(8192, 256), cat[:, 0:4], parts)
    norm_stage(k, "fourier_norm", cat[:, 0:4], cat[:, 0:4], [(0, SEQ, 0)],
               gain=lambda i: [(k.v("fourier_g", 0, 4), None)], shift=None, work=19200, tiles=4)
    x1, h2 = three(30208, KD, SEQ), three(35840, KD, SEQ)

    k.frees_later([k.number("w_out", g) for g in range(4)], "w_out_summed", 2)
    residual_stage(k, "w_out", 1, halves(k, "w_out"), cat, lambda m: m1[:, 16 + m, 0:1], x, x1)
    norm_stage(k, "norm2", x1, h2, [(0, SEQ, 0)], gain=lambda i: [(m1[:, 32:40, 0], k.v("norm2_g", 0, 8))],
               shift=lambda kt, i: m1[:, 24 + kt, 0:1], work=0)
    hidden = three(0, KF, SEQ)
    mod_sums = [k.at(21504, 6144), k.at(27648, 2048)]
    x2 = three(17408, KD, SEQ)

    def down(m):
        out = []
        for half in range(2):
            g = k.number("w_down", 2 * m + half)
            w = k.slot(g, 11 * P).rearrange("p (k m) -> p k m", k=11)
            out.append((g, [(w[:, i], 11 * half + i) for i in range(11)]))
        return out
    ffn_stage(k, h2, hidden, 11264, (down, hidden, lambda m: m1[:, 40 + m, 0:1], x1, x2), mod_sums)
    src = three(0, KD, ALL)
    norm_stage(k, "final1", x2, src[:, :, CTX:ALL], [(0, SEQ, 0)], gain=lambda i: [(k.v("final_g", 0, 8), None)],
               shift=None, work=35840, loads=[(src[:, :, 0:CTX], d["ctx2"])], mod2=(cut(mod_sums[0]) + cut(mod_sums[1]), k.at(34304, 512)))
    return src


def in_proj2_stage(k, h, q, kf, v_tok, upad, sig, gate_a, gate_b, conv):
    nc = k.nc
    s = {n: k.sem("proj2_" + n) for n in ("summed", "copied", "padded", "gated", "tap")}
    K2 = 31
    units = []
    for g in range(4):
        units += [(k.number("w_in2_q", g), "qk", 2 * g + j) for j in range(2)]
    for g in range(2):
        units += [(k.number("w_in2_v", g), "v", t) for t in range(6)]
    for g in range(12):
        units += [(k.number("w_in2_g", g), "glu" if g < 4 else "gate", 2 * g + j) for j in range(2)]
    for i, (g, _, _) in enumerate(units):
        k.freed[g] = [(s["summed"], i + 1)]
    glu_g = [i for i, u in enumerate(units) if u[1] == "glu" and u[2] >= 4]
    with nc.Block("in_proj2") as block:
        @block.sync
        def _(sp):
            k.send_weights(sp)

        @block.gpsimd
        def _(pool):
            pool.memset(upad[:, :, 0:15], 0.0).then_inc(s["padded"], 1)
            pool.memset(upad[:, :, SEQ + 15:SEQ + 30], 0.0).then_inc(s["padded"], 1)

        @block.tensor
        def _(pe):
            for i, (g, kind, t) in enumerate(units):
                k.weights_ready(pe, g)
                w = k.slot(g).rearrange("p (k m) -> p k m", k=KD)
                if i >= 3:
                    pe.wait_ge(s["copied"], i - 2)
                b = k.bank[2 * (i % 3)]
                for kt in range(KD):
                    if kind == "v":
                        last = pe.matmul(b[:, 0:256], h[:, kt, P * t:P * t + P], w[:, kt], start=kt == 0, stop=kt == KD - 1)
                    else:
                        last = pe.matmul(b[:, :], w[:, kt, P * (t % 2):P * (t % 2) + P], h[:, kt, CTX:ALL],
                                         start=kt == 0, stop=kt == KD - 1)
                if kind == "qk" and t >= 4:
                    for kt in range(KD):
                        last = pe.matmul(k.bank[2 * (i % 3) + 1][:, 0:CTX], w[:, kt, P * (t % 2):P * (t % 2) + P],
                                         h[:, kt, 0:CTX], start=kt == 0, stop=kt == KD - 1)
                last.then_inc(s["summed"], 1)

        @block.scalar
        def _(act):
            for i, (g, kind, t) in enumerate(units):
                act.wait_ge(s["summed"], i + 1)
                b = k.bank[2 * (i % 3)]
                if kind == "qk" and t < 4:
                    ins = act.activation(q[:, t], b[:, :], ACT.Copy)
                elif kind == "qk":
                    act.activation(kf[:, t - 4, CTX:ALL], b[:, :], ACT.Copy)
                    ins = act.activation(kf[:, t - 4, 0:CTX], k.bank[2 * (i % 3) + 1][:, 0:CTX], ACT.Copy)
                elif kind == "v":
                    half = g - k.number("w_in2_v", 0)
                    ins = act.activation(v_tok[:, t, 256 * half:256 * half + 256], b[:, 0:256], ACT.Copy)
                elif kind == "glu" and t < 4:
                    ins = act.activation(upad[:, t, 15:15 + SEQ], b[:, :], ACT.Copy)
                elif kind == "glu":
                    ins = act.activation(sig[:, t - 4], b[:, :], ACT.Sigmoid)
                else:
                    dst = gate_a[:, t - 8] if t < 16 else gate_b[:, t - 16]
                    ins = act.activation(dst, b[:, :], ACT.Sigmoid)
                ins.then_inc(s["copied"], 1)

        @block.vector
        def _(dve):
            for ct in range(KC):
                dve.wait_ge(s["copied"], glu_g[ct] + 1)
                u = upad[:, ct, 15:15 + SEQ]
                dve.tensor_tensor(u, u, sig[:, ct], MUL).then_inc(s["gated"], 1)
            dve.wait_ge(s["gated"], 4)
            dve.wait_ge(s["padded"], 2)
            for i in range(K2):
                for ct in range(KC):
                    src, w = upad[:, ct, i:i + SEQ], k.v("conv2_w", 4 * i + ct)
                    if i == 0:
                        ins = dve.tensor_scalar(conv[:, ct], src, w, k.v("conv2_b", ct), MUL, ADD)
                    else:
                        dve.wait_ge(s["tap"], 4 * (i - 1) + ct + 1)
                        ins = dve.scalar_tensor_tensor(out=conv[:, ct], in0=src, scalar=w, in1=conv[:, ct], op0=MUL, op1=ADD)
                    ins.then_inc(s["tap"], 1)


def layer_norm_stage(k, x, work):
    nc = k.nc
    squares = k.at(work, 4 * SEQ).rearrange("p (c t) -> p c t", c=4)
    rstd = k.at(work + 2048, SEQ)
    s = {n: k.sem("ln_" + n) for n in ("mean", "centred", "sq", "var", "root", "rstd", "scaled", "silu")}
    with nc.Block("layer_norm") as block:
        @block.tensor
        def _(pe):
            for ct in range(KC):
                last = pe.matmul(k.bank[0][:, :], k.c("ones"), x[:, ct], start=ct == 0, stop=ct == 3)
            last.then_inc(s["mean"], 1)
            for ct in range(KC):
                pe.wait_ge(s["sq"], ct + 1)
                last = pe.matmul(k.bank[1][:, :], k.c("ones"), squares[:, ct], start=ct == 0, stop=ct == 3)
            last.then_inc(s["var"], 1)

        @block.vector
        def _(dve):
            dve.wait_ge(s["mean"], 1)
            for ct in range(KC):
                dve.scalar_tensor_tensor(out=x[:, ct], in0=k.bank[0][:, :], scalar=-1.0 / CH, in1=x[:, ct],
                                         op0=MUL, op1=ADD).then_inc(s["centred"], 1)
            dve.wait_ge(s["root"], 1)
            dve.reciprocal(rstd, rstd).then_inc(s["rstd"], 1)
            dve.wait_ge(s["rstd"], 1)
            dve.wait_ge(s["sq"], 4)
            for ct in range(KC):
                dve.scalar_tensor_tensor(out=x[:, ct], in0=x[:, ct], scalar=k.v("ln_g", ct), in1=rstd,
                                         op0=MUL, op1=MUL).then_inc(s["scaled"], 1)

        @block.scalar
        def _(act):
            for ct in range(KC):
                act.wait_ge(s["centred"], ct + 1)
                act.activation(squares[:, ct], x[:, ct], ACT.Square).then_inc(s["sq"], 1)
            act.wait_ge(s["var"], 1)
            act.activation(rstd, k.bank[1][:, :], ACT.Sqrt, bias=k.v("eps_norm"), scale=1.0 / CH).then_inc(s["root"], 1)
            for ct in range(KC):
                act.wait_ge(s["scaled"], ct + 1)
                act.activation(x[:, ct], x[:, ct], ACT.Silu, bias=k.v("ln_b", ct)).then_inc(s["silu"], 1)


def attention_stage(k, q, kf, v_tok, att, work_bias, work_s, work_p):
    nc = k.nc
    NB = 3
    NS = 14
    bias = k.at(work_bias, 2 * NS * 64).rearrange("p (n s c) -> p n s c", n=2, s=NS)
    sc = k.at(work_s, NB * ALL).rearrange("p (n w) -> p n w", n=NB)
    pt = k.at(work_p, 2 * 6 * SEQ).rearrange("p (n j w) -> p n j w", n=2, j=6)
    col = k.small[:, 0:4 * NB].rearrange("p (n x) -> p n x", n=NB)
    s = {n: k.sem("att_" + n) for n in ("bias_ready", "masked", "s_mm", "s_lat", "s_ctx", "max", "neg", "exp", "inv", "p",
                                       "turned", "pt", "av_mm", "av")}
    landed = [k.sem(f"att_bias_landed_{i}") for i in range(2)]
    rpb = k.d["rpb"]
    N = 32
    SCALE = HEAD ** -0.5
    with nc.Block("attention") as block:
        @block.sync
        def _(sp):
            for hd in range(8):
                if hd >= 2:
                    sp.wait_ge(s["s_lat"], 4 * (hd - 1))
                for par in range(2):
                    off = 64 + hd * 465 + (1 - par) * 31 - 48
                    src = bass.AP(rpb.tensor, off, [[1, 64], [31, NS], [1, 64]])
                    sp.dma_start(bias[64 * par:64 * par + 64, hd % 2], src).then_inc(landed[hd % 2], 16)
            k.send_weights(sp)

        @block.gpsimd
        def _(pool):
            over = lambda name: k.c(name, 0, 64).rearrange("p (s c) -> p s c", s=1).broadcast_to([P, NS, 64])
            for hd in range(8):
                pool.wait_ge(landed[hd % 2], 32 * (hd // 2 + 1))
                pool.tensor_tensor(bias[:, hd % 2], bias[:, hd % 2], over("pair_mask"), MUL).then_inc(s["masked"], 1)
                pool.wait_ge(s["masked"], hd + 1)
                pool.tensor_tensor(bias[:, hd % 2], bias[:, hd % 2], over("pair_neg"), ADD).then_inc(s["bias_ready"], 1)

        @block.tensor
        def _(pe):
            def scores(u):
                hd, i = divmod(u, 4)
                r, ct = slice(64 * (hd % 2), 64 * (hd % 2) + 64), hd // 2
                if u >= 2:
                    pe.wait_ge(s["s_lat"], u - 1)
                    pe.wait_ge(s["s_ctx"], u - 1)
                b = 2 * (u % 2)
                pe.matmul(k.bank[b][:, :], q[r, ct, P * i:P * i + P], kf[r, ct, CTX:ALL], start=True, stop=True)
                pe.matmul(k.bank[b + 1][:, 0:CTX], q[r, ct, P * i:P * i + P], kf[r, ct, 0:CTX],
                          start=True, stop=True).then_inc(s["s_mm"], 1)

            def times_v(hd, part):
                if part == 0:
                    pe.wait_ge(s["pt"], 4 * hd + 4)
                    if hd >= 2:
                        pe.wait_ge(s["av"], hd - 1)
                r = slice(64 * (hd % 2), 64 * (hd % 2) + 64)
                for j in (2 * part, 2 * part + 1):
                    last = pe.matmul(k.bank[6 + hd % 2][r, :], v_tok[:, j, 64 * hd:64 * hd + 64], pt[:, hd % 2, j],
                                     start=j == 0, stop=j == 5)
                if part == 2:
                    last.then_inc(s["av_mm"], 1)

            scores(0)
            scores(1)
            for u in range(N):
                if u + 2 < N:
                    scores(u + 2)
                pe.wait_ge(s["p"], u + 1)
                if u:
                    pe.wait_ge(s["pt"], u)
                for j in range(6):
                    last = pe.transpose(k.bank[4 + j // 4][:, P * (j % 4):P * (j % 4) + P], sc[:, u % NB, P * j:P * j + P],
                                        k.c("ident"))
                last.then_inc(s["turned"], 1)
                if u >= 4 and u % 4 < 3:
                    times_v(u // 4 - 1, u % 4)
            for part in range(3):
                times_v(7, part)

        @block.scalar
        def _(act):
            def ctx_scores(u):
                act.wait_ge(s["s_mm"], u + 1)
                if u >= NB:
                    act.wait_ge(s["turned"], u - NB + 1)
                act.activation(sc[:, u % NB, 0:CTX], k.bank[2 * (u % 2) + 1][:, 0:CTX], ACT.Copy, scale=SCALE).then_inc(s["s_ctx"], 1)

            def exp(u):
                act.wait_ge(s["neg"], u + 1)
                c = col[:, u % NB]
                act.activation(sc[:, u % NB], sc[:, u % NB], ACT.Exp, bias=c[:, 1:2], accum_out=c[:, 2:3]).then_inc(s["exp"], 1)

            def take_out(hd):
                act.wait_ge(s["av_mm"], hd + 1)
                r = slice(64 * (hd % 2), 64 * (hd % 2) + 64)
                act.activation(att[r, hd // 2], k.bank[6 + hd % 2][r, :], ACT.Copy).then_inc(s["av"], 1)

            ctx_scores(0)
            exp(0)
            ctx_scores(1)
            for u in range(N):
                hd, i = divmod(u, 4)
                if u + 1 < N:
                    exp(u + 1)
                if u + 2 < N:
                    ctx_scores(u + 2)
                act.wait_ge(s["turned"], u + 1)
                if i == 0 and hd >= 2:
                    act.wait_ge(s["av_mm"], hd - 1)
                act.activation(pt[:, hd % 2, 0:4, P * i:P * i + P], k.bank[4][:, :].rearrange("p (j w) -> p j w", j=4), ACT.Copy)
                act.activation(pt[:, hd % 2, 4:6, P * i:P * i + P], k.bank[5][:, 0:256].rearrange("p (j w) -> p j w", j=2),
                               ACT.Copy).then_inc(s["pt"], 1)
                if i == 3 and hd:
                    take_out(hd - 1)
            take_out(7)

        @block.vector
        def _(dve):
            def lat_scores(u):
                hd, i = divmod(u, 4)
                dve.wait_ge(s["s_mm"], u + 1)
                if i == 0:
                    dve.wait_ge(s["bias_ready"], hd + 1)
                if u >= NB:
                    dve.wait_ge(s["turned"], u - NB + 1)
                dve.scalar_tensor_tensor(out=sc[:, u % NB, CTX:ALL].rearrange("p (s c) -> p s c", s=ROWS),
                                         in0=k.bank[2 * (u % 2)][:, :].rearrange("p (s c) -> p s c", s=ROWS), scalar=SCALE,
                                         in1=bias[:, hd % 2, 6 - 2 * i:14 - 2 * i, ::-1], op0=MUL, op1=ADD).then_inc(s["s_lat"], 1)

            def maximum(u):
                c = col[:, u % NB]
                dve.wait_ge(s["s_lat"], u + 1)
                dve.wait_ge(s["s_ctx"], u + 1)
                dve.tensor_reduce(c[:, 0:1], sc[:, u % NB], AX, MAX).then_inc(s["max"], 1)
                dve.wait_ge(s["max"], u + 1)
                dve.tensor_scalar(c[:, 1:2], c[:, 0:1], -1.0, None, MUL).then_inc(s["neg"], 1)

            lat_scores(0)
            maximum(0)
            lat_scores(1)
            for u in range(N):
                c = col[:, u % NB]
                if u + 1 < N:
                    maximum(u + 1)
                dve.wait_ge(s["exp"], u + 1)
                dve.reciprocal(c[:, 3:4], c[:, 2:3]).then_inc(s["inv"], 1)
                dve.wait_ge(s["inv"], u + 1)
                dve.tensor_scalar(sc[:, u % NB], sc[:, u % NB], c[:, 3:4], None, MUL).then_inc(s["p"], 1)
                if u + 2 < N:
                    lat_scores(u + 2)


def merge_stage(k, att, conv, gate_a, gate_b, mix):
    nc = k.nc
    s = {n: k.sem("merge_" + n) for n in ("summed", "a", "b", "mix")}
    for g in range(2):
        for name in ("w_att", "w_conv"):
            k.freed[k.number(name, g)] = [(s["summed"], 4 * (g + 1))]
    with nc.Block("merge") as block:
        @block.sync
        def _(sp):
            k.send_weights(sp)

        @block.tensor
        def _(pe):
            for m in range(KD):
                ga = k.number("w_att", m // 4)
                if m % 4 == 0:
                    k.weights_ready(pe, ga)
                    k.weights_ready(pe, ga + 1)
                if m >= 4:
                    pe.wait_ge(s["b"], m - 3)
                for n, rhs in enumerate((att, conv)):
                    w = k.slot(ga + n).rearrange("p (k m) -> p k m", k=4)
                    for kt in range(4):
                        last = pe.matmul(k.bank[2 * (m % 4) + n][:, :], w[:, kt, P * (m % 4):P * (m % 4) + P], rhs[:, kt],
                                         start=kt == 0, stop=kt == 3)
                last.then_inc(s["summed"], 1)

        @block.vector
        def _(dve):
            for m in range(KD):
                dve.wait_ge(s["summed"], m + 1)
                dve.tensor_tensor(gate_a[:, m], gate_a[:, m], k.bank[2 * (m % 4)][:, :], MUL).then_inc(s["a"], 1)
                dve.tensor_tensor(gate_b[:, m], gate_b[:, m], k.bank[2 * (m % 4) + 1][:, :], MUL).then_inc(s["b"], 1)
                dve.wait_ge(s["a"], m + 1)
                dve.wait_ge(s["b"], m + 1)
                dve.tensor_tensor(mix[:, m], gate_a[:, m], gate_b[:, m], ADD).then_inc(s["mix"], 1)


def route_stage(k, h, weights, table, h_dram, table_dram, w_router, ids, work, experts):
    nc = k.nc
    off = [work]

    def buf(*dims):
        n = int(np.prod(dims))
        off[0] += n
        x = k.at(off[0] - n, n)
        if len(dims) == 2:
            return x.rearrange("p (a b) -> p a b", a=dims[0])
        if len(dims) == 3:
            return x.rearrange("p (a b c) -> p a b c", a=dims[0], b=dims[1])
        return x
    L, tie, one_g, ex, pg = buf(4, 36), buf(4, 8), buf(4, 4), buf(4, 4), buf(4, 1)
    top = [buf(4, 1), buf(4, 1)]
    gmax, least, total = buf(4, 1), buf(4, 1), buf(4, 1)
    picked, masked, part = buf(4, 8), buf(4, 8), buf(4, 4, 8)
    one_e = [buf(4, 8), buf(4, 8)]
    X = [buf(4, 32), buf(4, 32)]
    M, dest, tmp = buf(4, 32), buf(4, 32), buf(4, 32)
    j_tile, count, extra, upto = buf(4, 32), buf(32), buf(32), buf(32)
    slot_f = buf(4, 2)
    slot_i = buf(4, 2).bitcast(I32)
    tok_rows = k.at(work + 2048, 2 * D).rearrange("p (n w) -> p n w", n=2)
    s = {n: k.sem("route_" + n) for n in ("logits", "step", "exped", "rank_in", "rank", "slots", "blank", "scattered",
                                         "loaded", "turned", "rows")}
    rows_out = [k.sem(f"route_rows_out_{i}") for i in range(2)]
    iota = k.c("expert_id", 0, 32)
    n_step = [0]
    with nc.Block("route") as block:
        @block.sync
        def _(sp):
            sp.dma_start(table_dram.rearrange("(p b) t -> p (b t)", p=P), k.blank).then_inc(s["blank"], 16)
            experts.send_gate_up(sp, 1, 1)
            experts.send_down(sp, 1, 1)
            for tt in range(4):
                sp.wait_ge(s["rows"], tt + 1)
                sp.dma_start(h_dram[P * tt:P * tt + P], tok_rows[:, tt % 2]).then_inc(rows_out[tt % 2], 16)
            sp.wait_ge(s["scattered"], 128)
            sp.dma_start(table, table_dram.rearrange("(p b) t -> p (b t)", p=P)).then_inc(s["loaded"], 16)
            sp.wait_ge(s["loaded"], 16)
            for out in rows_out:
                sp.wait_ge(out, 32)

        @block.tensor
        def _(pe):
            for tt in range(4):
                for kt in range(KD):
                    last = pe.matmul(k.bank[0][:, 36 * tt:36 * tt + 36], h[:, kt, P * tt:P * tt + P],
                                     w_router[:, kt], start=kt == 0, stop=kt == KD - 1)
            last.then_inc(s["logits"], 1)
            for tt in range(4):
                if tt:
                    pe.wait_ge(s["rows"], tt)
                for kt in range(KD):
                    last = pe.transpose(k.bank[2 + kt // 4][:, P * (kt % 4):P * (kt % 4) + P], h[:, kt, P * tt:P * tt + P],
                                        k.c("ident"))
                last.then_inc(s["turned"], 1)
            pe.wait_ge(s["rank_in"], 1)
            for tt in range(4):
                for t2 in range(tt + 1):
                    pe.matmul(k.bank[1][:, 32 * tt:32 * tt + 32], k.c("before") if t2 == tt else k.c("ones"), M[:, t2],
                              start=t2 == 0, stop=t2 == tt)
            for t2 in range(4):
                last = pe.matmul(k.bank[1][:, 128:160], k.c("ones"), M[:, t2], start=t2 == 0, stop=t2 == 3)
            last.then_inc(s["rank"], 1)

        @block.scalar
        def _(act):
            for tt in range(4):
                act.wait_ge(s["turned"], tt + 1)
                if tt >= 2:
                    act.wait_ge(rows_out[tt % 2], 16)
                act.activation(tok_rows[:, tt % 2, 0:512], k.bank[2][:, :], ACT.Copy)
                act.activation(tok_rows[:, tt % 2, 512:1024], k.bank[3][:, :], ACT.Copy).then_inc(s["rows"], 1)
            act.wait_ge(s["step"], route_steps["group_shifted"])
            act.activation(ex, ex, ACT.Exp).then_inc(s["exped"], 1)
            act.wait_ge(s["step"], route_steps["pair_shifted"])
            act.activation(top[1], top[1], ACT.Exp).then_inc(s["exped"], 1)

        @block.gpsimd
        def _(pool):
            pool.wait_ge(s["blank"], 16)
            pool.wait_ge(s["slots"], 1)
            for i in range(8):
                pool.indirect_dma_start(table_dram, bass.IndirectOffsetOnAxis(slot_i[:, i // 2, i % 2:i % 2 + 1].bitcast(U32), 0),
                                        ids[:, i], None).then_inc(s["scattered"], 16)

        @block.vector
        def _(dve):
            def step(ins):
                n_step[0] += 1
                ins.then_inc(s["step"], 1)
                dve.wait_ge(s["step"], n_step[0])

            def over(x, n):
                return x.broadcast_to([P, 4, n])

            def first_max(x, n, peak, one):
                step(dve.tensor_reduce(peak, x, AX, MAX))
                t = tie[:, :, 0:n]
                step(dve.tensor_tensor(t, x, over(peak, n), ALU.is_equal))
                ids_n = iota[:, 0:n].rearrange("p (a n) -> p a n", a=1).broadcast_to([P, 4, n])
                step(dve.scalar_tensor_tensor(out=t, in0=t, scalar=-100.0, in1=ids_n, op0=MUL, op1=ADD))
                step(dve.tensor_reduce(least, t, AX, ALU.min))
                step(dve.tensor_tensor(one, t, over(least, n), ALU.is_equal))

            dve.wait_ge(s["logits"], 1)
            b = k.v("router_b", 0, 36).rearrange("p (a n) -> p a n", a=1).broadcast_to([P, 4, 36])
            step(dve.tensor_tensor(L, k.bank[0][:, 0:144].rearrange("p (a n) -> p a n", a=4), b, ADD))
            first_max(L[:, :, 0:4], 4, gmax, one_g)
            step(dve.tensor_tensor(ex, L[:, :, 0:4], over(gmax, 4), SUB))
            assert route_steps["group_shifted"] == n_step[0], n_step[0]
            logits = L[:, :, 4:36].rearrange("p a (g e) -> p a g e", g=4)
            for tt in range(4):
                one = one_g[:, tt, :].rearrange("p (g e) -> p g e", e=1).broadcast_to([P, 4, 8])
                step(dve.tensor_tensor(part[:, tt], logits[:, tt], one, MUL))
            step(dve.tensor_tensor(picked, part[:, :, 0], part[:, :, 1], ADD))
            step(dve.tensor_tensor(masked, part[:, :, 2], part[:, :, 3], ADD))
            step(dve.tensor_tensor(picked, picked, masked, ADD))
            first_max(picked, 8, top[0], one_e[0])
            step(dve.scalar_tensor_tensor(out=masked, in0=one_e[0], scalar=NEG, in1=picked, op0=MUL, op1=ADD))
            first_max(masked, 8, top[1], one_e[1])
            step(dve.tensor_tensor(top[1], top[1], top[0], SUB))
            assert route_steps["pair_shifted"] == n_step[0], n_step[0]
            for i in range(2):
                for tt in range(4):
                    g = one_g[:, tt, :].rearrange("p (g e) -> p g e", e=1).broadcast_to([P, 4, 8])
                    e = one_e[i][:, tt, :].rearrange("p (g e) -> p g e", g=1).broadcast_to([P, 4, 8])
                    step(dve.tensor_tensor(X[i][:, tt].rearrange("p (g e) -> p g e", g=4), g, e, MUL))
            dve.tensor_tensor(M, X[0], X[1], ADD).then_inc(s["rank_in"], 1)
            dve.wait_ge(s["exped"], 2)
            step(dve.tensor_reduce(total, ex, AX, ADD))
            step(dve.reciprocal(pg, total))
            step(dve.tensor_scalar(total, top[1], 1.0, None, ADD))
            step(dve.reciprocal(total, total))
            step(dve.tensor_tensor(total, total, pg, MUL))
            step(dve.tensor_copy(weights[:, :, 0:1], total))
            step(dve.tensor_tensor(weights[:, :, 1:2], total, top[1], MUL))
            dve.wait_ge(s["rank"], 1)
            step(dve.tensor_copy(dest, k.bank[1][:, 0:128].rearrange("p (a n) -> p a n", a=4)))
            step(dve.tensor_copy(count, k.bank[1][:, 128:160]))
            step(dve.tensor_scalar(j_tile, dest, 128.0, None, ALU.is_ge))
            step(dve.tensor_scalar(extra, count, 128.0, None, ALU.is_gt))
            for t in (256.0, 384.0):
                step(dve.scalar_tensor_tensor(out=j_tile, in0=dest, scalar=t, in1=j_tile, op0=ALU.is_ge, op1=ADD))
                step(dve.scalar_tensor_tensor(out=extra, in0=count, scalar=t, in1=extra, op0=ALU.is_gt, op1=ADD))
            step(dve.tensor_tensor_scan(upto, k.c("ones", 0, 32), extra, 0.0, MUL, ADD))
            step(dve.scalar_tensor_tensor(out=dest, in0=j_tile, scalar=-128.0, in1=dest, op0=MUL, op1=ADD))
            step(dve.tensor_tensor(count, upto, extra, SUB))
            step(dve.scalar_tensor_tensor(out=count, in0=count, scalar=31.0, in1=iota, op0=ADD, op1=SUB))
            flat = count.rearrange("p (a n) -> p a n", a=1).broadcast_to([P, 4, 32])
            step(dve.tensor_tensor(tmp, j_tile, flat, ADD))
            step(dve.scalar_tensor_tensor(out=tmp, in0=j_tile, scalar=0.5, in1=tmp, op0=ALU.is_gt, op1=MUL))
            ids4 = iota.rearrange("p (a n) -> p a n", a=1).broadcast_to([P, 4, 32])
            step(dve.tensor_tensor(tmp, tmp, ids4, ADD))
            step(dve.scalar_tensor_tensor(out=dest, in0=dest, scalar=float(N_BLK), in1=tmp, op0=MUL, op1=ADD))
            for i in range(2):
                step(dve.tensor_tensor(tmp, X[i], dest, MUL))
                step(dve.tensor_reduce(slot_f[:, :, i:i + 1], tmp, AX, ADD))
            for i in range(OVER):
                step(dve.tensor_scalar(tmp[:, 0], upto, float(i), None, ALU.is_le))
                step(dve.tensor_reduce(k.over_f[:, i:i + 1], tmp[:, 0], AX, ADD))
            step(dve.tensor_copy(k.over_f[:, OVER:OVER + 1], upto[:, 31:32]))
            step(dve.tensor_copy(k.over_i, k.over_f))
            dve.tensor_copy(slot_i, slot_f).then_inc(s["slots"], 1)


route_steps = {"group_shifted": 7, "pair_shifted": 26}


class Experts:

    def __init__(self, k, at):
        self.d = k.d
        self.gate_w, self.up_w, self.down_w = (
            [k.at(at + 4096 * (2 * i + h), 4096).rearrange("p (k n) -> p k n", k=kt) for h in range(2)]
            for i, kt in enumerate((KD, KD, 4)))
        self.gate_up_landed = [k.sem(f"moe_gate_up_landed_{i}") for i in range(2)]
        self.down_landed = [k.sem(f"moe_down_landed_{i}") for i in range(2)]

    def load(self, sp, name, e, to, landed):
        src = self.d[name][bass.ds(e, 1)].rearrange("a p n -> (a p) n")
        sp.dma_start(to.rearrange("p k n -> p (k n)"), src).then_inc(landed, 16)

    def send_gate_up(self, sp, e, h):
        self.load(sp, "w_gate", e, self.gate_w[h], self.gate_up_landed[h])
        self.load(sp, "w_upe", e, self.up_w[h], self.gate_up_landed[h])

    def send_down(self, sp, e, h):
        self.load(sp, "w_downe", e, self.down_w[h], self.down_landed[h])


def moe_stage(k, experts, table, h_dram, y_dram, at):
    nc = k.nc

    def buf(n, *shape):
        at[0] += n
        return k.mem[:, at[0] - n:at[0]]
    gate_w, up_w, down_w = experts.gate_w, experts.up_w, experts.down_w
    gu_landed, down_landed = experts.gate_up_landed, experts.down_landed
    rows = [buf(D) for _ in range(2)]
    y = [buf(D) for _ in range(2)]
    x = buf(D).rearrange("p (k n) -> p k n", k=KD)
    act_g, hid, hid_t = buf(D_EXP), buf(D_EXP), buf(D_EXP).rearrange("p (k n) -> p k n", k=4)
    token, row = [buf(1).bitcast(I32) for _ in range(2)], [buf(1).bitcast(I32) for _ in range(2)]
    s = {n: k.sem("moe_" + n) for n in ("token", "row", "x_turned", "x", "gate_mm", "up_mm", "silu", "hid", "h_turned", "hid_t",
                                       "down_mm", "y")}
    gathered = [k.sem(f"moe_gathered_{i}") for i in range(2)]
    stored = [k.sem(f"moe_stored_{i}") for i in range(2)]
    n_ready = k.sem("moe_count_ready")
    turns = k.sem("moe_pool_turns")

    def send_gate_up(sp, e, n, h):
        sp.wait_ge(s["up_mm"], n - 1)
        experts.send_gate_up(sp, e, h)

    def send_down(sp, e, n, h):
        sp.wait_ge(s["down_mm"], n - 1)
        experts.send_down(sp, e, h)

    def gather(pool, n, h, first):
        if not first:
            pool.wait_ge(s["x_turned"], n - 1)
            pool.sem_inc(turns, 1)
        pool.tensor_copy(token[h].rearrange("p (a t) -> p a t", a=1), table[:, bass.ds(n, 1), 1:2]).then_inc(s["token"], 1)
        pool.wait_ge(s["token"], n + 1)
        pool.sem_inc(turns, 1)
        pool.indirect_dma_start(rows[h], None, h_dram,
                                bass.IndirectOffsetOnAxis(token[h].bitcast(U32), 0)).then_inc(gathered[h], 16)

    def scatter(pool, n, i, h, first):
        if not first:
            pool.wait_ge(stored[h], 16 * i)
            pool.sem_inc(turns, 1)
        pool.tensor_copy(row[h].rearrange("p (a t) -> p a t", a=1), table[:, bass.ds(n, 1), 0:1]).then_inc(s["row"], 1)
        pool.wait_ge(s["row"], n + 1)
        pool.wait_ge(s["y"], n + 1)
        pool.sem_inc(turns, 1)
        pool.indirect_dma_start(y_dram, bass.IndirectOffsetOnAxis(row[h].bitcast(U32), 0), y[h], None,
                                bounds_check=N_PAIR - 1, oob_is_err=False).then_inc(stored[h], 16)

    def turn_x(pe, n, i, h, first):
        pe.wait_ge(gathered[h], 16 * (i + 1))
        if not first:
            pe.wait_ge(s["x"], n)
        for kt in range(KD):
            last = pe.transpose(k.bank[kt // 4][:, P * (kt % 4):P * (kt % 4) + P], rows[h][:, kt:D:KD], k.c("ident"))
        last.then_inc(s["x_turned"], 1)

    def gate_up(pe, n, i, h, first):
        pe.wait_ge(s["x"], n + 1)
        pe.wait_ge(gu_landed[h], 32 * (i + 1))
        if not first:
            pe.wait_ge(s["hid"], n)
        for kt in range(KD):
            last = pe.matmul(k.bank[2][:, :], x[:, kt], gate_w[h][:, kt], start=kt == 0, stop=kt == KD - 1)
        last.then_inc(s["gate_mm"], 1)
        for kt in range(KD):
            last = pe.matmul(k.bank[3][:, :], x[:, kt], up_w[h][:, kt], start=kt == 0, stop=kt == KD - 1)
        last.then_inc(s["up_mm"], 1)

    def turn_hidden(pe, n):
        pe.wait_ge(s["hid"], n + 1)
        for kt in range(4):
            last = pe.transpose(k.bank[4][:, P * kt:P * kt + P], hid[:, kt:D_EXP:4], k.c("ident"))
        last.then_inc(s["h_turned"], 1)

    def down(pe, n, i, h, first):
        pe.wait_ge(s["hid_t"], n + 1)
        pe.wait_ge(down_landed[h], 16 * (i + 1))
        if not first:
            pe.wait_ge(s["y"], n)
        for half in range(2):
            for kt in range(4):
                last = pe.matmul(k.bank[5 + half][:, :], hid_t[:, kt], down_w[h][:, kt, 512 * half:512 * half + 512],
                                 start=kt == 0, stop=kt == 3)
        last.then_inc(s["down_mm"], 1)

    def act_part(act, n, first):
        act.wait_ge(s["x_turned"], n + 1)
        if not first:
            act.wait_ge(s["up_mm"], n)
        act.activation(x[:, 0:4].rearrange("p k n -> p (k n)"), k.bank[0][:, :], ACT.Copy)
        act.activation(x[:, 4:8].rearrange("p k n -> p (k n)"), k.bank[1][:, :], ACT.Copy).then_inc(s["x"], 1)

    def act_silu(act, n, first):
        act.wait_ge(s["gate_mm"], n + 1)
        if not first:
            act.wait_ge(s["hid"], n)
        act.activation(act_g, k.bank[2][:, :], ACT.Silu).then_inc(s["silu"], 1)

    def dve_hidden(dve, n, first):
        dve.wait_ge(s["silu"], n + 1)
        dve.wait_ge(s["up_mm"], n + 1)
        if not first:
            dve.wait_ge(s["h_turned"], n)
        dve.tensor_tensor(hid, act_g, k.bank[3][:, :], MUL).then_inc(s["hid"], 1)

    def dve_turned(dve, n, first):
        dve.wait_ge(s["h_turned"], n + 1)
        if not first:
            dve.wait_ge(s["down_mm"], n)
        dve.tensor_copy(hid_t.rearrange("p k n -> p (k n)"), k.bank[4][:, :]).then_inc(s["hid_t"], 1)

    def dve_rows(dve, n, i, h, first_half):
        dve.wait_ge(s["down_mm"], n + 1)
        if not first_half:
            dve.wait_ge(stored[h], 16 * i)
        dve.tensor_copy(y[h][:, 0:512], k.bank[5][:, :])
        dve.tensor_copy(y[h][:, 512:1024], k.bank[6][:, :]).then_inc(s["y"], 1)

    def over_blocks(eng, run):
        eng.wait_ge(n_ready, 1)
        for o in range(OVER):
            count = eng.value_load(k.over_i[0:1, OVER:OVER + 1], min_val=0, max_val=OVER)
            with eng.If(count > o):
                run(o)

    LAST = N_EXP - 1
    with nc.Block("moe") as block:
        @block.sync
        def _(sp):
            send_gate_up(sp, 2, 2, 0)
            with sp.Fori(1, N_EXP // 2 - 1) as i:
                for h in range(2):
                    n = 2 * i + 1 + h
                    send_gate_up(sp, n, n, 1 - h)
                    send_down(sp, n - 1, n - 1, h)
            send_gate_up(sp, LAST, LAST, 1)
            send_down(sp, LAST - 1, LAST - 1, 0)
            send_down(sp, LAST, LAST, 1)

            def over(o):
                n = N_EXP + o
                e = sp.value_load(k.over_i[0:1, o:o + 1], min_val=0, max_val=N_EXP - 1)
                send_gate_up(sp, e, n, n % 2)
                send_down(sp, e, n, n % 2)
            over_blocks(sp, over)

        @block.gpsimd
        def _(pool):
            pool.sem_inc(n_ready, 1)
            gather(pool, 0, 0, True)
            gather(pool, 1, 1, True)
            for n in range(2, 4):
                gather(pool, n, n % 2, False)
                scatter(pool, n - 2, 0, n % 2, True)
            with pool.Fori(2, N_EXP // 2) as i:
                for h in range(2):
                    gather(pool, 2 * i + h, h, False)
                    scatter(pool, 2 * i + h - 2, i - 1, h, False)
            scatter(pool, LAST - 1, N_EXP // 2 - 1, 0, False)
            scatter(pool, LAST, N_EXP // 2 - 1, 1, False)

            def over(o):
                n = N_EXP + o
                gather(pool, n, n % 2, False)
                scatter(pool, n, n // 2, n % 2, False)
            over_blocks(pool, over)
            pool.wait_ge(stored[0], 8 * N_EXP)
            pool.wait_ge(stored[1], 8 * N_EXP)
            for o in range(OVER):
                count = pool.value_load(k.over_i[0:1, OVER:OVER + 1], min_val=0, max_val=OVER)
                with pool.If(count > o):
                    pool.wait_ge(stored[o % 2], 8 * N_EXP + 16 * (o // 2 + 1))

        @block.tensor
        def _(pe):
            def block_of(n, i, h, first=False, i_before=None, i_next=None):
                gate_up(pe, n, i, h, first)
                if i_next is not None:
                    turn_x(pe, n + 1, i_next, 1 - h, False)
                if i_before is not None:
                    down(pe, n - 1, i_before, 1 - h, False)
                turn_hidden(pe, n)
            turn_x(pe, 0, 0, 0, True)
            block_of(0, 0, 0, first=True, i_next=0)
            gate_up(pe, 1, 0, 1, False)
            turn_x(pe, 2, 1, 0, False)
            down(pe, 0, 0, 0, True)
            turn_hidden(pe, 1)
            with pe.Fori(1, N_EXP // 2 - 1) as i:
                block_of(2 * i, i, 0, i_before=i - 1, i_next=i)
                block_of(2 * i + 1, i, 1, i_before=i, i_next=i + 1)
            i = N_EXP // 2 - 1
            block_of(LAST - 1, i, 0, i_before=i - 1, i_next=i)
            block_of(LAST, i, 1, i_before=i)
            down(pe, LAST, i, 1, False)

            def over(o):
                n = N_EXP + o
                turn_x(pe, n, n // 2, n % 2, False)
                block_of(n, n // 2, n % 2)
                down(pe, n, n // 2, n % 2, False)
            over_blocks(pe, over)

        @block.scalar
        def _(act):
            act_part(act, 0, True)
            act_silu(act, 0, True)
            with act.Fori(1, N_EXP) as n:
                act_part(act, n, False)
                act_silu(act, n, False)

            def over(o):
                act_part(act, N_EXP + o, False)
                act_silu(act, N_EXP + o, False)
            over_blocks(act, over)

        @block.vector
        def _(dve):
            dve_hidden(dve, 0, True)
            dve_turned(dve, 0, True)
            dve_hidden(dve, 1, False)
            dve_rows(dve, 0, 0, 0, True)
            dve_turned(dve, 1, False)
            dve_hidden(dve, 2, False)
            dve_rows(dve, 1, 0, 1, True)
            dve_turned(dve, 2, False)
            with dve.Fori(1, N_EXP // 2 - 1) as i:
                for h in range(2):
                    n = 2 * i + 1 + h
                    dve_hidden(dve, n, False)
                    dve_rows(dve, n - 1, i, h, False)
                    dve_turned(dve, n, False)
            dve_hidden(dve, LAST, False)
            dve_rows(dve, LAST - 1, N_EXP // 2 - 1, 0, False)
            dve_turned(dve, LAST, False)
            dve_rows(dve, LAST, N_EXP // 2 - 1, 1, False)

            def over(o):
                n = N_EXP + o
                dve_hidden(dve, n, False)
                dve_turned(dve, n, False)
                dve_rows(dve, n, n // 2, n % 2, False)
            over_blocks(dve, over)


def combine_stage(k, y_dram, weights, x, gate, at):
    nc = k.nc
    yr = k.at(at, 8192).rearrange("p (t c w) -> p t c w", t=4, c=2)
    s = {n: k.sem("combine_" + n) for n in ("first", "both", "turned", "done")}
    landed = [k.sem(f"combine_landed_{tt}") for tt in range(4)]
    with nc.Block("combine") as block:
        @block.sync
        def _(sp):
            for tt in range(4):
                src = y_dram[2 * P * tt:2 * P * (tt + 1)].rearrange("(p c) w -> p (c w)", c=2)
                sp.dma_start(yr[:, tt].rearrange("p c w -> p (c w)"), src).then_inc(landed[tt], 16)

        @block.vector
        def _(dve):
            for tt in range(4):
                dve.wait_ge(landed[tt], 16)
                dve.tensor_scalar(yr[:, tt, 0], yr[:, tt, 0], weights[:, tt, 0:1], None, MUL).then_inc(s["first"], 1)
                dve.wait_ge(s["first"], tt + 1)
                dve.scalar_tensor_tensor(out=yr[:, tt, 0], in0=yr[:, tt, 1], scalar=weights[:, tt, 1:2], in1=yr[:, tt, 0],
                                         op0=MUL, op1=ADD).then_inc(s["both"], 1)
            for kt in range(KD):
                dve.wait_ge(s["turned"], kt + 1)
                dve.scalar_tensor_tensor(out=x[:, kt], in0=k.bank[kt % 4][:, :], scalar=gate(kt), in1=x[:, kt],
                                         op0=MUL, op1=ADD).then_inc(s["done"], 1)

        @block.tensor
        def _(pe):
            pe.wait_ge(s["both"], 4)
            for kt in range(KD):
                if kt >= 4:
                    pe.wait_ge(s["done"], kt - 3)
                for tt in range(4):
                    last = pe.transpose(k.bank[kt % 4][:, P * tt:P * tt + P], yr[:, tt, 0, P * kt:P * kt + P], k.c("ident"))
                last.then_inc(s["turned"], 1)


def block_two(k, src):
    nc, d = k.nc, k.d
    three = lambda at, n, w: k.at(at, n * w).rearrange("p (n w) -> p n w", n=n)
    k.retire()
    x = src[:, :, CTX:ALL]
    m2 = k.mod[1]
    hm = three(6144, KD, ALL)
    norm_stage(k, "norm_mix", src, hm, [(0, CTX, 0), (CTX, SEQ, 1)],
               gain=lambda i: [(m2[:, 8:16, 1 - i], k.v("norm_mix", 0, 8))],
               shift=lambda kt, i: m2[:, kt, 1 - i:2 - i], work=18432)
    q, kf, v_tok = three(12288, 4, SEQ), three(14336, 4, ALL), three(17408, 6, 512)
    upad, ga, gb = three(20480, 4, 542), three(22656, 8, SEQ), three(26752, 8, SEQ)
    conv, sig = three(30848, 4, SEQ), three(32896, 4, SEQ)
    in_proj2_stage(k, hm, q, kf, v_tok, upad, sig, ga, gb, conv)
    layer_norm_stage(k, conv, 34944)
    att = three(32896, 4, SEQ)
    attention_stage(k, q, kf, v_tok, att, 6144, 7936, 34944)
    mix = three(34944, 8, SEQ)
    x4 = three(6144, KD, SEQ)
    merge_stage(k, att, conv, ga, gb, mix)
    k.frees_later([k.number("w_o", g) for g in range(4)], "w_o_summed", 2)
    residual_stage(k, "w_o", 1, halves(k, "w_o"), mix, lambda m: m2[:, 16 + m, 0:1], x, x4)
    k.retire()
    h, x = three(0, KD, SEQ), x4
    experts = Experts(k, 10240)
    w_router = three(4096, KD, 36)
    table = k.at(4384, 2 * N_BLK).bitcast(I32).rearrange("p (b t) -> p b t", t=2)
    k.blank = k.at(4464, 2 * N_BLK).bitcast(I32)
    ids = k.at(4544, 16).bitcast(I32).rearrange("p (i t) -> p i t", t=2)
    weights = k.at(4560, 8).rearrange("p (t c) -> p t c", t=4)
    k.over_f, k.over_i = k.at(4568, 8), k.at(4576, 8).bitcast(I32)
    h_dram = nc.dram_tensor("h_rows", [SEQ, D], F32, kind="Internal").ap()
    y_dram = nc.dram_tensor("y_rows", [N_PAIR, D], F32, kind="Internal").ap()
    table_dram = nc.dram_tensor("slot_table", [P * N_BLK, 2], I32, kind="Internal").ap()
    norm_stage(k, "norm_ffn", x, h, [(0, SEQ, 0)], gain=lambda i: [(m2[:, 32:40, 0], k.v("norm_ffn", 0, 8))],
               shift=lambda kt, i: m2[:, 24 + kt, 0:1], work=34816, experts=experts,
               loads=[(k.at(4096, 288), d["w_router"]), (k.blank, d["blank"]), (k.at(4544, 16).bitcast(I32), d["ids"])])
    route_stage(k, h, weights, table, h_dram, table_dram, w_router, ids, 34816, experts)
    moe_stage(k, experts, table, h_dram, y_dram, [k.free_at + 10240 + 6 * 4096])
    combine_stage(k, y_dram, weights, x, lambda m: m2[:, 40 + m, 0:1], 10240)
    out = three(0, KD, SEQ)
    norm_stage(k, "final2", x, out, [(0, SEQ, 0)], gain=lambda i: [(k.v("final_norm", 0, 8), None)], shift=None, work=10240)
    return out


def order_of_use(k):
    for g in range(8):
        k.put("ada1", g)
    order = [*range(8, 16), *range(4, 8), 16, 17, 18, *range(4)]
    for i, m in enumerate(order):
        k.put("w_in", m)
        if i < 16:
            k.put("ada1", 8 + i)
    for g in range(4):
        k.put("w_out", g)
    for m in range(KF):
        k.put("w_up", m)
    k.put("w_down", 0)
    k.put("w_down", 1)
    for m in range(1, KD):
        beside = MOD_BESIDE[m - 1]
        k.put("w_down", 2 * m)
        k.put("ada2", beside[0])
        k.put("w_down", 2 * m + 1)
        for g in beside[1:]:
            k.put("ada2", g)
    for name, n in (("w_in2_q", 4), ("w_in2_v", 2), ("w_in2_g", 12)):
        for g in range(n):
            k.put(name, g)
    for g in range(2):
        k.put("w_att", g)
        k.put("w_conv", g)
    for g in range(4):
        k.put("w_o", g)


def build(nc, d, out, only_first=False):
    k = Core(nc, d, out)
    order_of_use(k)
    load_stage(k)
    x = block_one(k)
    if not only_first:
        x = block_two(k, x)
    stored = k.sem("result_stored")
    with nc.Block("store") as block:
        @block.sync
        def _(sp):
            sp.dma_start(out, x).then_inc(stored, 16)
            sp.wait_ge(stored, 16)


def kernel(**inputs):
    import concourse.bacc as bacc
    from concourse.bass_utils import run_bass_kernel_spmd

    nc = bacc.Bacc("TRN2", target_bir_lowering=False, num_devices=1)
    arrays = lay_out(inputs)
    d = {name: nc.dram_tensor(f"in_{name}", a.shape, mybir.dt.from_np(a.dtype), kind="ExternalInput").ap() for name, a in arrays.items()}
    out = nc.dram_tensor("out", [P, KD, SEQ], F32, kind="ExternalOutput").ap()
    build(nc, d, out)
    r = run_bass_kernel_spmd(nc, [{f"in_{name}": a for name, a in arrays.items()}], core_ids=[0])
    got = r.results[0]["out"]
    return np.ascontiguousarray(got.transpose(2, 1, 0)).reshape(1, SEQ, D)
```
